# Optimizing a Trainium2 kernel written in Bass

```python
import jax, jax.numpy as jnp
from jax import lax
import numpy as np

D_MODEL = 1024
BATCH = 1
SEQ = 256
DEPTH = 2

ML_HEADS = 4
ML_DIM = 128
ML_W = ML_HEADS * ML_DIM
ML_CONV = 4
ML_CHUNK = 64
GLA_HEADS = 4
GLA_DK = 64
GLA_DV = 128
GLA_K_W = GLA_HEADS * GLA_DK
GLA_V_W = GLA_HEADS * GLA_DV
GLA_RANK = 16
GLA_TAU = 16.0
GLA_CHUNK = 32
RET_HEADS = 4
RET_DIM = 128
RET_W = RET_HEADS * RET_DIM
RET_CHUNK = 64
ROPE_BASE = 10000.0
RW_HEADS = 8
RW_DIM = 64
RW_W = RW_HEADS * RW_DIM
RW_DECAY_RANK = 64
RW_A_RANK = 64
RW_GATE_RANK = 128
RW_LN_EPS = 64e-5
D_FF = 3584
N_EXPERTS = 8
TOP_K = 2
EPS = 1e-6

E_SPLITS = (2 * ML_W, ML_W, ML_W, 2 * ML_HEADS, GLA_K_W, GLA_K_W, GLA_V_W, GLA_V_W, GLA_RANK)
E_COLS = sum(E_SPLITS)
E_MIX_W = ML_W + GLA_V_W
RET_SPLITS = (RET_W, RET_W, RET_W, RET_W)
RET_COLS = sum(RET_SPLITS)
RW_SPLITS = (RW_W, RW_W, RW_W, RW_DECAY_RANK, RW_A_RANK, RW_GATE_RANK)
RW_COLS = sum(RW_SPLITS)
O_COLS = RET_COLS + RW_COLS
O_MIX_W = RET_W + RW_W

kernel_name = 'hybrid_mlstm_gla_retnet_rwkv7_moe'

def rms_norm(x, g):
    xf = x.astype(jnp.float32)
    y = xf * lax.rsqrt(jnp.mean(xf * xf, axis=-1, keepdims=True) + EPS)
    return (y * g).astype(x.dtype)

def head_layer_norm(x, eps):
    xf = x.astype(jnp.float32)
    xc = xf - jnp.mean(xf, axis=-1, keepdims=True)
    return xc * lax.rsqrt(jnp.mean(xc * xc, axis=-1, keepdims=True) + eps)

def head_rms_norm(x, eps):
    xf = x.astype(jnp.float32)
    return xf * lax.rsqrt(jnp.mean(xf * xf, axis=-1, keepdims=True) + eps)

def split_cols(p, sizes):
    idx = np.cumsum(sizes)[:-1].tolist()
    return jnp.split(p, idx, axis=-1)

def heads(a, n):
    return a.reshape(a.shape[:-1] + (n, -1)).astype(jnp.float32)

def token_shift(x):
    return jnp.pad(x[:, :-1], ((0, 0), (1, 0), (0, 0)))

def causal_depthwise_conv(x, w, b):
    c = x.shape[-1]
    y = lax.conv_general_dilated(x, w[:, None, :].astype(x.dtype), window_strides=(1,),
                                 padding=[(w.shape[0] - 1, 0)],
                                 dimension_numbers=('NWC', 'WIO', 'NWC'), feature_group_count=c)
    return y + b

def apply_rotary(x, positions):
    d = x.shape[-1]
    inv = ROPE_BASE ** (-jnp.arange(0, d, 2, dtype=jnp.float32) / d)
    ang = positions.astype(jnp.float32)[:, None] * inv[None, :]
    cos = jnp.cos(ang)[None, :, None, :]
    sin = jnp.sin(ang)[None, :, None, :]
    x1, x2 = x[..., : d // 2], x[..., d // 2:]
    return jnp.concatenate([x1 * cos - x2 * sin, x1 * sin + x2 * cos], axis=-1)

def to_chunks(a, L):
    b, t = a.shape[:2]
    a = a.reshape((b, t // L, L) + a.shape[2:])
    return jnp.moveaxis(a, (1, 3), (0, 2))

def from_chunks(a):
    a = jnp.moveaxis(a, (0, 2), (1, 3))
    return a.reshape((a.shape[0], a.shape[1] * a.shape[2]) + a.shape[3:])

def mlstm_chunkwise(q, k, v, i_pre, f_pre):
    bsz, t, nh, d = q.shape
    L = ML_CHUNK
    causal = jnp.tril(jnp.ones((L, L), dtype=bool))
    log_f = jax.nn.log_sigmoid(f_pre)
    xs = (to_chunks(q * d ** -0.5, L), to_chunks(k, L), to_chunks(v, L),
          to_chunks(i_pre, L), to_chunks(log_f, L))

    def step(carry, inp):
        c_st, n_st, m_st = carry
        qc, kc, vc, ic, fc = inp
        b = jnp.cumsum(fc, axis=-1)
        d_intra = jnp.where(causal, b[..., :, None] - b[..., None, :] + ic[..., None, :], -jnp.inf)
        d_inter = b + m_st[..., None]
        m_row = jnp.maximum(d_inter, jnp.max(d_intra, axis=-1))
        w_intra = jnp.exp(d_intra - m_row[..., None])
        w_inter = jnp.exp(d_inter - m_row)
        s = jnp.einsum('bhid,bhjd->bhij', qc, kc) * w_intra
        num = jnp.einsum('bhij,bhje->bhie', s, vc) + w_inter[..., None] * jnp.einsum('bhid,bhde->bhie', qc, c_st)
        den = jnp.sum(s, axis=-1) + w_inter * jnp.einsum('bhid,bhd->bhi', qc, n_st)
        h = num / jnp.maximum(jnp.abs(den), jnp.exp(-m_row))[..., None]
        g = b[..., -1]
        d_state = g[..., None] - b + ic
        m_new = jnp.maximum(g + m_st, jnp.max(d_state, axis=-1))
        w_state = jnp.exp(d_state - m_new[..., None])
        carry_decay = jnp.exp(g + m_st - m_new)
        c_st = carry_decay[..., None, None] * c_st + jnp.einsum('bhj,bhjd,bhje->bhde', w_state, kc, vc)
        n_st = carry_decay[..., None] * n_st + jnp.einsum('bhj,bhjd->bhd', w_state, kc)
        return (c_st, n_st, m_new), h

    init = (jnp.zeros((bsz, nh, d, v.shape[-1]), jnp.float32), jnp.zeros((bsz, nh, d), jnp.float32),
            jnp.zeros((bsz, nh), jnp.float32))
    _, h = lax.scan(step, init, xs)
    return from_chunks(h)

def gla_chunkwise(q, k, v, log_a):
    bsz, t, nh, dk = q.shape
    L = GLA_CHUNK
    causal = jnp.tril(jnp.ones((L, L), dtype=bool))[:, :, None]
    xs = (to_chunks(q, L), to_chunks(k, L), to_chunks(v, L), to_chunks(log_a, L))

    def step(s_st, inp):
        qc, kc, vc, ac = inp
        b = jnp.cumsum(ac, axis=2)
        diff = jnp.where(causal, b[:, :, :, None, :] - b[:, :, None, :, :], -jnp.inf)
        att = jnp.einsum('bhid,bhjd,bhijd->bhij', qc, kc, jnp.exp(diff))
        o = jnp.einsum('bhij,bhje->bhie', att, vc) + jnp.einsum('bhid,bhde->bhie', qc * jnp.exp(b), s_st)
        g = b[:, :, -1]
        s_st = jnp.exp(g)[..., None] * s_st + jnp.einsum('bhjd,bhje->bhde', kc * jnp.exp(g[:, :, None] - b), vc)
        return s_st, o

    init = jnp.zeros((bsz, nh, dk, v.shape[-1]), jnp.float32)
    _, o = lax.scan(step, init, xs)
    return from_chunks(o)

def retention_chunkwise(q, k, v, log_gamma):
    bsz, t, nh, d = q.shape
    L = RET_CHUNK
    idx = jnp.arange(L, dtype=jnp.float32)
    causal = idx[:, None] >= idx[None, :]
    rel = jnp.where(causal, idx[:, None] - idx[None, :], 0.0)
    intra_decay = jnp.where(causal, jnp.exp(log_gamma[:, None, None] * rel), 0.0)
    inter_decay = jnp.exp(log_gamma[:, None] * (idx + 1.0))[:, :, None]
    state_decay = jnp.exp(log_gamma[:, None] * (L - 1.0 - idx))[:, :, None]
    chunk_decay = jnp.exp(log_gamma * L)[:, None, None]
    xs = (to_chunks(q, L), to_chunks(k, L), to_chunks(v, L))

    def step(s_st, inp):
        qc, kc, vc = inp
        s = jnp.einsum('bhid,bhjd->bhij', qc, kc) * intra_decay
        o = jnp.einsum('bhij,bhje->bhie', s, vc) + inter_decay * jnp.einsum('bhid,bhde->bhie', qc, s_st)
        s_st = chunk_decay * s_st + jnp.einsum('bhjd,bhje->bhde', kc * state_decay, vc)
        return s_st, o

    init = jnp.zeros((bsz, nh, d, v.shape[-1]), jnp.float32)
    _, o = lax.scan(step, init, xs)
    return from_chunks(o)

def rwkv7_recurrence(r, w, k, v, a, b):
    bsz, t, nh, n = r.shape

    def step(s_st, inp):
        rt, wt, kt, vt, at, bt = inp
        sa = jnp.einsum('bhij,bhj->bhi', s_st, at)
        s_st = s_st * wt[:, :, None, :] + sa[..., None] * bt[:, :, None, :] + vt[..., None] * kt[:, :, None, :]
        return s_st, jnp.einsum('bhij,bhj->bhi', s_st, rt)

    xs = tuple(jnp.moveaxis(z, 1, 0) for z in (r, w, k, v, a, b))
    _, y = lax.scan(step, jnp.zeros((bsz, nh, n, n), jnp.float32), xs)
    return jnp.moveaxis(y, 0, 1)

def swiglu(h, w_gate, w_up, w_down):
    return (jax.nn.silu(h @ w_gate) * (h @ w_up)) @ w_down

def moe_swiglu(h, router, w_gate, w_up, w_down):
    logits = (h @ router).astype(jnp.float32)
    top_val, top_idx = lax.top_k(logits, TOP_K)
    top_w = jax.nn.softmax(top_val, axis=-1)
    gate = jnp.sum(jax.nn.one_hot(top_idx, N_EXPERTS, dtype=jnp.float32) * top_w[..., None], axis=-2)
    out = jnp.zeros(h.shape, jnp.float32)
    for e in range(N_EXPERTS):
        out = out + gate[..., e:e + 1] * swiglu(h, w_gate[e], w_up[e], w_down[e]).astype(jnp.float32)
    return out.astype(h.dtype)

def even_mixer(h, w_in, ml_conv_w, ml_conv_b, ml_gate_b, ml_norm_g, gla_gate_up, gla_gate_b, gla_norm_g, w_out):
    bsz, t, _ = h.shape
    p = h @ w_in
    ml_qk, ml_v, ml_o, ml_if, g_q, g_k, g_v, g_r, g_low = split_cols(p, E_SPLITS)
    ml_qk = jax.nn.silu(causal_depthwise_conv(ml_qk, ml_conv_w, ml_conv_b))
    q_ml, k_ml = jnp.split(ml_qk, 2, axis=-1)
    gates = (ml_if + ml_gate_b).astype(jnp.float32)
    h_ml = mlstm_chunkwise(heads(q_ml, ML_HEADS), heads(k_ml, ML_HEADS), heads(ml_v, ML_HEADS),
                           gates[..., :ML_HEADS], gates[..., ML_HEADS:])
    h_ml = jax.nn.sigmoid(heads(ml_o, ML_HEADS)) * h_ml
    h_ml = head_layer_norm(h_ml, EPS).reshape(bsz, t, ML_W) * ml_norm_g
    log_a = jax.nn.log_sigmoid((g_low @ gla_gate_up + gla_gate_b).astype(jnp.float32)) / GLA_TAU
    o_gla = gla_chunkwise(heads(g_q, GLA_HEADS) * GLA_DK ** -0.5, heads(g_k, GLA_HEADS), heads(g_v, GLA_HEADS),
                          log_a.reshape(bsz, t, GLA_HEADS, GLA_DK))
    o_gla = head_rms_norm(o_gla, EPS).reshape(bsz, t, GLA_V_W) * gla_norm_g * jax.nn.silu(g_r.astype(jnp.float32))
    mixed = jnp.concatenate([h_ml, o_gla], axis=-1).astype(h.dtype)
    return mixed @ w_out

def odd_mixer(h, w_in, ret_norm_g, rw_mu, rw_w_up, rw_w0, rw_a_up, rw_a0, rw_g_up, rw_k_k, rw_k_a, rw_r_k,
              rw_ln_g, rw_ln_b, w_out):
    bsz, t, _ = h.shape
    p = h @ w_in
    p_ret, p_rw = p[..., :RET_COLS], p[..., RET_COLS:]
    r_q, r_k, r_v, r_g = split_cols(p_ret, RET_SPLITS)
    positions = jnp.arange(t)
    log_gamma = jnp.log1p(-jnp.exp2(-5.0 - jnp.arange(RET_HEADS, dtype=jnp.float32)))
    q_ret = apply_rotary(heads(r_q, RET_HEADS), positions) * RET_DIM ** -0.5
    k_ret = apply_rotary(heads(r_k, RET_HEADS), positions)
    y_ret = retention_chunkwise(q_ret, k_ret, heads(r_v, RET_HEADS), log_gamma)
    y_ret = head_layer_norm(y_ret, EPS).reshape(bsz, t, RET_W) * ret_norm_g * jax.nn.silu(r_g.astype(jnp.float32))
    p_rw = (p_rw + (token_shift(p_rw) - p_rw) * rw_mu).astype(jnp.float32)
    x_r, x_k, x_v, x_dl, x_al, x_gl = split_cols(p_rw, RW_SPLITS)
    w_log = -jax.nn.softplus(-(rw_w0 + jnp.tanh(x_dl) @ rw_w_up)) - 0.5
    decay = jnp.exp(-jnp.exp(w_log))
    a = jax.nn.sigmoid(rw_a0 + x_al @ rw_a_up)
    g_out = jax.nn.sigmoid(x_gl) @ rw_g_up
    kk = heads(x_k * rw_k_k, RW_HEADS)
    kk = kk / jnp.maximum(jnp.linalg.norm(kk, axis=-1, keepdims=True), 1e-12)
    k_h = heads(x_k * (1.0 + (a - 1.0) * rw_k_a), RW_HEADS)
    r_h, v_h, a_h = heads(x_r, RW_HEADS), heads(x_v, RW_HEADS), heads(a, RW_HEADS)
    y_rw = rwkv7_recurrence(r_h, heads(decay, RW_HEADS), k_h, v_h, -kk, kk * a_h)
    y_rw = head_layer_norm(y_rw, RW_LN_EPS).reshape(bsz, t, RW_W) * rw_ln_g + rw_ln_b
    bonus = jnp.sum(r_h * k_h * rw_r_k, axis=-1, keepdims=True) * v_h
    y_rw = (y_rw + bonus.reshape(bsz, t, RW_W)) * g_out
    mixed = jnp.concatenate([y_ret, y_rw], axis=-1).astype(h.dtype)
    return mixed @ w_out

def setup_inputs(seed: int = 0) -> dict:
    key = jax.random.key(seed)
    ks = iter(jax.random.split(key, 64))
    f32 = jnp.float32
    ne, no = (DEPTH + 1) // 2, DEPTH // 2

    def normal(shape, scale):
        return jax.random.normal(next(ks), shape, f32) * scale

    def gain(n, dim):
        return 1.0 + normal((n, dim), 0.02)

    d = D_MODEL
    inp = {}
    inp['x'] = normal((BATCH, SEQ, d), 1.0)
    inp['e_norm1_g'] = gain(ne, d)
    inp['e_w_in'] = normal((ne, d, E_COLS), d ** -0.5)
    inp['e_ml_conv_w'] = normal((ne, ML_CONV, 2 * ML_W), 0.5)
    inp['e_ml_conv_b'] = normal((ne, 2 * ML_W), 0.02)
    inp['e_ml_gate_b'] = jnp.concatenate(
        [normal((ne, ML_HEADS), 0.1),
         jnp.linspace(3.0, 6.0, ML_HEADS, dtype=f32)[None, :] + normal((ne, ML_HEADS), 0.1)], axis=-1)
    inp['e_ml_norm_g'] = gain(ne, ML_W)
    inp['e_gla_gate_up'] = normal((ne, GLA_RANK, GLA_K_W), GLA_RANK ** -0.5)
    inp['e_gla_gate_b'] = normal((ne, GLA_K_W), 0.1)
    inp['e_gla_norm_g'] = gain(ne, GLA_V_W)
    inp['e_w_out'] = normal((ne, E_MIX_W, d), E_MIX_W ** -0.5)
    inp['e_norm2_g'] = gain(ne, d)
    inp['e_ffn_w_gate'] = normal((ne, d, D_FF), d ** -0.5)
    inp['e_ffn_w_up'] = normal((ne, d, D_FF), d ** -0.5)
    inp['e_ffn_w_down'] = normal((ne, D_FF, d), D_FF ** -0.5)
    inp['o_norm1_g'] = gain(no, d)
    inp['o_w_in'] = normal((no, d, O_COLS), d ** -0.5)
    inp['o_ret_norm_g'] = gain(no, RET_W)
    inp['o_rw_mu'] = jax.random.uniform(next(ks), (no, RW_COLS), f32)
    inp['o_rw_w_up'] = normal((no, RW_DECAY_RANK, RW_W), 0.1 * RW_DECAY_RANK ** -0.5)
    w0_ramp = jnp.broadcast_to(jnp.linspace(-6.0, -1.0, RW_DIM, dtype=f32), (RW_HEADS, RW_DIM)).reshape(-1)
    inp['o_rw_w0'] = w0_ramp[None, :] + normal((no, RW_W), 0.1)
    inp['o_rw_a_up'] = normal((no, RW_A_RANK, RW_W), 0.5 * RW_A_RANK ** -0.5)
    inp['o_rw_a0'] = normal((no, RW_W), 0.1)
    inp['o_rw_g_up'] = normal((no, RW_GATE_RANK, RW_W), RW_GATE_RANK ** -0.5)
    inp['o_rw_k_k'] = 0.85 + normal((no, RW_W), 0.02)
    inp['o_rw_k_a'] = 1.0 + normal((no, RW_W), 0.02)
    inp['o_rw_r_k'] = normal((no, RW_HEADS, RW_DIM), 0.1)
    inp['o_rw_ln_g'] = gain(no, RW_W)
    inp['o_rw_ln_b'] = normal((no, RW_W), 0.02)
    inp['o_w_out'] = normal((no, O_MIX_W, d), O_MIX_W ** -0.5)
    inp['o_norm2_g'] = gain(no, d)
    inp['o_moe_router'] = normal((no, d, N_EXPERTS), d ** -0.5)
    inp['o_moe_w_gate'] = normal((no, N_EXPERTS, d, D_FF), d ** -0.5)
    inp['o_moe_w_up'] = normal((no, N_EXPERTS, d, D_FF), d ** -0.5)
    inp['o_moe_w_down'] = normal((no, N_EXPERTS, D_FF, d), D_FF ** -0.5)
    inp['final_norm_g'] = 1.0 + normal((d,), 0.02)
    return inp

def reference(x, e_norm1_g, e_w_in, e_ml_conv_w, e_ml_conv_b, e_ml_gate_b, e_ml_norm_g, e_gla_gate_up,
              e_gla_gate_b, e_gla_norm_g, e_w_out, e_norm2_g, e_ffn_w_gate, e_ffn_w_up, e_ffn_w_down,
              o_norm1_g, o_w_in, o_ret_norm_g, o_rw_mu, o_rw_w_up, o_rw_w0, o_rw_a_up, o_rw_a0, o_rw_g_up,
              o_rw_k_k, o_rw_k_a, o_rw_r_k, o_rw_ln_g, o_rw_ln_b, o_w_out, o_norm2_g, o_moe_router,
              o_moe_w_gate, o_moe_w_up, o_moe_w_down, final_norm_g):
    h = x
    for layer in range(DEPTH):
        j = layer // 2
        if layer % 2 == 0:
            h = h + even_mixer(rms_norm(h, e_norm1_g[j]), e_w_in[j], e_ml_conv_w[j], e_ml_conv_b[j],
                               e_ml_gate_b[j], e_ml_norm_g[j], e_gla_gate_up[j], e_gla_gate_b[j],
                               e_gla_norm_g[j], e_w_out[j])
            h = h + swiglu(rms_norm(h, e_norm2_g[j]), e_ffn_w_gate[j], e_ffn_w_up[j], e_ffn_w_down[j])
        else:
            h = h + odd_mixer(rms_norm(h, o_norm1_g[j]), o_w_in[j], o_ret_norm_g[j], o_rw_mu[j], o_rw_w_up[j],
                              o_rw_w0[j], o_rw_a_up[j], o_rw_a0[j], o_rw_g_up[j], o_rw_k_k[j], o_rw_k_a[j],
                              o_rw_r_k[j], o_rw_ln_g[j], o_rw_ln_b[j], o_w_out[j])
            h = h + moe_swiglu(rms_norm(h, o_norm2_g[j]), o_moe_router[j], o_moe_w_gate[j], o_moe_w_up[j],
                               o_moe_w_down[j])
    return rms_norm(h, final_norm_g)


_drawn_inputs = setup_inputs


def setup_inputs(seed=0):
    import zlib

    import numpy as np

    out = dict(_drawn_inputs(seed))
    spreads = {}
    factors = {'o_ret_norm_g': 11.606,
     'o_rw_w_up': 8.0,
     'o_rw_k_k': 10.154,
     'o_rw_k_a': 2.776,
     'o_rw_ln_g': 15.368,
     'o_rw_ln_b': 15.687,
     'final_norm_g': 19.362,
     'e_gla_norm_g': 3.243,
     'o_norm2_g': 5.379,
     'o_rw_r_k': 2.793}
    for name, (base, spread) in spreads.items():
        noise = np.random.default_rng([zlib.crc32(name.encode()), seed]).standard_normal(out[name].shape)
        drawn = base * np.exp(spread * noise) if base else spread * noise
        out[name] = __import__('jax').numpy.asarray(drawn.astype(out[name].dtype))
    for name, factor in factors.items():
        out[name] = (out[name] * factor).astype(out[name].dtype)
    return out
```

```python
from collections import namedtuple
from contextlib import ExitStack

import numpy as np
import concourse.bass as bass
from concourse import mybir

F32 = mybir.dt.float32
I32 = mybir.dt.int32
ALU = mybir.AluOpType
ACT = mybir.ActivationFunctionType
AX = mybir.AxisListType

P = 128
T = 256
TH = T // P
D = 1024
KT = D // P
D_FF = 3584
FT = D_FF // P
E = 8
CAP = 96
PASSES = -(-T // CAP)
EPS = 1e-6
RW_LN_EPS = 64e-5
BIG = 1e30
GC = 16
GN = T // GC
RC = 64
RN = T // RC
CH = 512
SLOTS = 5
X_SLOTS = 7
MF = CH // P
FC = D_FF // CH
LEVELS = (1, 2, 4, 8, 16, 32)

CONST_COLS = [
    ("ident", P), ("ones", P), ("head_ones", P), ("head_mean", P), ("mean", P), ("future", T),
    ("reset16", T), ("gla_block", P), ("parity", 2), ("select", 4 * P),
    ("before", P), ("slots", CAP), ("earlier", E * E), ("chunk_of16", 8),
]
RET_COLS = [("rot", P), ("cos", T), ("sin", T), ("decay", 4 * T), ("reset64", T)]
RW_COLS = [("strict", P), ("upto", P), ("levels", len(LEVELS) * P), ("head_cols", 2 * P)]
PARAM_COLS = [
    ("norm1_e", 8), ("conv_w", 32), ("conv_b", 8), ("ml_norm", 4), ("gla_b", 2), ("gla_norm", 4), ("norm2_e", 8),
    ("norm1_o", 8), ("ret_norm", 4), ("mu", 14), ("w0", 4), ("a0", 4), ("k_k", 4), ("k_a", 4), ("r_k", 4),
    ("ln_g", 4), ("ln_b", 4), ("norm2_o", 8), ("final", 8), ("gate_b", 2),
]


FFN_ORDER = [("gate", 0), ("up", 0)]
for _c in range(1, FC):
    FFN_ORDER += [("gate", _c), ("down", _c - 1), ("up", _c)]
FFN_ORDER += [("down", FC - 1)]


def column_ranges(cols):
    at, out = 0, {}
    for name, n in cols:
        out[name] = (at, at + n)
        at += n
    return out, at


CONST_AT, CONST_N = column_ranges(CONST_COLS)
RET_AT, RET_N = column_ranges(RET_COLS)
RW_AT, RW_N = column_ranges(RW_COLS)
PARAM_AT, PARAM_N = column_ranges(PARAM_COLS)


def constants():
    c = {}
    r, t = np.arange(P)[:, None], np.arange(T)[None, :]
    s = t[:, :P]
    c["ident"] = r == s
    c["ones"] = np.ones((P, P))
    c["mean"] = np.full((P, P), 1.0 / P)
    c["head_ones"] = r // 64 == s // 64
    c["head_mean"] = (r // 64 == s // 64) / 64.0
    c["future"] = np.where(t >= r, 0.0, BIG)
    c["rot"] = 1.0 * (s == r + 64) - 1.0 * (s == r - 64)
    inv = np.float32(10000.0) ** (-np.arange(0, P, 2, dtype=np.float32) / np.float32(P))
    ang = np.arange(T, dtype=np.float32)[None, :] * inv[:, None]
    c["cos"] = np.tile(np.cos(ang), (2, 1))
    c["sin"] = np.tile(np.sin(ang), (2, 1))
    gamma = np.log1p(-np.exp2(-5.0 - np.arange(4)))
    c["decay"] = np.concatenate(
        [np.where(t >= r, np.exp(g * (t - r)), 0.0) * P ** -0.5 for g in gamma], axis=1)
    c["reset16"] = np.broadcast_to(t % GC != 0, (P, T))
    c["reset64"] = np.broadcast_to(t % RC != 0, (P, T))
    c["gla_block"] = (r // GC == s // GC) & (r % GC <= s % GC)
    c["parity"] = r // 64 == np.arange(2)[None, :]
    c["chunk_of16"] = r // GC == np.arange(8)[None, :]
    c["select"] = np.repeat(np.arange(4), P)[None, :] == r
    block = r // RC == s // RC
    c["strict"] = block & (r < s)
    c["upto"] = block & (r <= s)
    c["levels"] = np.concatenate([(r // (2 * m) == s // (2 * m)) & (r // m < s // m) for m in LEVELS], axis=1)
    c["before"] = r < s
    c["head_cols"] = np.broadcast_to(np.arange(2 * P)[None, :] // 64 % 2 == np.arange(2 * P)[None, :] // P, (P, 2 * P))
    c["slots"] = np.broadcast_to(np.arange(CAP)[None, :], (P, CAP))
    e = np.arange(E)
    c["earlier"] = np.broadcast_to((e[None, :] < e[:, None]).reshape(1, E * E), (P, E * E))
    pack = lambda cols: np.concatenate([np.asarray(c[n], np.float32) for n, _ in cols], axis=1)
    return pack(CONST_COLS), pack(RET_COLS), pack(RW_COLS)


def Names(**named):
    return namedtuple("Names", named)(**named)


def bc(ap, axis, n):
    a = ap.unsqueeze(axis)
    return a.broadcast_to([*a.shape[:axis], n, *a.shape[axis + 1:]])


def counted(engine, sem):
    n = [0]

    def after(ins):
        n[0] += 1
        ins.then_inc(sem, 1)
        engine.wait_ge(sem, n[0])

    return after


def weight_chunks(g):
    def cols(w, c0, n=CH):
        return w[:, c0:c0 + n].rearrange("(k p) c -> p k c", p=P)

    def rows(w, r0):
        return w[r0:r0 + CH, :].rearrange("(k p) c -> p k c", p=P)

    e_in, o_in = g.e_w_in[0], g.o_w_in[0]
    out = [cols(e_in, c) for c in (2056, 0, 512, 1024, 1536, 2568, 3080)]
    out += [cols(g.e_w_out[0], c) for c in (0, 512)]
    for kind, c in FFN_ORDER:
        out.append({"gate": lambda: cols(g.e_ffn_w_gate[0], c * CH), "up": lambda: cols(g.e_ffn_w_up[0], c * CH),
                    "down": lambda: rows(g.e_ffn_w_down[0], c * CH)}[kind]())
    out += [cols(o_in, c, min(CH, 3840 - c)) for c in (3584, 2560, 2048, 3072, 0, 512, 1024, 1536)]
    out += [cols(g.o_w_out[0], c) for c in (0, 512)]
    return out


E_IN, E_OUT, FFN, O_IN, O_OUT, DENSE = 0, 7, 9, 30, 38, 40


class Program:
    def __init__(self, nc, g, ctx):
        self.nc, self.g, self.ctx = nc, g, ctx
        self.loads = weight_chunks(g)
        self.issued = 0
        self.stage_sems = []
        sb = self.sb
        self.ps = ctx.enter_context(nc.psum_tensor("ps", [P, 8, 512], F32))
        self.ring = sb("ring", [P, SLOTS, 8 * CH])
        self.consts = sb("consts", [P, CONST_N])
        self.params = sb("params", [P, PARAM_N])
        self.res = sb("res", [P, KT, T])
        self.h = sb("h", [P, KT, T])
        self.slot_filled = [self.sem(f"slot_filled{i}") for i in range(SLOTS)]
        self.more_filled = [self.sem(f"slot_filled{i}") for i in range(SLOTS, X_SLOTS)]
        self.chunk_used = self.sem("chunk_used")
        self.stage_sems = []

    def sb(self, name, shape, ctx=None, dt=F32):
        return (ctx or self.ctx).enter_context(self.nc.sbuf_tensor(name, shape, dt))

    def sem(self, name):
        self.stage_sems.append(self.nc.alloc_semaphore(name))
        return self.stage_sems[-1]

    def recycle(self):
        self.nc.clear_and_free_semaphores(self.stage_sems)
        self.nc.all_engine_barrier()
        self.stage_sems = []

    def c(self, name, rows=P):
        a, b = CONST_AT[name]
        return self.consts[0:rows, a:b]

    def p(self, name, i=None, rows=P):
        a, b = PARAM_AT[name]
        return self.params[0:rows, a:b] if i is None else self.params[0:rows, a + i:a + i + 1]

    def bank(self, b, n=1):
        return self.ps[:, b:b + n, :].rearrange("p b c -> p (b c)")

    def chunk(self, n):
        w = self.ring[:, n % SLOTS, :]
        if tuple(self.loads[n].shape) == (P, MF, D):
            return w.rearrange("p (k c) -> p k c", k=MF)
        return w.rearrange("p (k c) -> p k c", k=KT)[:, :, 0:self.loads[n].shape[2]]

    def load_chunks(self, sp, end):
        for n in range(self.issued, min(end, DENSE)):
            if n >= SLOTS:
                sp.wait_ge(self.chunk_used, n - SLOTS + 1)
            sp.dma_start(self.chunk(n), self.loads[n]).then_inc(self.slot_filled[n % SLOTS], 16)
        self.issued = max(self.issued, min(end, DENSE))

    def wait_chunk(self, pe, n):
        pe.wait_ge(self.slot_filled[n % SLOTS], 16 * (n // SLOTS + 1))


def embed(k):
    nc, g = k.nc, k.g
    loaded, turned, kept = k.sem("x_loaded"), k.sem("x_turned"), k.sem("x_kept")
    with ExitStack() as own:
        x = k.sb("x_rows", [P, TH, D], own)
        block = own.enter_context(nc.Block())

        @block.sync
        def _(sp):
            sp.dma_start(k.consts[:, :], g.consts).then_inc(loaded, 16)
            sp.dma_start(x[:, :, :], g.x[0].rearrange("(a p) d -> p a d", p=P)).then_inc(loaded, 16)
            sp.dma_start(k.params[:, :], g.params).then_inc(loaded, 16)
            k.load_chunks(sp, SLOTS)

        @block.tensor
        def _(pe):
            pe.wait_ge(loaded, 48)
            for kt in range(KT):
                for a in range(TH):
                    ins = pe.transpose(k.bank(kt)[:, a * P:(a + 1) * P], x[:, a, kt * P:(kt + 1) * P], k.c("ident"))
                ins.then_inc(turned, 1)

        @block.vector
        def _(dve):
            for kt in range(KT):
                dve.wait_ge(turned, kt + 1)
                dve.tensor_copy(k.res[:, kt, :], k.bank(kt)[:, 0:T]).then_inc(kept, 1)
            dve.wait_ge(kept, KT)


def rms_norm(k, name, gain, end, out=None):
    nc = k.nc
    squared, summed, scaled = k.sem(name + "_squared"), k.sem(name + "_summed"), k.sem(name + "_scaled")
    rooted = k.sem(name + "_rooted")
    with ExitStack() as own:
        sq = k.sb(name + "_sq", [P, KT, T], own)
        rstd = k.sb(name + "_rstd", [P, T], own)
        mean = k.sb(name + "_mean", [P, T], own)
        block = own.enter_context(nc.Block())

        @block.sync
        def _(sp):
            k.load_chunks(sp, end)

        @block.scalar
        def _(act):
            for kt in range(0, KT, 2):
                act.activation(sq[:, kt:kt + 2, :], k.res[:, kt:kt + 2, :], ACT.Square).then_inc(squared, 1)
            act.wait_ge(rooted, 2)
            act.activation(rstd[:, :], mean[:, :], ACT.Sqrt).then_inc(rooted, 1)

        @block.tensor
        def _(pe):
            for kt in range(KT):
                pe.wait_ge(squared, kt // 2 + 1)
                ins = pe.matmul(k.bank(0)[:, 0:T], k.c("ones"), sq[:, kt, :], start=kt == 0, stop=kt == KT - 1)
            ins.then_inc(summed, 1)

        @block.vector
        def _(dve):
            dve.wait_ge(summed, 1)
            dve.tensor_scalar(mean[:, :], k.bank(0)[:, 0:T], 1.0 / D, EPS, ALU.mult, ALU.add).then_inc(rooted, 1)
            dve.wait_ge(rooted, 1)
            dve.reciprocal(mean[:, :], mean[:, :]).then_inc(rooted, 1)
            dve.wait_ge(rooted, 3)
            for kt in range(KT):
                dve.scalar_tensor_tensor(out=(out or k.h)[:, kt, :], in0=k.res[:, kt, :], scalar=k.p(gain, kt),
                                         in1=rstd[:, :], op0=ALU.mult, op1=ALU.mult).then_inc(scaled, 1)
            dve.wait_ge(scaled, KT)


def project(pe, k, n, out, used, tokens_out=False, m_tiles=MF):
    w = k.chunk(n)
    k.wait_chunk(pe, n)
    if tokens_out:
        for a in range(TH):
            for kt in range(KT):
                ins = pe.matmul(out[:, a * CH:(a + 1) * CH], k.h[:, kt, a * P:(a + 1) * P], w[:, kt, :],
                                start=kt == 0, stop=kt == KT - 1)
    else:
        for m in range(m_tiles):
            for kt in range(KT):
                ins = pe.matmul(out[:, m * T:(m + 1) * T], w[:, kt, m * P:(m + 1) * P], k.h[:, kt, :],
                                start=kt == 0, stop=kt == KT - 1)
    return ins.then_inc(used, 1)


def out_project(k, name, n, end, after=None):
    used, added = k.sem(name + "_done"), k.sem(name + "_added")
    with ExitStack() as own:
        block = own.enter_context(k.nc.Block())

        @block.sync
        def _(sp):
            k.load_chunks(sp, end)
            if after:
                after(sp)

        @block.tensor
        def _(pe):
            for i in range(2):
                project(pe, k, n + i, k.bank(4 * i, 2), k.chunk_used)

        @block.vector
        def _(dve):
            for i in range(2):
                dve.wait_ge(k.chunk_used, n + i + 1)
                r = k.res[:, 4 * i:4 * i + 4, :]
                dve.tensor_tensor(r, r, k.bank(4 * i, 2).rearrange("p (m t) -> p m t", m=4), ALU.add).then_inc(added, 1)
            dve.wait_ge(added, 2)


def even_mixer(k):
    with ExitStack() as own:
        sb = lambda n, shape: k.sb("e_" + n, shape, own)
        m = Names(
            gqk=sb("gqk", [P, 4, T]),
            gv=sb("gv", [P, TH, CH]), gr=sb("gr", [P, 4, T]),
            qk=sb("qk", [P, 8, T]),
            v=sb("v", [P, TH, CH]), o=sb("o", [P, 4, T]),
            gates=sb("gates", [4, 10, T]),
            la=sb("la", [P, 4, 2, T]),
            expb=sb("expb", [P, 2, T]),
            kdec=sb("kdec", [P, 2, T]),
            qe=sb("qe", [P, 2, 2, T]),
            pair=sb("pair", [P, 16 * GC * GC]),
            pads=sb("pads", [P, 2, 4, T + 3]),
            att=sb("att", [P, 8, P]),
            tmp=sb("tmp", [P, 4, T]),
        )
        even_project(k, m)
        even_attend(k, m, sb)


(LOG_I, ABS_F, EXP_F, LN_F, NEG_F, LOG_F, SUM_F, U, MAX_U, MAX_M) = range(10)


def even_project(k, m):
    nc, g = k.nc, k.g
    s = Names(**{n: k.sem("ep_" + n) for n in (
        "small_loaded", "small_done", "small_kept", "proj_kept", "low_done", "gates_split", "gates_exp", "gates_ln",
        "decay_summed", "decay_exp", "diff_ready", "pair_exp", "pair_ready", "att_done", "dve_chain", "act_chain",
        "zeroed", "conv_done", "qk_done", "gated")})
    with ExitStack() as own:
        wsm = k.sb("ep_w_small", [P, KT, 24], own)
        gup = k.sb("ep_gate_up", [16, T], own)
        low = k.sb("ep_low", [16, T], own)
        attc = k.sb("ep_attc", [P, 8, GC], own)
        block = own.enter_context(nc.Block())
        icj = m.pair[:, :].rearrange("p (i c j) -> p i c j", i=GC, j=GC)
        flat = m.pair[:, :].rearrange("p (i t) -> p i t", i=GC)

        @block.sync
        def _(sp):
            w = g.e_w_in[0]
            sp.dma_start(wsm[:, :, 0:8], w[:, 2048:2056].rearrange("(k p) c -> p k c", p=P)).then_inc(s.small_loaded, 16)
            sp.dma_start(wsm[:, :, 8:24], w[:, 3592:3608].rearrange("(k p) c -> p k c", p=P)).then_inc(s.small_loaded, 16)
            sp.dma_start(gup[:, :], g.e_gla_gate_up[0]).then_inc(s.small_loaded, 16)
            k.load_chunks(sp, E_OUT + SLOTS)

        @block.gpsimd
        def _(pool):
            pool.memset(m.pads[:, :, :, 0:3], 0.0).then_inc(s.zeroed, 1)
            pool.memset(m.qe[:, :, :, :], 0.0).then_inc(s.zeroed, 1)

        @block.tensor
        def _(pe):
            pe.wait_ge(s.small_loaded, 48)
            for a, b, out in ((0, 4, k.bank(6)[0:4, 0:T]), (4, 8, k.bank(6)[0:4, T:2 * T]), (8, 24, k.bank(7)[0:16, 0:T])):
                for kt in range(KT):
                    ins = pe.matmul(out, wsm[:, kt, a:b], k.h[:, kt, :], start=kt == 0, stop=kt == KT - 1)
            ins.then_inc(s.small_done, 1)
            project(pe, k, 0, k.bank(0, 2), k.chunk_used)
            pe.wait_ge(s.small_kept, 1)
            for i in range(2):
                ins = pe.matmul(k.bank(7)[:, i * T:(i + 1) * T], gup[:, i * P:(i + 1) * P], low[:, :], start=True, stop=True)
            ins.then_inc(s.low_done, 1)
            for n in range(1, 7):
                if n >= 3:
                    pe.wait_ge(s.proj_kept, n - 2)
                project(pe, k, n, k.bank(2 * (n % 3), 2), k.chunk_used, tokens_out=n in (3, 5))
                if n in (4, 6):
                    hp = n // 2 - 2
                    pe.wait_ge(s.pair_ready, hp + 1)
                    for a in range(TH):
                        for i in range(GC):
                            at = (hp * TH + a) * 2
                            ins = pe.matmul(k.bank(6)[:, 0:P].rearrange("p (g i) -> p g i", i=GC)[:, at:at + 2, i],
                                            flat[:, i, a * P:(a + 1) * P], k.c("parity"), start=True, stop=True)
                    ins.then_inc(s.att_done, 1)

        @block.scalar
        def _(act):
            act.wait_ge(s.small_done, 1)
            act.copy(low[:, :], k.bank(7)[0:16, 0:T]).then_inc(s.small_kept, 1)
            act.wait_ge(k.chunk_used, 1)
            act.mul(m.gqk[:, 0:2, :].rearrange("p a t -> p (a t)"), k.bank(0), 64 ** -0.5).then_inc(s.gated, 1)
            act.copy(m.gqk[:, 2:4, :].rearrange("p a t -> p (a t)"), k.bank(1)).then_inc(s.proj_kept, 1)
            act.wait_ge(s.gates_split, 2)
            act.activation(m.gates[:, EXP_F, :], m.gates[:, ABS_F, :], ACT.Exp, scale=-1.0).then_inc(s.gates_exp, 1)
            act.activation(m.la[:, 1, :, :], m.la[:, 0, :, :], ACT.Exp, scale=-1.0).then_inc(s.gates_exp, 1)
            act.wait_ge(s.gates_exp, 2)
            act.activation(m.gates[:, LN_F, :], m.gates[:, EXP_F, :], ACT.Ln, bias=1.0).then_inc(s.gates_ln, 1)
            act.activation(m.la[:, 2, :, :], m.la[:, 1, :, :], ACT.Ln, bias=1.0).then_inc(s.gates_ln, 1)
            act.wait_ge(s.decay_summed, 1)
            act.activation(m.expb[:, :, :], m.la[:, 0, :, :], ACT.Exp).then_inc(s.decay_exp, 1)
            act.activation(m.la[:, 3, :, :], m.la[:, 1, :, :], ACT.Exp).then_inc(s.decay_exp, 1)
            act.wait_ge(s.diff_ready, 1)
            act.activation(m.pair[:, :], m.pair[:, :], ACT.Exp).then_inc(s.pair_exp, 1)
            act.wait_ge(s.zeroed, 1)
            for n in range(1, 7):
                act.wait_ge(k.chunk_used, n + 1)
                if n in (1, 2):
                    act.copy(m.pads[:, n - 1, :, 3:], k.bank(2 * (n % 3), 2).rearrange("p (m t) -> p m t", m=4)).then_inc(s.proj_kept, 1)
                else:
                    dst = (m.v, m.o, m.gv, m.gr)[n - 3]
                    act.copy(dst[:, :, :].rearrange("p a b -> p (a b)"), k.bank(2 * (n % 3), 2)).then_inc(s.proj_kept, 1)
                if n == 5:
                    act.wait_ge(s.diff_ready, 2)
                    act.activation(m.pair[:, :], m.pair[:, :], ACT.Exp).then_inc(s.pair_exp, 1)
            act.wait_ge(s.conv_done, 2)
            act.wait_ge(s.proj_kept, 7)
            act.activation(m.qk[:, :, :], m.qk[:, :, :], ACT.Silu).then_inc(s.gated, 1)
            act.activation(m.gr[:, :, :], m.gr[:, :, :], ACT.Silu).then_inc(s.gated, 1)
            act.activation(m.o[:, :, :], m.o[:, :, :], ACT.Sigmoid).then_inc(s.gated, 1)
            act.wait_ge(s.gated, 4)

        @block.vector
        def _(dve):
            step = counted(dve, s.dve_chain)
            gt = m.gates
            dve.wait_ge(s.small_done, 1)
            step(dve.tensor_scalar(gt[:, LOG_I, :], k.bank(6)[0:4, 0:T], k.p("gate_b", 0, 4), None, ALU.add))
            step(dve.tensor_scalar(gt[:, LOG_F, :], k.bank(6)[0:4, T:2 * T], k.p("gate_b", 1, 4), None, ALU.add))
            step(dve.tensor_scalar(gt[:, NEG_F, :], gt[:, LOG_F, :], 0.0, None, ALU.min))
            step(dve.scalar_tensor_tensor(out=gt[:, ABS_F, :], in0=gt[:, LOG_F, :], scalar=-1.0, in1=gt[:, LOG_F, :],
                                          op0=ALU.mult, op1=ALU.max))
            dve.wait_ge(s.low_done, 1)
            for i in range(2):
                x = k.bank(7)[:, i * T:(i + 1) * T]
                step(dve.tensor_scalar(m.la[:, 2, i, :], x, k.p("gla_b", i), None, ALU.add))
                step(dve.tensor_scalar(m.la[:, 3, i, :], m.la[:, 2, i, :], 0.0, None, ALU.min))
                dve.scalar_tensor_tensor(out=m.la[:, 0, i, :], in0=m.la[:, 2, i, :], scalar=-1.0, in1=m.la[:, 2, i, :],
                                         op0=ALU.mult, op1=ALU.max).then_inc(s.gates_split, 1)
            dve.wait_ge(s.gates_ln, 2)
            step(dve.tensor_tensor(m.la[:, 0, :, :], m.la[:, 3, :, :], m.la[:, 2, :, :], ALU.subtract))
            step(dve.tensor_scalar(m.la[:, 2, :, :], m.la[:, 0, :, :], 1.0 / 16.0, None, ALU.mult))
            for hp in range(2):
                step(dve.tensor_tensor_scan(m.la[:, 0, hp, :], k.c("reset16"), m.la[:, 2, hp, :], 0.0, ALU.mult, ALU.add))
            b = m.la[:, 0, :, :].rearrange("p h (c t) -> p (h c) t", t=GC)
            dve.tensor_tensor(m.la[:, 1, :, :].rearrange("p h (c t) -> p (h c) t", t=GC),
                              b[:, :, GC - 1:GC].broadcast_to([P, 2 * GN, GC]), b, ALU.subtract).then_inc(s.decay_summed, 1)

            def pair_diff(hp):
                bb = m.la[:, 0, hp, :].rearrange("p (c t) -> p c t", t=GC)
                dve.tensor_tensor(icj, bc(bb.rearrange("p c i -> p i c"), 3, GC), bc(bb, 1, GC), ALU.subtract).then_inc(s.diff_ready, 1)

            def pair_product(hp):
                dve.wait_ge(s.pair_exp, hp + 1)
                step(dve.scalar_tensor_tensor(out=flat, in0=flat, scalar=1.0, in1=bc(m.gqk[:, 2 + hp, :], 1, GC),
                                              op0=ALU.min, op1=ALU.mult))
                q = m.gqk[:, hp, :].rearrange("p (c i) -> p i c", i=GC)
                dve.tensor_tensor(icj, icj, bc(q, 3, GC), ALU.mult).then_inc(s.pair_ready, 1)

            def conv(n):
                dve.wait_ge(s.proj_kept, n + 1)
                for i in range(4):
                    ch = (n - 1) * 4 + i
                    step(dve.tensor_scalar(m.tmp[:, i, :], m.pads[:, n - 1, i, 3:], k.p("conv_w", 24 + ch),
                                           k.p("conv_b", ch), ALU.mult, ALU.add))
                    for tap in (2, 1, 0):
                        out = m.tmp[:, i, :] if tap else m.qk[:, ch, :]
                        step(dve.scalar_tensor_tensor(out=out, in0=m.pads[:, n - 1, i, tap:tap + T],
                                                      scalar=k.p("conv_w", tap * 8 + ch), in1=m.tmp[:, i, :],
                                                      op0=ALU.mult, op1=ALU.add))
                dve.sem_inc(s.conv_done, 1)

            pair_diff(0)
            step(dve.tensor_tensor(gt[:, LOG_F, :], gt[:, NEG_F, :], gt[:, LN_F, :], ALU.subtract))
            step(dve.tensor_tensor_scan(gt[:, SUM_F, :], k.c("ones", 4)[:, 0:1].broadcast_to([4, T]), gt[:, LOG_F, :], 0.0,
                                        ALU.mult, ALU.add))
            step(dve.tensor_tensor(gt[:, U, :], gt[:, LOG_I, :], gt[:, SUM_F, :], ALU.subtract))
            step(dve.tensor_tensor_scan(gt[:, MAX_U, :], gt[:, U, :], gt[:, U, :], 0.0, ALU.max, ALU.max))
            step(dve.tensor_tensor(gt[:, MAX_M, :], gt[:, MAX_U, :], gt[:, SUM_F, :], ALU.add))
            dve.wait_ge(s.decay_exp, 2)
            dve.wait_ge(s.zeroed, 2)
            dve.wait_ge(s.proj_kept, 1)
            dve.wait_ge(s.gated, 1)
            for hd in range(2):
                r = slice(64 * hd, 64 * hd + 64)
                step(dve.tensor_tensor(m.qe[r, :, hd, :], m.gqk[r, 0:2, :], m.expb[r, :, :], ALU.mult))
            step(dve.tensor_tensor(m.kdec[:, :, :], m.gqk[:, 2:4, :], m.la[:, 3, :, :], ALU.mult))
            pair_product(0)
            conv(1)
            conv(2)
            dve.wait_ge(s.att_done, 1)
            pair_diff(1)
            pair_product(1)
            dve.wait_ge(s.att_done, 2)
            step(dve.tensor_copy(attc[:, :, :], k.bank(6)[:, 0:P].rearrange("p (g i) -> p g i", i=GC)))
            blocks = k.c("gla_block").rearrange("p (c i) -> p c i", i=GC)
            step(dve.tensor_tensor(m.att[:, :, :].rearrange("p g (c i) -> p g c i", i=GC), bc(attc[:, :, :], 2, 8),
                                   bc(blocks, 1, 8), ALU.mult))


def even_attend(k, m, sb):
    nc = k.nc
    s = Names(**{n: k.sem("ea_" + n) for n in (
        "turned", "turned_kept", "spread", "spread_kept", "spread_exp", "limited", "weighted", "scored", "p_ready",
        "num_done", "gated", "mean_done", "centred", "squared", "var_done", "mixed", "u_done", "state_ready",
        "inter_done", "dve_chain", "inverted", "rooted", "gla_squared", "gla_var_done", "gla_mixed")})
    with ExitStack() as own:
        ucol = k.sb("ea_u_cols", [P, TH, 4], own)
        wts = k.sb("ea_wts", [P, 4, T + P], own)
        ot = m.gqk
        spread = m.la[:, :, :, :].rearrange("p a b t -> p a (b t)")
        kex = m.pair[:, :].rearrange("p (g c f) -> p g c f", c=8, f=P)
        pads = m.pads[:, :, :, :].rearrange("p a b t -> p (a b t)")
        state = pads[:, 0:8 * T].rearrange("p (c a t) -> p c a t", c=4, a=2)
        tmp = m.tmp
        block = own.enter_context(nc.Block())

        @block.sync
        def _(sp):
            k.load_chunks(sp, E_OUT + SLOTS)

        def inter(pe, c):
            pe.wait_ge(s.state_ready, c + 1)
            for hd in range(4):
                b = k.bank(4 + hd // 2)[:, (hd % 2) * T + c * GC:(hd % 2) * T + (c + 1) * GC]
                ins = pe.matmul(b, state[:, c % 4, hd // 2, (hd % 2) * P:(hd % 2 + 1) * P],
                                m.qe[:, hd // 2, hd % 2, c * GC:(c + 1) * GC], start=False, stop=False, skip_group_check=True)
            return ins.then_inc(s.inter_done, 1)

        @block.tensor
        def _(pe):
            for a in range(TH):
                pe.transpose(k.bank(6)[:, a * 4:a * 4 + 4], m.gates[:, U, a * P:(a + 1) * P], k.c("ident", 4)[:, 0:4])
            for gi in range(4):
                ins = pe.transpose(k.bank(7)[:, gi * P:(gi + 1) * P], m.kdec[:, gi // 2, (gi % 2) * P:(gi % 2 + 1) * P], k.c("ident"))
            ins.then_inc(s.turned, 1)
            for hd in range(4):
                ins = pe.matmul(k.bank(hd), k.c("select", 4)[:, hd * P:(hd + 1) * P], m.gates[:, MAX_U:MAX_U + 2, :],
                                start=True, stop=True)
            ins.then_inc(s.spread, 1)
            pe.wait_ge(s.turned_kept, 2)
            for hd in range(4):
                b = k.bank(4 + hd)
                pe.matmul(b[:, 0:T], m.qk[:, 4 + hd, 0:P], m.qk[:, hd, :], start=True, stop=True)
                pe.matmul(b[:, T:T + P], m.qk[:, 4 + hd, P:T], m.qk[:, hd, P:T], start=True, stop=True).then_inc(s.scored, 1)
            pe.wait_ge(s.spread_kept, 1)
            for hd in range(4):
                pe.wait_ge(s.p_ready, hd + 1)
                b = k.bank(hd)
                cols = slice(hd * P, (hd + 1) * P)
                for w0, w1, at in ((m.v[:, 0, cols], m.v[:, 1, cols], 0), (k.c("ones"), k.c("ones"), T)):
                    pe.matmul(b[:, at:at + T], w0, wts[:, hd, 0:T], start=True, stop=False, skip_group_check=True)
                    ins = pe.matmul(b[:, at + P:at + T], w1, wts[:, hd, T:T + P], start=False, stop=True, skip_group_check=True)
                ins.then_inc(s.num_done, 1)
            for hd in range(4):
                for a in range(TH):
                    b = k.bank(4 + hd // 2)[:, (hd % 2) * T + a * P:(hd % 2) * T + (a + 1) * P]
                    pe.matmul(b, m.gv[:, a, hd * P:(hd + 1) * P], m.att[:, ((hd // 2) * TH + a) * 2 + hd % 2, :],
                              start=hd % 2 == 0 and a == 0, stop=False, skip_group_check=True)
            for ready, sums, done in ((s.gated, 0, s.mean_done), (s.squared, 2, s.var_done)):
                pe.wait_ge(ready, 4 if ready is s.gated else 1)
                src = ot if ready is s.gated else tmp
                for i in range(2):
                    ins = pe.matmul(k.bank(sums + i), k.c("mean"), src[:, 2 * i:2 * i + 2, :], start=True, stop=True)
                ins.then_inc(done, 1)
            for c in range(GN - 1):
                if c >= 2:
                    pe.wait_ge(s.state_ready, c)
                for hp in range(2):
                    ins = pe.matmul(k.bank(6 + c % 2)[:, hp * T:(hp + 1) * T], kex[:, hp * 2 + c // 8, c % 8, :],
                                    m.gv[:, c // 8, hp * T:(hp + 1) * T], start=True, stop=True)
                ins.then_inc(s.u_done, 1)
                if c >= 1:
                    inter(pe, c)
            inter(pe, GN - 1)
            pe.wait_ge(s.gla_squared, 1)
            for i in range(2):
                ins = pe.matmul(k.bank(6 + i), k.c("mean"), tmp[:, 2 * i:2 * i + 2, :], start=True, stop=True)
            ins.then_inc(s.gla_var_done, 1)

        @block.scalar
        def _(act):
            act.wait_ge(s.spread, 1)
            act.copy(spread.rearrange("p h c -> p (h c)"), k.bank(0, 4)).then_inc(s.spread_kept, 1)
            act.wait_ge(s.spread_kept, 1)
            act.activation(spread[:, :, T:2 * T], spread[:, :, T:2 * T], ACT.Exp, scale=-1.0).then_inc(s.spread_exp, 1)
            for hd in range(4):
                act.wait_ge(s.limited, 2 * hd + 2)
                act.activation(wts[:, hd, :], wts[:, hd, :], ACT.Exp, scale=-1.0).then_inc(s.weighted, 1)
            act.wait_ge(s.centred, 1)
            act.activation(tmp[:, :, :], ot[:, :, :], ACT.Square).then_inc(s.squared, 1)
            act.wait_ge(s.inverted, 1)
            act.activation(tmp[:, :, :], tmp[:, :, :], ACT.Sqrt).then_inc(s.rooted, 1)
            act.wait_ge(s.inter_done, GN - 1)
            act.wait_ge(s.mixed, 1)
            act.activation(tmp[:, :, :].rearrange("p h t -> p (h t)"), k.bank(4, 2), ACT.Square).then_inc(s.gla_squared, 1)
            act.wait_ge(s.inverted, 2)
            act.activation(tmp[:, :, :], tmp[:, :, :], ACT.Sqrt).then_inc(s.rooted, 1)

        @block.vector
        def _(dve):
            step = counted(dve, s.dve_chain)
            dve.wait_ge(s.turned, 1)
            dve.tensor_copy(ucol[:, :, :], k.bank(6)[:, 0:8].rearrange("p (a h) -> p a h", a=TH)).then_inc(s.turned_kept, 1)
            kt = k.bank(7).rearrange("p (g f) -> p g f", f=P)
            in_chunk = bc(k.c("chunk_of16"), 2, P)
            for gi in range(4):
                ins = dve.tensor_tensor(kex[:, gi, :, :], bc(kt[:, gi, :], 1, 8), in_chunk, ALU.mult)
                if gi < 3:
                    step(ins)
            ins.then_inc(s.turned_kept, 1)
            dve.wait_ge(s.spread_kept, 1)
            dve.wait_ge(s.turned_kept, 1)
            for hd in range(4):
                dve.scalar_tensor_tensor(out=wts[:, hd, 0:T], in0=spread[:, hd, 0:T], scalar=ucol[:, 0, hd:hd + 1],
                                         in1=k.c("future"), op0=ALU.subtract, op1=ALU.max).then_inc(s.limited, 1)
                dve.scalar_tensor_tensor(out=wts[:, hd, T:T + P], in0=spread[:, hd, P:T], scalar=ucol[:, 1, hd:hd + 1],
                                         in1=k.c("future")[:, 0:P], op0=ALU.subtract, op1=ALU.max).then_inc(s.limited, 1)
            for hd in range(4):
                dve.wait_ge(s.weighted, hd + 1)
                dve.wait_ge(s.scored, hd + 1)
                dve.scalar_tensor_tensor(out=wts[:, hd, :], in0=k.bank(4 + hd)[:, 0:T + P], scalar=P ** -0.5,
                                         in1=wts[:, hd, :], op0=ALU.mult, op1=ALU.mult).then_inc(s.p_ready, 1)
            dve.wait_ge(s.spread_exp, 1)
            for hd in range(4):
                dve.wait_ge(s.num_done, hd + 1)
                step(dve.tensor_copy(tmp[:, hd, :], k.bank(hd)[:, T:2 * T]))
                step(dve.scalar_tensor_tensor(out=tmp[:, hd, :], in0=tmp[:, hd, :], scalar=-1.0, in1=tmp[:, hd, :],
                                              op0=ALU.mult, op1=ALU.max))
                step(dve.tensor_tensor(tmp[:, hd, :], tmp[:, hd, :], spread[:, hd, T:2 * T], ALU.max))
                step(dve.reciprocal(tmp[:, hd, :], tmp[:, hd, :]))
                step(dve.tensor_tensor(ot[:, hd, :], k.bank(hd)[:, 0:T], tmp[:, hd, :], ALU.mult))
                dve.tensor_tensor(ot[:, hd, :], ot[:, hd, :], m.o[:, hd, :], ALU.mult).then_inc(s.gated, 1)
            dve.wait_ge(s.gated, 4)
            dve.wait_ge(s.mean_done, 1)
            flat = lambda a: a.rearrange("p h t -> p (h t)")
            dve.tensor_tensor(flat(ot[:, :, :]), flat(ot[:, :, :]), k.bank(0, 2), ALU.subtract).then_inc(s.centred, 1)
            dve.wait_ge(s.centred, 1)
            dve.wait_ge(s.var_done, 1)
            step(dve.tensor_scalar(flat(tmp[:, :, :]), k.bank(2, 2), EPS, None, ALU.add))
            dve.reciprocal(tmp[:, :, :], tmp[:, :, :]).then_inc(s.inverted, 1)
            dve.wait_ge(s.rooted, 1)
            for hd in range(4):
                ins = dve.scalar_tensor_tensor(out=k.h[:, hd, :], in0=ot[:, hd, :], scalar=k.p("ml_norm", hd),
                                               in1=tmp[:, hd, :], op0=ALU.mult, op1=ALU.mult)
                if hd < 3:
                    step(ins)
            ins.then_inc(s.mixed, 1)
            for c in range(GN - 1):
                dve.wait_ge(s.u_done, c + 1)
                if c == 0:
                    dve.memset(state[:, 0, :, :], 0.0).then_inc(s.state_ready, 1)
                    dve.wait_ge(s.state_ready, 1)
                if c >= 4:
                    dve.wait_ge(s.inter_done, c - 3)
                for hp in range(2):
                    ins = dve.scalar_tensor_tensor(out=state[:, (c + 1) % 4, hp, :], in0=state[:, c % 4, hp, :],
                                                   scalar=m.expb[:, hp, c * GC + GC - 1:c * GC + GC],
                                                   in1=k.bank(6 + c % 2)[:, hp * T:(hp + 1) * T], op0=ALU.mult, op1=ALU.add)
                    if hp == 0:
                        step(ins)
                ins.then_inc(s.state_ready, 1)
                dve.wait_ge(s.state_ready, c + 2)
            dve.wait_ge(s.gla_var_done, 1)
            step(dve.tensor_scalar(flat(tmp[:, :, :]), k.bank(6, 2), EPS, None, ALU.add))
            dve.reciprocal(tmp[:, :, :], tmp[:, :, :]).then_inc(s.inverted, 1)
            dve.wait_ge(s.rooted, 2)
            step(dve.tensor_tensor(flat(tmp[:, :, :]), flat(tmp[:, :, :]), k.bank(4, 2), ALU.mult))
            for hd in range(4):
                step(dve.scalar_tensor_tensor(out=k.h[:, 4 + hd, :], in0=tmp[:, hd, :], scalar=k.p("gla_norm", hd),
                                              in1=m.gr[:, hd, :], op0=ALU.mult, op1=ALU.mult))


def dense_ffn(k):
    with ExitStack() as own:
        s = Names(**{n: k.sem("ffn_" + n) for n in ("gate_done", "up_done", "gate_kept", "act_ready", "down_done", "added")})
        gate = k.sb("ffn_gate", [P, 2, MF, T], own)
        hid = k.sb("ffn_hidden", [P, 2, MF, T], own)
        block = own.enter_context(k.nc.Block())
        flat = lambda a: a.rearrange("p m t -> p (m t)")

        @block.sync
        def _(sp):
            k.load_chunks(sp, O_IN + SLOTS)

        @block.tensor
        def _(pe):
            for i, (kind, c) in enumerate(FFN_ORDER):
                n = FFN + i
                k.wait_chunk(pe, n)
                w = k.chunk(n)
                if kind == "down":
                    pe.wait_ge(s.act_ready, c + 1)
                    for m in range(KT):
                        for f in range(MF):
                            first = c == 0 and m % 2 == 0 and f == 0
                            ins = pe.matmul(k.bank(4 + m // 2)[:, (m % 2) * T:(m % 2 + 1) * T], w[:, f, m * P:(m + 1) * P],
                                            hid[:, c % 2, f, :], start=first, stop=c == FC - 1 and f == MF - 1,
                                            skip_group_check=True)
                else:
                    if c >= 1:
                        pe.wait_ge(s.gate_kept if kind == "gate" else s.act_ready, c)
                    for m in range(MF):
                        out = k.bank(0 if kind == "gate" else 2, 2)[:, m * T:(m + 1) * T]
                        for kt in range(KT):
                            ins = pe.matmul(out, w[:, kt, m * P:(m + 1) * P], k.h[:, kt, :], start=kt == 0, stop=kt == KT - 1)
                ins.then_inc(k.chunk_used, 1)

        @block.scalar
        def _(act):
            for c in range(FC):
                act.wait_ge(k.chunk_used, FFN + FFN_ORDER.index(("gate", c)) + 1)
                if c >= 2:
                    act.wait_ge(s.act_ready, c - 1)
                act.activation(flat(gate[:, c % 2, :, :]), k.bank(0, 2), ACT.Silu).then_inc(s.gate_kept, 1)

        @block.vector
        def _(dve):
            for c in range(FC):
                dve.wait_ge(k.chunk_used, FFN + FFN_ORDER.index(("up", c)) + 1)
                dve.wait_ge(s.gate_kept, c + 1)
                if c >= 2:
                    dve.wait_ge(k.chunk_used, FFN + FFN_ORDER.index(("down", c - 2)) + 1)
                dve.tensor_tensor(flat(hid[:, c % 2, :, :]), flat(gate[:, c % 2, :, :]), k.bank(2, 2), ALU.mult).then_inc(s.act_ready, 1)
            dve.wait_ge(k.chunk_used, O_IN)
            for i in range(2):
                r = flat(k.res[:, 4 * i:4 * i + 4, :])
                dve.tensor_tensor(r, r, k.bank(4 + 2 * i, 2), ALU.add).then_inc(s.added, 1)
            dve.wait_ge(s.added, 2)


def odd_mixer(k):
    with ExitStack() as own:
        m = Names(**{n: k.sb("o_" + n, [P, 4, T], own) for n in (
            "r",
            "kh",
            "a",
            "kk",
            "v", "g",
            "bonus")},
            chunk_decay=k.sb("o_chunk_decay", [P, 4, RN], own))
        with ExitStack() as early:
            e = Names(**{n: k.sb("o_" + n, [P, 4, T], early) for n in ("ret_q", "ret_k", "ret_g")},
                      ret_v=k.sb("o_ret_v", [P, TH, CH], early), consts=k.sb("o_ret_consts", [P, RET_N], early))
            odd_project(k, m, e)
            retention(k, e)
        rwkv(k, m)


def odd_project(k, m, e):
    nc, g = k.nc, k.g
    s = Names(**{n: k.sem("op_" + n) for n in (
        "loaded", "zeroed", "proj_kept", "mixed_low", "low_ready", "up_done", "extra_kept", "decay_summed", "exp_ready",
        "kk_squared", "bonus_ready", "dve_chain", "chunk_read", "act_chain")})
    rc = lambda n: e.consts[:, RET_AT[n][0]:RET_AT[n][1]]
    with ExitStack() as own:
        sb = lambda n, shape: k.sb("op_" + n, shape, own)
        ups = sb("ups", [P, 3, CH])
        pads = sb("pads", [P, 2, 4, T + 1])
        lowp = sb("low_pads", [P, 2, T + 1])
        low = sb("low", [P, 2, T])
        lw, b, en = sb("log_w", [P, 4, T]), sb("sum_w", [P, 4, T]), sb("exp_minus", [P, 4, T])
        block = own.enter_context(nc.Block())
        flat = lambda a: a.rearrange("p m t -> p (m t)")

        @block.sync
        def _(sp):
            sp.dma_start(e.consts[:, :], g.ret_consts).then_inc(s.loaded, 16)
            sp.wait_ge(s.zeroed, 1)
            sp.dma_start(ups[0:64, 0, :], g.o_rw_w_up[0]).then_inc(s.loaded, 16)
            sp.dma_start(ups[64:P, 1, :], g.o_rw_a_up[0]).then_inc(s.loaded, 16)
            sp.dma_start(ups[:, 2, :], g.o_rw_g_up[0]).then_inc(s.loaded, 16)
            k.load_chunks(sp, O_OUT + SLOTS)

        @block.gpsimd
        def _(pool):
            pool.memset(ups[:, :, :], 0.0).then_inc(s.zeroed, 1)
            pool.memset(pads[:, :, :, 0:1], 0.0).then_inc(s.zeroed, 1)
            pool.memset(lowp[:, :, 0:1], 0.0).then_inc(s.zeroed, 1)

        @block.tensor
        def _(pe):
            def extra(i, lhsT, rhs, ready, value, tiles=4):
                pe.wait_ge(ready, value)
                if i:
                    pe.wait_ge(s.extra_kept, i)
                for t in range(tiles):
                    ins = pe.matmul(k.bank(6, 2)[:, t * T:(t + 1) * T], lhsT(t), rhs(t), start=True, stop=True)
                ins.then_inc(s.up_done, 1)

            head = lambda t: k.c("head_ones")
            up = lambda i: lambda t: ups[:, i, t * P:(t + 1) * P]
            for i in range(8):
                if i >= 3:
                    pe.wait_ge(s.proj_kept, i - 2)
                project(pe, k, O_IN + i, k.bank(2 * (i % 3), 2), k.chunk_used, tokens_out=i == 6, m_tiles=2 if i == 0 else 4)
                if i == 1:
                    pe.wait_ge(s.loaded, 64)
                    extra(0, up(0), lambda t: low[:, 0, :], s.low_ready, 3)
                if i == 2:
                    extra(1, up(1), lambda t: low[:, 0, :], s.low_ready, 3)
                if i == 3:
                    extra(2, head, lambda t: en[:, t, :], s.kk_squared, 1)
                if i == 4:
                    extra(3, up(2), lambda t: low[:, 1, :], s.low_ready, 3)
                if i == 5:
                    extra(4, head, lambda t: m.bonus[:, t, :], s.bonus_ready, 1)

        @block.scalar
        def _(act):
            def keep(i, dst):
                act.wait_ge(k.chunk_used, O_IN + i + 1)
                act.copy(dst, k.bank(2 * (i % 3), 2).rearrange("p (m t) -> p m t", t=dst.shape[2])[:, 0:dst.shape[1], :])\
                   .then_inc(s.proj_kept, 1)

            act.wait_ge(s.zeroed, 3)
            keep(0, lowp[:, :, 1:])
            act.wait_ge(s.mixed_low, 1)
            act.activation(low[0:64, 0, :], low[0:64, 0, :], ACT.Tanh).then_inc(s.low_ready, 2)
            act.activation(low[:, 1, :], low[:, 1, :], ACT.Sigmoid).then_inc(s.low_ready, 1)
            keep(1, pads[:, 0, :, 1:])
            act.wait_ge(s.up_done, 1)
            for t in range(4):
                ins = act.activation(lw[:, t, :], k.bank(6, 2)[:, t * T:(t + 1) * T], ACT.Sigmoid, bias=k.p("w0", t))
            ins.then_inc(s.extra_kept, 1)
            keep(2, pads[:, 1, :, 1:])
            act.wait_ge(s.up_done, 2)
            for t in range(4):
                ins = act.activation(m.a[:, t, :], k.bank(6, 2)[:, t * T:(t + 1) * T], ACT.Sigmoid, bias=k.p("a0", t))
            ins.then_inc(s.extra_kept, 1)
            act.wait_ge(s.chunk_read, 1)
            keep(3, pads[:, 0, :, 1:])
            act.wait_ge(s.up_done, 3)
            act.activation(flat(en[:, :, :]), k.bank(6, 2), ACT.Sqrt).then_inc(s.extra_kept, 1)
            keep(4, e.ret_q[:, :, :])
            act.wait_ge(s.up_done, 4)
            act.copy(flat(m.g[:, :, :]), k.bank(6, 2)).then_inc(s.extra_kept, 1)
            keep(5, e.ret_k[:, :, :])
            act.wait_ge(s.decay_summed, 2)
            act.activation(en[:, :, :], b[:, :, :], ACT.Exp, scale=-1.0).then_inc(s.exp_ready, 1)
            act.wait_ge(s.exp_ready, 1)
            act.activation(b[:, :, :], b[:, :, :], ACT.Exp).then_inc(s.exp_ready, 1)
            act.activation(lw[:, :, :], lw[:, :, :], ACT.Exp).then_inc(s.exp_ready, 1)
            keep(6, e.ret_v[:, :, :])
            keep(7, e.ret_g[:, :, :])
            act.wait_ge(s.proj_kept, 8)
            act.activation(e.ret_g[:, :, :], e.ret_g[:, :, :], ACT.Silu).then_inc(s.act_chain, 1)
            act.wait_ge(s.act_chain, 1)

        @block.vector
        def _(dve):
            step = counted(dve, s.dve_chain)

            def shift_mix(dst, src, mu, tiles):
                step(dve.tensor_tensor(dst, src[:, :, 0:T], src[:, :, 1:], ALU.subtract))
                for t in range(tiles):
                    ins = dve.scalar_tensor_tensor(out=dst[:, t, :], in0=dst[:, t, :], scalar=k.p("mu", mu + t),
                                                   in1=src[:, t, 1:], op0=ALU.mult, op1=ALU.add)
                    if t < tiles - 1:
                        step(ins)
                return ins

            dve.wait_ge(s.proj_kept, 1)
            shift_mix(low[:, :, :], lowp[:, :, :], 12, 2).then_inc(s.mixed_low, 1)
            dve.wait_ge(s.proj_kept, 2)
            shift_mix(m.kh[:, :, :], pads[:, 0, :, :], 4, 4).then_inc(s.chunk_read, 1)
            dve.wait_ge(s.chunk_read, 1)
            for t in range(4):
                step(dve.tensor_scalar(m.kk[:, t, :], m.kh[:, t, :], k.p("k_k", t), None, ALU.mult))
            dve.tensor_tensor(en[:, :, :], m.kk[:, :, :], m.kk[:, :, :], ALU.mult).then_inc(s.kk_squared, 1)
            dve.wait_ge(s.extra_kept, 1)
            step(dve.tensor_scalar(lw[:, :, :], lw[:, :, :], -float(np.exp(-0.5)), None, ALU.mult))
            for t in range(4):
                step(dve.tensor_tensor_scan(b[:, t, :], rc("reset64"), lw[:, t, :], 0.0, ALU.mult, ALU.add))
            step(dve.tensor_tensor(lw[:, :, :], b[:, :, :], lw[:, :, :], ALU.subtract))
            dve.wait_ge(s.proj_kept, 3)
            step(shift_mix(m.r[:, :, :], pads[:, 1, :, :], 0, 4))
            dve.wait_ge(s.extra_kept, 2)
            for t in range(4):
                step(dve.tensor_scalar(m.bonus[:, t, :], m.a[:, t, :], -1.0, k.p("k_a", t), ALU.add, ALU.mult))
            step(dve.scalar_tensor_tensor(out=flat(m.kh[:, :, :]), in0=flat(m.bonus[:, :, :]), scalar=1.0, in1=flat(m.kh[:, :, :]),
                                          op0=ALU.add, op1=ALU.mult))
            for t in range(4):
                ins = dve.scalar_tensor_tensor(out=m.bonus[:, t, :], in0=m.r[:, t, :], scalar=k.p("r_k", t),
                                               in1=m.kh[:, t, :], op0=ALU.mult, op1=ALU.mult)
                if t < 3:
                    step(ins)
            ins.then_inc(s.bonus_ready, 1)
            dve.wait_ge(s.proj_kept, 4)
            step(shift_mix(m.v[:, :, :], pads[:, 0, :, :], 8, 4))
            dve.wait_ge(s.extra_kept, 3)
            step(dve.tensor_scalar(en[:, :, :], en[:, :, :], 1e-12, None, ALU.max))
            step(dve.reciprocal(en[:, :, :], en[:, :, :]))
            dve.tensor_tensor(m.kk[:, :, :], m.kk[:, :, :], en[:, :, :], ALU.mult).then_inc(s.decay_summed, 2)
            dve.wait_ge(s.decay_summed, 2)
            step(dve.tensor_tensor(m.a[:, :, :], m.a[:, :, :], m.kk[:, :, :], ALU.mult))
            dve.wait_ge(s.up_done, 5)
            step(dve.tensor_tensor(flat(m.bonus[:, :, :]), k.bank(6, 2), flat(m.v[:, :, :]), ALU.mult))
            dve.wait_ge(s.exp_ready, 3)
            step(dve.tensor_tensor(m.r[:, :, :], m.r[:, :, :], b[:, :, :], ALU.mult))
            step(dve.scalar_tensor_tensor(out=flat(m.kk[:, :, :]), in0=flat(m.kk[:, :, :]), scalar=-1.0, in1=flat(lw[:, :, :]),
                                          op0=ALU.mult, op1=ALU.mult))
            step(dve.tensor_tensor(m.kh[:, :, :], m.kh[:, :, :], en[:, :, :], ALU.mult))
            step(dve.tensor_tensor(m.a[:, :, :], m.a[:, :, :], en[:, :, :], ALU.mult))
            step(dve.tensor_copy(m.chunk_decay[:, :, :], b[:, :, RC - 1::RC]))


def retention(k, e):
    nc = k.nc
    s = Names(**{n: k.sem("rt_" + n) for n in (
        "turned", "rotated", "scored", "p_ready", "o_done", "o_kept", "mean_done", "centred", "squared", "var_done",
        "inverted", "rooted", "dve_chain")})
    rc = lambda n: e.consts[:, RET_AT[n][0]:RET_AT[n][1]]
    with ExitStack() as own:
        wts = k.sb("rt_wts", [P, 4, T + P], own)
        ot, tmp = (k.sb("rt_" + n, [P, 4, T], own) for n in ("ot", "tmp"))
        block = own.enter_context(nc.Block())
        flat = lambda a: a.rearrange("p m t -> p (m t)")

        @block.sync
        def _(sp):
            k.load_chunks(sp, O_OUT + SLOTS)

        @block.tensor
        def _(pe):
            for i, src in enumerate((e.ret_q, e.ret_k)):
                for j in range(2):
                    ins = pe.matmul(k.bank(2 * i + j), rc("rot"), src[:, 2 * j:2 * j + 2, :], start=True, stop=True)
                ins.then_inc(s.turned, 1)
            pe.wait_ge(s.rotated, 2)
            for hd in range(4):
                b = k.bank(4 + hd)
                pe.matmul(b[:, 0:T], e.ret_k[:, hd, 0:P], e.ret_q[:, hd, :], start=True, stop=True)
                pe.matmul(b[:, T:T + P], e.ret_k[:, hd, P:T], e.ret_q[:, hd, P:T], start=True, stop=True).then_inc(s.scored, 1)
            for hd in range(4):
                pe.wait_ge(s.p_ready, hd + 1)
                cols = slice(hd * P, (hd + 1) * P)
                b = k.bank(hd)
                pe.matmul(b[:, 0:T], e.ret_v[:, 0, cols], wts[:, hd, 0:T], start=True, stop=False, skip_group_check=True)
                pe.matmul(b[:, P:T], e.ret_v[:, 1, cols], wts[:, hd, T:T + P], start=False, stop=True,
                          skip_group_check=True).then_inc(s.o_done, 1)
            pe.wait_ge(s.o_kept, 4)
            for i in range(2):
                ins = pe.matmul(k.bank(4 + i), k.c("mean"), ot[:, 2 * i:2 * i + 2, :], start=True, stop=True)
            ins.then_inc(s.mean_done, 1)
            pe.wait_ge(s.squared, 1)
            for i in range(2):
                ins = pe.matmul(k.bank(6 + i), k.c("mean"), tmp[:, 2 * i:2 * i + 2, :], start=True, stop=True)
            ins.then_inc(s.var_done, 1)

        @block.scalar
        def _(act):
            for hd in range(4):
                act.wait_ge(s.o_done, hd + 1)
                act.copy(ot[:, hd, :], k.bank(hd)[:, 0:T]).then_inc(s.o_kept, 1)
            act.wait_ge(s.centred, 1)
            act.activation(tmp[:, :, :], ot[:, :, :], ACT.Square).then_inc(s.squared, 1)
            act.wait_ge(s.inverted, 1)
            act.activation(tmp[:, :, :], tmp[:, :, :], ACT.Sqrt).then_inc(s.rooted, 1)

        @block.vector
        def _(dve):
            step = counted(dve, s.dve_chain)
            for i, x in enumerate((e.ret_q, e.ret_k)):
                dve.wait_ge(s.turned, i + 1)
                step(dve.tensor_tensor(tmp[:, :, :], k.bank(2 * i, 2).rearrange("p (m t) -> p m t", m=4), bc(rc("sin"), 1, 4), ALU.mult))
                step(dve.tensor_tensor(x[:, :, :], x[:, :, :], bc(rc("cos"), 1, 4), ALU.mult))
                dve.tensor_tensor(x[:, :, :], x[:, :, :], tmp[:, :, :], ALU.add).then_inc(s.rotated, 1)
                dve.wait_ge(s.rotated, i + 1)
            decay = rc("decay").rearrange("p (h t) -> p h t", h=4)
            for hd in range(4):
                dve.wait_ge(s.scored, hd + 1)
                step(dve.tensor_tensor(wts[:, hd, 0:T], k.bank(4 + hd)[:, 0:T], decay[:, hd, :], ALU.mult))
                dve.tensor_tensor(wts[:, hd, T:T + P], k.bank(4 + hd)[:, T:T + P], decay[:, hd, 0:P], ALU.mult).then_inc(s.p_ready, 1)
            dve.wait_ge(s.mean_done, 1)
            dve.wait_ge(s.o_kept, 4)
            dve.tensor_tensor(flat(ot[:, :, :]), flat(ot[:, :, :]), k.bank(4, 2), ALU.subtract).then_inc(s.centred, 1)
            dve.wait_ge(s.var_done, 1)
            step(dve.tensor_scalar(flat(tmp[:, :, :]), k.bank(6, 2), EPS, None, ALU.add))
            dve.reciprocal(tmp[:, :, :], tmp[:, :, :]).then_inc(s.inverted, 1)
            dve.wait_ge(s.rooted, 1)
            step(dve.tensor_tensor(tmp[:, :, :], tmp[:, :, :], ot[:, :, :], ALU.mult))
            for hd in range(4):
                step(dve.scalar_tensor_tensor(out=k.h[:, hd, :], in0=tmp[:, hd, :], scalar=k.p("ret_norm", hd),
                                              in1=e.ret_g[:, hd, :], op0=ALU.mult, op1=ALU.mult))


def rwkv(k, m):
    nc, g = k.nc, k.g
    s = Names(**{n: k.sem("rw_" + n) for n in (
        "loaded", "gram_done", "gram_kept", "padded", "turned", "v_kept", "rows_kept", "w1_done", "w1_kept", "off_ready",
        "u_done", "u_kept", "dx_done", "x_ready", "xa_done", "xa_kept", "q_done", "q_kept", "m_kept", "state_done",
        "state_ready", "y_done", "y_kept", "dve_chain", "act_chain", "pool_chain", "mean_done", "centred", "squared",
        "var_done", "inverted", "rooted")})
    HD = 8
    with ExitStack() as own:
        sb = lambda n, shape: k.sb("rw_" + n, shape, own)
        consts = sb("consts", [P, RW_N])
        gram = sb("gram", [P, HD, 4, P])
        ar = sb("ar", [P, HD, 2, P])
        vp = sb("vp", [P, HD, P])
        aw = sb("aw", [P, HD, 2, 64])
        bk = sb("bk", [P, 2, 2, CH])
        x, xt = sb("x", [P, HD, P]), sb("xt", [P, HD, P])
        u, off = sb("u", [P, HD, P]), sb("off", [P, HD, P])
        xa, xw, mt = u, off, x
        q = sb("q", [P, 4, P])
        grown = sb("grown", [P, 4, P])
        state = sb("state", [P, 3, 4, P])
        wc = lambda n: consts[:, RW_AT[n][0]:RW_AT[n][1]]
        block = own.enter_context(nc.Block())
        L = len(LEVELS)
        pair_cols = lambda t, p: t[:, 2 * p:2 * p + 2, :].rearrange("p h c -> p (h c)")[:, 0:T].rearrange(
            "p (a c) -> p a c", c=64)[:, 0::3, :]

        @block.sync
        def _(sp):
            sp.dma_start(consts[:, :], g.rw_consts).then_inc(s.loaded, 16)
            k.load_chunks(sp, O_OUT + SLOTS)

        @block.gpsimd
        def _(pool):
            pool.memset(ar[:, :, :, :], 0.0).then_inc(s.padded, 1)
            pool.memset(state[:, 0, :, :], 0.0).then_inc(s.state_ready, 1)
            pool.wait_ge(s.loaded, 16)
            pool.wait_ge(s.padded, 1)
            pool.wait_ge(s.state_ready, 1)
            for a in range(TH):
                half = slice(a * P, (a + 1) * P)
                if a:
                    pool.wait_ge(s.gram_done, HD)
                for hd in range(2):
                    rows = slice(64 * hd, 64 * hd + 64)
                    for i, src in enumerate((m.kk, m.r)):
                        pool.tensor_copy(ar[rows, hd::2, i, :], src[rows, :, half]).then_inc(s.padded, 1)
                        pool.wait_ge(s.padded, 2 + 4 * a + 2 * hd + i)
                for lv in range(L):
                    for grp in range(2):
                        hs = slice(4 * grp, 4 * grp + 4)
                        if lv == 0:
                            pool.wait_ge(s.gram_kept, HD * a + 4 * grp + 4)
                            if a:
                                pool.wait_ge(s.y_done, 1)
                        else:
                            pool.wait_ge(s.u_done, 2 * (L * a + lv - 1) + grp + 1)
                            if lv == 1:
                                pool.wait_ge(s.x_ready, 2 * L * a + grp + 1)
                        pool.tensor_tensor(off[:, hs, :], gram[:, hs, 0, :], bc(wc("levels")[:, lv * P:(lv + 1) * P], 1, 4),
                                           ALU.mult).then_inc(s.off_ready, 1)
                pool.wait_ge(s.off_ready, 2 * L * (a + 1))

        @block.tensor
        def _(pe):
            for a in range(TH):
                half = slice(a * P, (a + 1) * P)
                pe.wait_ge(s.padded, 5 + 4 * a)
                if a:
                    pe.wait_ge(s.y_kept, 1)
                    pe.wait_ge(s.state_ready, 3)
                for h in range(HD):
                    pe.matmul(k.bank(h)[:, 0:T], m.a[:, h // 2, half], ar[:, h, :, :], start=True, stop=True)
                    pe.matmul(k.bank(h)[:, T:2 * T], m.kh[:, h // 2, half], ar[:, h, :, :], start=True, stop=True).then_inc(s.gram_done, 1)
                pe.wait_ge(s.gram_kept, HD * (a + 1))
                for i, src in enumerate((m.v, m.kk, m.a, m.kh)):
                    for p in range(4):
                        ins = pe.transpose(k.bank(i)[:, p * P:(p + 1) * P], src[:, p, half], k.c("ident"))
                    ins.then_inc(s.turned, 1)
                pe.wait_ge(s.v_kept, a + 1)
                for h in range(HD):
                    ins = pe.matmul(k.bank(4)[:, h * 64:(h + 1) * 64], gram[:, h, 2, :], vp[:, h, (h % 2) * 64:(h % 2) * 64 + 64],
                                    start=True, stop=True)
                ins.then_inc(s.w1_done, 1)
                for lv in range(L):
                    for grp in range(2):
                        pe.wait_ge(s.off_ready, 2 * (L * a + lv) + grp + 1)
                        if lv or a:
                            pe.wait_ge(s.x_ready, 2 * (L * a + lv - 1) + grp + 1)
                        if a == 1 and lv == 0:
                            pe.wait_ge(s.y_done, 1)
                        for h in range(4 * grp, 4 * grp + 4):
                            ins = pe.matmul(k.bank(6 + grp)[:, (h % 4) * P:(h % 4 + 1) * P], off[:, h, :],
                                            x[:, h, :] if lv else k.c("ident"), start=True, stop=True)
                        ins.then_inc(s.u_done, 1)
                    if lv == 0:
                        continue
                    for grp in range(2):
                        pe.wait_ge(s.u_kept, 2 * ((L - 1) * a + lv - 1) + grp + 1)
                        if lv == 1:
                            pe.wait_ge(s.rows_kept, a + 1)
                        for h in range(4 * grp, 4 * grp + 4):
                            cols = slice((h % 4) * P, (h % 4 + 1) * P)
                            if lv < L - 1:
                                pe.matmul(k.bank(2 * grp)[:, cols], xt[:, h, :], u[:, h, :], start=True, stop=True)
                            ins = pe.matmul(k.bank(2 * grp + 1)[:, cols], u[:, h, :], xt[:, h, :], start=True, stop=True)
                        ins.then_inc(s.dx_done, 1)
                pe.wait_ge(s.w1_kept, a + 1)
                pe.wait_ge(s.x_ready, 2 * L * (a + 1))
                for h in range(HD):
                    ins = pe.matmul(k.bank(4 + h // 4)[:, (h % 4) * P:(h % 4 + 1) * P], xt[:, h, :], aw[:, h, :, :], start=True, stop=True)
                ins.then_inc(s.xa_done, 1)
                pe.wait_ge(s.xa_kept, a + 1)
                for p in range(4):
                    for h in (2 * p, 2 * p + 1):
                        ins = pe.matmul(k.bank(6)[:, p * P:(p + 1) * P], xa[:, h, :], gram[:, h, 1, :], start=h % 2 == 0, stop=h % 2 == 1)
                for p in range(4):
                    for c in range(2):
                        for h in (2 * p, 2 * p + 1):
                            ins = pe.matmul(k.bank(c)[:, p * P:(p + 1) * P], xa[:, h, :], bk[:, 0, c, p * P:(p + 1) * P],
                                            start=h % 2 == 0, stop=h % 2 == 1)
                ins.then_inc(s.q_done, 1)
                pe.wait_ge(s.m_kept, a + 1)
                for n in range(2 * a, min(2 * a + 2, RN - 1)):
                    c = n - 2 * a
                    pe.wait_ge(s.state_ready, n + 1)
                    for p in range(4):
                        out = k.bank(2 + c)[:, p * P:(p + 1) * P]
                        cols = slice(p * P, (p + 1) * P)
                        pe.matmul(out, bk[:, 0, c, cols], pair_cols(xw, p), start=True, stop=False)
                        pe.matmul(out, bk[:, 1, c, cols], pair_cols(vp, p), start=False, stop=False)
                        ins = pe.matmul(out, mt[:, 4 * c + p, :], state[:, n % 3, p, :], start=False, stop=True)
                    ins.then_inc(s.state_done, 1)
                pe.wait_ge(s.q_kept, a + 1)
                pe.wait_ge(s.state_ready, 2 * a + 2)
                for p in range(4):
                    out = k.bank(7)[:, p * P:(p + 1) * P]
                    for h in (2 * p, 2 * p + 1):
                        pe.matmul(out, xw[:, h, :], gram[:, h, 1, :], start=h % 2 == 0, stop=False, skip_group_check=True)
                        pe.matmul(out, vp[:, h, :], gram[:, h, 3, :], start=False, stop=False, skip_group_check=True)
                    for c in range(2):
                        ins = pe.matmul(out[:, c * 64:(c + 1) * 64], state[:, (2 * a + c) % 3, p, :], q[:, p, c * 64:(c + 1) * 64],
                                        start=False, stop=True, skip_group_check=True)
                ins.then_inc(s.y_done, 1)
            pe.wait_ge(s.y_kept, 2)
            for i in range(2):
                ins = pe.matmul(k.bank(i), k.c("head_mean"), k.h[:, 4 + 2 * i:6 + 2 * i, :], start=True, stop=True)
            ins.then_inc(s.mean_done, 1)
            pe.wait_ge(s.squared, 1)
            for i in range(2):
                ins = pe.matmul(k.bank(2 + i), k.c("head_mean"), gram[:, i, :, :], start=True, stop=True)
            ins.then_inc(s.var_done, 1)

        @block.scalar
        def _(act):
            astep = counted(act, s.act_chain)
            for a in range(TH):
                act.wait_ge(s.turned, 4 * a + 4)
                astep(act.copy(aw[:, :, 0, :], k.bank(1).rearrange("p (h c) -> p h c", c=64)))
                for i in range(2):
                    for c in range(2):
                        ins = act.activation(bk[:, i, c, :], k.bank(2 + i), ACT.Copy, scale=k.c("parity")[:, c:c + 1])
                        if (i, c) != (1, 1):
                            astep(ins)
                ins.then_inc(s.rows_kept, 1)
                act.wait_ge(s.w1_done, a + 1)
                act.copy(aw[:, :, 1, :], k.bank(4).rearrange("p (h c) -> p h c", c=64)).then_inc(s.w1_kept, 1)
                for lv in range(1, L):
                    for grp in range(2):
                        act.wait_ge(s.u_done, 2 * (L * a + lv) + grp + 1)
                        act.copy(u[:, 4 * grp:4 * grp + 4, :], k.bank(6 + grp).rearrange("p (h c) -> p h c", c=P)).then_inc(s.u_kept, 1)
                act.wait_ge(s.y_done, a + 1)
                act.copy(k.h[:, 4:8, a * P:(a + 1) * P], k.bank(7).rearrange("p (h c) -> p h c", c=P)).then_inc(s.y_kept, 1)
            act.wait_ge(s.centred, 1)
            act.activation(gram[:, :, :, :].rearrange("p a b c -> p (a b c)")[:, 0:4 * T], k.h[:, 4:8, :].rearrange("p a t -> p (a t)"), ACT.Square).then_inc(s.squared, 1)
            act.wait_ge(s.inverted, 1)
            act.activation(gram[:, 0:2, :, :], gram[:, 0:2, :, :], ACT.Sqrt).then_inc(s.rooted, 1)

        @block.vector
        def _(dve):
            step = counted(dve, s.dve_chain)
            dve.wait_ge(s.loaded, 16)
            masks = consts[:, RW_AT["strict"][0]:RW_AT["upto"][1]].rearrange("p (b c) -> p b c", b=2)
            cols = wc("head_cols").rearrange("p (h c) -> p h c", h=2)
            for a in range(TH):
                for h in range(HD):
                    dve.wait_ge(s.gram_done, HD * a + h + 1)
                    dve.tensor_tensor(gram[:, h, :, :].rearrange("p (x y) c -> p x y c", x=2),
                                      k.bank(h).rearrange("p (x y c) -> p x y c", x=2, y=2), bc(masks, 1, 2), ALU.mult).then_inc(s.gram_kept, 1)
                dve.wait_ge(s.turned, 4 * a + 1)
                dve.tensor_tensor(vp[:, :, :].rearrange("p (q h) c -> p q h c", h=2),
                                  bc(k.bank(0).rearrange("p (q c) -> p q c", c=P), 2, 2), bc(cols, 1, 4), ALU.mult).then_inc(s.v_kept, 1)
                for lv in range(L):
                    for grp in range(2):
                        hs = slice(4 * grp, 4 * grp + 4)
                        n = 2 * (L * a + lv) + grp + 1
                        if lv == 0:
                            ident = bc(k.c("ident"), 1, 4)
                            dve.wait_ge(s.off_ready, n)
                            step(dve.tensor_tensor(xt[:, hs, :], off[:, hs, :], ident, ALU.add))
                            dve.wait_ge(s.u_done, n)
                            dve.tensor_tensor(x[:, hs, :], k.bank(6 + grp).rearrange("p (h c) -> p h c", c=P), ident, ALU.add).then_inc(s.x_ready, 1)
                            continue
                        dve.wait_ge(s.dx_done, 2 * ((L - 1) * a + lv - 1) + grp + 1)
                        if lv < L - 1:
                            step(dve.tensor_tensor(x[:, hs, :], x[:, hs, :], k.bank(2 * grp).rearrange("p (h c) -> p h c", c=P), ALU.add))
                        dve.tensor_tensor(xt[:, hs, :], xt[:, hs, :], k.bank(2 * grp + 1).rearrange("p (h c) -> p h c", c=P), ALU.add).then_inc(s.x_ready, 1)
                dve.wait_ge(s.xa_done, a + 1)
                for hd in range(2):
                    for i, dst in enumerate((xa, xw)):
                        src = k.bank(4, 2).rearrange("p (q h i c) -> p q h i c", q=4, h=2, i=2)[:, :, hd, i, :]
                        ins = dve.tensor_tensor(dst[:, hd::2, :].rearrange("p q (r c) -> p q r c", r=2), bc(src, 2, 2),
                                                bc(cols[:, hd, :].rearrange("p (r c) -> p r c", r=2), 1, 4), ALU.mult)
                        if (hd, i) != (1, 1):
                            step(ins)
                ins.then_inc(s.xa_kept, 1)
                dve.wait_ge(s.q_done, a + 1)
                dve.tensor_tensor(mt[:, :, :].rearrange("p n c -> p (n c)").rearrange("p (n c) -> p n c", c=P),
                                  k.bank(0, 2).rearrange("p (n c) -> p n c", c=P), bc(k.c("head_ones"), 1, 8), ALU.mult).then_inc(s.m_kept, 1)
                dve.tensor_tensor(q[:, :, :], k.bank(6).rearrange("p (n c) -> p n c", c=P), m.r[:, :, a * P:(a + 1) * P], ALU.add).then_inc(s.q_kept, 1)
                for n in range(2 * a, min(2 * a + 2, RN - 1)):
                    c = n - 2 * a
                    dve.wait_ge(s.state_done, n + 1)
                    if n == 2:
                        dve.wait_ge(s.y_done, 1)
                    step(dve.tensor_tensor(grown[:, :, :], k.bank(2 + c).rearrange("p (n c) -> p n c", c=P), state[:, n % 3, :, :], ALU.add))
                    step(dve.tensor_tensor(grown[:, :, :], grown[:, :, :], m.chunk_decay[:, :, n:n + 1].broadcast_to([P, 4, P]), ALU.mult))
                    dve.tensor_tensor(state[:, (n + 1) % 3, :, :], grown[:, :, :], bc(k.c("head_ones"), 1, 4), ALU.mult).then_inc(s.state_ready, 1)
            y = k.h[:, 4:8, :]
            flat = lambda t: t.rearrange("p m t -> p (m t)")
            tmp = gram[:, 0:2, :, :].rearrange("p a b c -> p (a b c)").rearrange("p (m t) -> p m t", m=4)
            dve.wait_ge(s.mean_done, 1)
            dve.tensor_tensor(flat(y), flat(y), k.bank(0, 2), ALU.subtract).then_inc(s.centred, 1)
            dve.wait_ge(s.centred, 1)
            dve.wait_ge(s.var_done, 1)
            step(dve.tensor_scalar(flat(tmp), k.bank(2, 2), RW_LN_EPS, None, ALU.add))
            dve.reciprocal(flat(tmp), flat(tmp)).then_inc(s.inverted, 1)
            dve.wait_ge(s.rooted, 1)
            step(dve.tensor_tensor(y, y, tmp, ALU.mult))
            for t in range(4):
                step(dve.tensor_scalar(y[:, t, :], y[:, t, :], k.p("ln_g", t), k.p("ln_b", t), ALU.mult, ALU.add))
            step(dve.tensor_tensor(y, y, m.bonus[:, :, :], ALU.add))
            step(dve.tensor_tensor(y, y, m.g[:, :, :], ALU.mult))


def route(k, x):
    nc, g = k.nc, k.g
    s = Names(**{n: k.sem("ro_" + n) for n in (
        "loaded", "logits_done", "rows_done", "rows_kept", "chosen", "places_done", "shifted", "exp_ready", "dve_chain")})
    with ExitStack() as own:
        sb = lambda n, shape: k.sb("ro_" + n, shape, own)
        router = sb("router", [P, KT, E])
        lg, ez, w = sb("logits", [P, TH, E]), sb("exp", [P, TH, E]), sb("weights", [P, TH, E])
        above, same = sb("above", [P, E, E]), sb("same", [P, E, E])
        rank, top, total = sb("rank", [P, TH, E]), sb("top", [P, TH]), sb("total", [P, TH])
        most = sb("most", [P, 1])
        block = own.enter_context(nc.Block())

        @block.sync
        def _(sp):
            sp.dma_start(router[:, :, :], g.o_moe_router[0].rearrange("(k p) e -> p k e", p=P)).then_inc(s.loaded, 16)

        @block.tensor
        def _(pe):
            pe.wait_ge(s.loaded, 16)
            for a in range(TH):
                for kt in range(KT):
                    ins = pe.matmul(k.bank(4)[:, a * E:(a + 1) * E], k.h[:, kt, a * P:(a + 1) * P], router[:, kt, :],
                                    start=kt == 0, stop=kt == KT - 1)
            ins.then_inc(s.logits_done, 1)
            for a in range(TH):
                for kt in range(KT):
                    ins = pe.transpose(k.bank(2 * a + kt // 4)[:, (kt % 4) * P:(kt % 4 + 1) * P], k.h[:, kt, a * P:(a + 1) * P], k.c("ident"))
                ins.then_inc(s.rows_done, 1)
            pe.wait_ge(s.chosen, 1)
            pe.matmul(k.bank(5)[:, 0:E], k.c("before"), x.chosen[:, 0, :], start=True, stop=True)
            pe.matmul(k.bank(5)[:, E:2 * E], k.c("ones"), x.chosen[:, 0, :], start=True, stop=False)
            pe.matmul(k.bank(5)[:, E:2 * E], k.c("before"), x.chosen[:, 1, :], start=False, stop=True)
            for a in range(TH):
                ins = pe.matmul(k.bank(5)[:, 2 * E:3 * E], k.c("ones"), x.chosen[:, a, :], start=a == 0, stop=a == 1)
            ins.then_inc(s.places_done, 1)

        @block.scalar
        def _(act):
            for a in range(TH):
                act.wait_ge(s.rows_done, a + 1)
                act.copy(x.rows[:, a, :], k.bank(2 * a, 2)).then_inc(s.rows_kept, 1)
            act.wait_ge(s.shifted, 1)
            act.activation(ez[:, :, :], ez[:, :, :], ACT.Exp).then_inc(s.exp_ready, 1)

        @block.vector
        def _(dve):
            step = counted(dve, s.dve_chain)
            dve.wait_ge(s.logits_done, 1)
            step(dve.tensor_copy(lg[:, :, :], k.bank(4)[:, 0:TH * E].rearrange("p (a e) -> p a e", a=TH)))
            step(dve.tensor_reduce(top[:, :], lg[:, :, :], AX.X, ALU.max))
            dve.tensor_tensor(ez[:, :, :], lg[:, :, :], bc(top[:, :], 2, E), ALU.subtract).then_inc(s.shifted, 1)
            for a in range(TH):
                mine, other = bc(lg[:, a, :], 2, E), bc(lg[:, a, :], 1, E)
                step(dve.tensor_tensor(above[:, :, :], other, mine, ALU.is_gt))
                step(dve.tensor_tensor(same[:, :, :], other, mine, ALU.is_equal))
                step(dve.tensor_tensor(same[:, :, :], same[:, :, :], k.c("earlier").rearrange("p (e f) -> p e f", e=E), ALU.mult))
                step(dve.tensor_tensor(above[:, :, :], above[:, :, :], same[:, :, :], ALU.add))
                step(dve.tensor_reduce(rank[:, a, :], above[:, :, :], AX.X, ALU.add))
            dve.tensor_scalar(x.chosen[:, :, :], rank[:, :, :], float(TOP_K), None, ALU.is_lt).then_inc(s.chosen, 1)
            dve.wait_ge(s.chosen, 1)
            dve.wait_ge(s.exp_ready, 1)
            step(dve.tensor_tensor(w[:, :, :], ez[:, :, :], x.chosen[:, :, :], ALU.mult))
            step(dve.tensor_reduce(total[:, :], w[:, :, :], AX.X, ALU.add))
            step(dve.reciprocal(total[:, :], total[:, :]))
            step(dve.tensor_tensor(x.gate[:, :, :], w[:, :, :], bc(total[:, :], 2, E), ALU.mult))
            dve.wait_ge(s.places_done, 1)
            step(dve.tensor_copy(x.place[:, :, :], k.bank(5)[:, 0:2 * E].rearrange("p (a e) -> p a e", a=TH)))
            step(dve.tensor_reduce(most[:, :], k.bank(5)[:, 2 * E:3 * E], AX.X, ALU.max))
            step(dve.tensor_copy(x.most[:, :], most[:, :]))
            dve.wait_ge(s.rows_kept, TH)


TOP_K = 2
XCH = len(FFN_ORDER)
FREE = 1


def expert_chunk(k, e, i):
    g = k.g
    kind, c = FFN_ORDER[i]
    w = {"gate": g.o_moe_w_gate, "up": g.o_moe_w_up, "down": g.o_moe_w_down}[kind][0]
    if kind == "down":
        return w[bass.ds(e, 1), c * CH:(c + 1) * CH, :].rearrange("o (k p) c -> p (o k) c", p=P)
    return w[bass.ds(e, 1), :, c * CH:(c + 1) * CH].rearrange("o (k p) c -> p (o k) c", p=P)


def expert_slot(k, i):
    j = i % X_SLOTS
    w = k.ring[:, j, :] if j < SLOTS else k.ring_more[:, j - SLOTS, :]
    return w.rearrange("p (k c) -> p k c", k=MF if FFN_ORDER[i][0] == "down" else KT)


def expert_filled(i, e, p):
    dense = 16 * (DENSE // SLOTS) if i % X_SLOTS < SLOTS else 0
    return dense + 16 * (XCH // X_SLOTS) * (E * p) + 16 * (i // X_SLOTS + 1) + 16 * (XCH // X_SLOTS) * e


def load_expert_chunk(k, sp, e, i, p, ahead):
    if ahead:
        sp.wait_ge(k.chunk_used, DENSE + XCH * E * p + i - ahead + 1 + XCH * e)
    sp.dma_start(expert_slot(k, i), expert_chunk(k, e, i)).then_inc((k.slot_filled + k.more_filled)[i % X_SLOTS], 16)


def load_first_expert_chunks(k, sp, p):
    for i in range(X_SLOTS):
        load_expert_chunk(k, sp, 0, i, p, X_SLOTS if p else SLOTS if i < SLOTS else 0)


def expert_pass(k, x, s, p):
    nc = k.nc

    def guarded(engine, program, frees=()):
        if p == 0:
            for sem in frees:
                engine.sem_inc(sem, FREE)
            return program()
        most = engine.value_load(x.most[0:1, 0:1], min_val=0, max_val=T)
        with engine.If(most > CAP * p):
            program()

    with ExitStack() as own:
        block = own.enter_context(nc.Block())
        first = DENSE + XCH * E * p
        at = FFN_ORDER.index

        @block.sync
        def _(sp):
            def program():
                if p:
                    load_first_expert_chunks(k, sp, p)
                with sp.Fori(0, E - 1) as e:
                    for i in range(X_SLOTS, XCH):
                        load_expert_chunk(k, sp, e, i, p, X_SLOTS)
                    for i in range(X_SLOTS):
                        sp.wait_ge(k.chunk_used, first + XCH + i - X_SLOTS + 1 + XCH * e)
                        sp.dma_start(expert_slot(k, i), expert_chunk(k, e + 1, i)).then_inc((k.slot_filled + k.more_filled)[i], 16)
                for i in range(X_SLOTS, XCH):
                    load_expert_chunk(k, sp, E - 1, i, p, X_SLOTS)
            guarded(sp, program)

        @block.vector
        def _(dve):
            def program():
                dve.tensor_scalar(x.here[:, :, :], x.place[:, :, :], -float(CAP * p), None, ALU.add).then_inc(s.hot, 1)
                dve.wait_ge(s.hot, 18 * p + 1)
                for a in range(TH):
                    for e in range(E):
                        dve.tensor_scalar(x.hot[:, a, e, :], k.c("slots"), x.here[:, a, e:e + 1], x.chosen[:, a, e:e + 1],
                                          ALU.is_equal, ALU.mult).then_inc(s.hot, 1)
                dve.wait_ge(s.hot, 18 * p + 17)
                dve.tensor_tensor(x.weighted[:, :, :, :].rearrange("p a e c -> p (a e) c"), x.hot[:, :, :, :].rearrange("p a e c -> p (a e) c"),
                                  bc(x.gate[:, :, :].rearrange("p a e -> p (a e)"), 2, CAP), ALU.mult).then_inc(s.hot, 1)
                for b in range(4):
                    dve.wait_ge(s.scatter_turned, 4 * p + b + 1)
                    dve.tensor_copy(x.scatter[:, 2 * b:2 * b + 2, :], k.bank(b)[0:CAP, :].rearrange("p (e t) -> p e t", e=2)).then_inc(s.scatter_kept, 1)
                with dve.Fori(0, E) as e:
                    for c in range(FC):
                        dve.wait_ge(k.chunk_used, first + at(("up", c)) + 1 + XCH * e)
                        dve.wait_ge(s.gate_kept, FREE + FC * E * p + c + 1 + FC * e)
                        if c == 0:
                            dve.wait_ge(k.chunk_used, first + XCH * e)
                        if c >= 2:
                            dve.wait_ge(k.chunk_used, first + at(("down", c - 2)) + 1 + XCH * e)
                        dve.tensor_tensor(x.hid[:, c % 2, :], x.gated[:, c % 2, :], k.bank(1)[:, 0:MF * CAP], ALU.mult).then_inc(s.act_ready, 1)
                    dve.wait_ge(s.out_done, FREE + E * p + 1 + e)
                    dve.wait_ge(s.added, FREE + 2 * E * p + 2 * e)
                    for i in range(2):
                        r = k.res[:, 4 * i:4 * i + 4, :].rearrange("p m t -> p (m t)")
                        dve.tensor_tensor(r, r, k.bank(4 + 2 * i, 2), ALU.add).then_inc(s.added, 1)
                dve.wait_ge(s.added, FREE + 2 * E * (p + 1))
            guarded(dve, program, (s.act_ready, s.added))

        @block.gpsimd
        def _(pool):
            def program():
                pool.wait_ge(s.gather_kept, 16 * (p + 1))
                pool.wait_ge(s.scatter_kept, 4 * (p + 1))
                with pool.Fori(0, E) as e:
                    pool.wait_ge(k.chunk_used, first - 1 + XCH * e)
                    pool.tensor_copy(x.tokens[:, :], x.gathered[:, bass.ds(e, 1), :].rearrange("p o c -> p (o c)")).then_inc(s.tokens_ready, 1)
                    pool.wait_ge(s.out_done, FREE + E * p + e)
                    pool.wait_ge(s.tokens_ready, E * p + 1 + e)
                    pool.tensor_copy(x.places[:, :], x.scatter[:, bass.ds(e, 1), :].rearrange("p o c -> p (o c)")).then_inc(s.places_ready, 1)
                    pool.wait_ge(s.places_ready, E * p + 1 + e)
            guarded(pool, program)

        @block.scalar
        def _(act):
            def program():
                for j in range(16):
                    act.wait_ge(s.gather_done, 16 * p + j + 1)
                    act.copy(x.gathered[:, :, :].rearrange("p e (k c) -> p e k c", k=KT)[:, 4 * (j % 2):4 * (j % 2) + 4, j // 2, :],
                             k.bank(j % 8)[:, 0:4 * CAP].rearrange("p (e c) -> p e c", e=4)).then_inc(s.gather_kept, 1)
                with act.Fori(0, E) as e:
                    for c in range(FC):
                        act.wait_ge(k.chunk_used, first + at(("gate", c)) + 1 + XCH * e)
                        if c != 1:
                            act.wait_ge(s.act_ready, FREE + FC * E * p + max(c - 1, 0) + FC * e)
                        act.activation(x.gated[:, c % 2, :], k.bank(0)[:, 0:MF * CAP], ACT.Silu).then_inc(s.gate_kept, 1)
                    act.wait_ge(k.chunk_used, first + XCH + XCH * e)
                    act.wait_ge(s.out_done, FREE + E * p + e)
                    act.copy(x.y[:, :], k.bank(2, 2)[0:CAP, :]).then_inc(s.y_kept, 1)
            guarded(act, program, (s.gate_kept, s.y_kept))

        @block.tensor
        def _(pe):
            def program():
                pe.wait_ge(s.hot, 18 * p + 17)
                for j in range(16):
                    if j >= 8:
                        pe.wait_ge(s.gather_kept, 16 * p + j - 7)
                    for a in range(TH):
                        ins = pe.matmul(k.bank(j % 8)[:, 0:4 * CAP], x.rows[:, a, (j // 2) * P:(j // 2 + 1) * P],
                                        x.hot[:, a, 4 * (j % 2):4 * (j % 2) + 4, :], start=a == 0, stop=a == 1)
                    ins.then_inc(s.gather_done, 1)
                pe.wait_ge(s.hot, 18 * p + 18)
                for b in range(4):
                    pe.wait_ge(s.gather_kept, 16 * p + 9 + b)
                    for i in range(4):
                        ins = pe.transpose(k.bank(b)[0:CAP, i * P:(i + 1) * P], x.weighted[:, i % 2, 2 * b + i // 2, :], k.c("ident"))
                    ins.then_inc(s.scatter_turned, 1)
                pe.wait_ge(s.scatter_kept, 4 * (p + 1))
                pe.wait_ge(s.gather_kept, 16 * (p + 1))
                with pe.Fori(0, E) as e:
                    pe.wait_ge(s.tokens_ready, E * p + 1 + e)
                    for i, (kind, c) in enumerate(FFN_ORDER):
                        pe.wait_ge((k.slot_filled + k.more_filled)[i % X_SLOTS], expert_filled(i, e, p))
                        w = expert_slot(k, i)
                        if kind == "down":
                            pe.wait_ge(s.act_ready, FREE + FC * E * p + c + 1 + FC * e)
                            if c == 0:
                                pe.wait_ge(s.y_kept, FREE + E * p + e)
                            for f in range(MF):
                                for n in range(2):
                                    ins = pe.matmul(k.bank(2 + n)[0:CAP, :], x.hid[:, c % 2, f * CAP:(f + 1) * CAP],
                                                    w[:, f, n * CH:(n + 1) * CH], start=c == 0 and f == 0, stop=c == FC - 1 and f == MF - 1)
                        else:
                            pe.wait_ge(s.gate_kept if kind == "gate" else s.act_ready, FREE + FC * E * p + c + FC * e)
                            for m in range(MF):
                                for kt in range(KT):
                                    ins = pe.matmul(k.bank(0 if kind == "gate" else 1)[:, m * CAP:(m + 1) * CAP],
                                                    w[:, kt, m * P:(m + 1) * P], x.tokens[:, kt * CAP:(kt + 1) * CAP],
                                                    start=kt == 0, stop=kt == KT - 1)
                        ins.then_inc(k.chunk_used, 1)
                    pe.wait_ge(s.y_kept, FREE + E * p + 1 + e)
                    pe.wait_ge(s.places_ready, E * p + 1 + e)
                    pe.wait_ge(s.added, FREE + 2 * E * p + 2 * e)
                    for m in range(KT):
                        ins = pe.matmul(k.bank(4 + m // 2)[:, (m % 2) * T:(m % 2 + 1) * T], x.y[:, m * P:(m + 1) * P], x.places[:, :],
                                        start=True, stop=True)
                    ins.then_inc(s.out_done, 1)
            guarded(pe, program, (s.out_done,))


def experts(k):
    with ExitStack() as own:
        k.ring_more = k.sb("ring_more", [P, X_SLOTS - SLOTS, 8 * CH], own)
        out_project(k, "odd_out", O_OUT, DENSE, after=lambda sp: load_first_expert_chunks(k, sp, 0))
        rms_norm(k, "norm4", "norm2_o", DENSE)
        sb = lambda n, shape, dt=F32: k.sb("expert_" + n, shape, own, dt)
        routed = dict(
            rows=sb("rows", [P, TH, D]),
            chosen=sb("chosen", [P, TH, E]), gate=sb("gate", [P, TH, E]), place=sb("place", [P, TH, E]),
            here=sb("here", [P, TH, E]), most=sb("most", [P, 1], I32))
        route(k, Names(**routed))
        x = Names(
            **routed,
            hot=sb("hot", [P, TH, E, CAP]),
            weighted=sb("weighted", [P, TH, E, CAP]), scatter=sb("scatter", [CAP, E, T]),
            gathered=sb("gathered", [P, E, KT * CAP]), tokens=sb("tokens", [P, KT * CAP]), places=sb("places", [CAP, T]),
            gated=sb("gated", [P, 2, MF * CAP]), hid=sb("hid", [P, 2, MF * CAP]), y=sb("y", [CAP, D]))
        s = Names(**{n: k.sem("expert_" + n) for n in (
            "hot", "gather_done", "gather_kept", "scatter_turned", "scatter_kept", "tokens_ready", "places_ready",
            "gate_kept", "act_ready", "y_kept", "out_done", "added")})
        for p in range(PASSES):
            expert_pass(k, x, s, p)


def emit(k):
    turned, kept, stored = k.sem("out_turned"), k.sem("out_kept"), k.sem("out_stored")
    with ExitStack() as own:
        y = k.sb("out_rows", [P, TH, D], own)
        block = own.enter_context(k.nc.Block())

        @block.tensor
        def _(pe):
            for a in range(TH):
                for kt in range(KT):
                    ins = pe.transpose(k.bank(2 * a + kt // 4)[:, (kt % 4) * P:(kt % 4 + 1) * P], k.h[:, kt, a * P:(a + 1) * P], k.c("ident"))
                ins.then_inc(turned, 1)

        @block.vector
        def _(dve):
            for a in range(TH):
                dve.wait_ge(turned, a + 1)
                dve.tensor_copy(y[:, a, :], k.bank(2 * a, 2)).then_inc(kept, 1)

        @block.sync
        def _(sp):
            for a in range(TH):
                sp.wait_ge(kept, a + 1)
                sp.dma_start(k.g.out[0, a * P:(a + 1) * P, :], y[:, a, :]).then_inc(stored, 16)
            sp.wait_ge(stored, 16 * TH)


def build(nc, g):
    with ExitStack() as ctx:
        k = Program(nc, g, ctx)
        embed(k)
        rms_norm(k, "norm1", "norm1_e", SLOTS)
        even_mixer(k)
        out_project(k, "even_out", E_OUT, FFN + SLOTS)
        rms_norm(k, "norm2", "norm2_e", FFN + SLOTS)
        dense_ffn(k)
        k.recycle()
        rms_norm(k, "norm3", "norm1_o", O_IN + SLOTS)
        odd_mixer(k)
        k.recycle()
        experts(k)
        rms_norm(k, "norm5", "final", DENSE)
        emit(k)


INPUTS = ["x", "e_w_in", "e_gla_gate_up", "e_w_out", "e_ffn_w_gate", "e_ffn_w_up", "e_ffn_w_down", "o_w_in",
          "o_rw_w_up", "o_rw_a_up", "o_rw_g_up", "o_w_out", "o_moe_router", "o_moe_w_gate", "o_moe_w_up",
          "o_moe_w_down"]


def packed_params(i):
    cols = lambda a: np.asarray(a).reshape(-1, P).T
    gate_b = np.zeros((P, 2), np.float32)
    gate_b[0:4, :] = np.asarray(i["e_ml_gate_b"]).reshape(2, 4).T
    v = {
        "norm1_e": i["e_norm1_g"], "conv_w": i["e_ml_conv_w"], "conv_b": i["e_ml_conv_b"], "ml_norm": i["e_ml_norm_g"],
        "gla_b": i["e_gla_gate_b"], "gla_norm": i["e_gla_norm_g"], "norm2_e": i["e_norm2_g"], "norm1_o": i["o_norm1_g"],
        "ret_norm": i["o_ret_norm_g"], "mu": i["o_rw_mu"], "w0": i["o_rw_w0"], "a0": i["o_rw_a0"], "k_k": i["o_rw_k_k"],
        "k_a": i["o_rw_k_a"], "r_k": i["o_rw_r_k"], "ln_g": i["o_rw_ln_g"], "ln_b": i["o_rw_ln_b"],
        "norm2_o": i["o_norm2_g"], "final": i["final_norm_g"],
    }
    return np.concatenate([gate_b if n == "gate_b" else cols(v[n]) for n, _ in PARAM_COLS], axis=1)


def kernel(**inputs):
    import concourse.bacc as bacc
    from concourse.bass_utils import run_bass_kernel_spmd as run
    nc = bacc.Bacc("TRN2", target_bir_lowering=False, num_devices=1)
    arrays = {n: np.ascontiguousarray(inputs[n]) for n in INPUTS}
    arrays["params"] = np.ascontiguousarray(packed_params(inputs))
    arrays["consts"], arrays["ret_consts"], arrays["rw_consts"] = constants()
    sent = {f"in_{n}_dram": a for n, a in arrays.items()}
    g = Names(**{n: nc.dram_tensor(f"in_{n}_dram", a.shape, mybir.dt.from_np(a.dtype), kind="ExternalInput").ap()
                 for n, a in arrays.items()}, out=nc.dram_tensor("out_0_dram", (1, T, D), F32, kind="ExternalOutput").ap())
    build(nc, g)
    r = run(nc, [sent], core_ids=[0])
    return r.results[0]["out_0_dram"]
```

```python
from collections import namedtuple
from contextlib import ExitStack

import numpy as np
import concourse.bass as bass
from concourse import mybir

F32 = mybir.dt.float32
F32R = mybir.dt.float32r
I32 = mybir.dt.int32
ALU = mybir.AluOpType
ACT = mybir.ActivationFunctionType
AX = mybir.AxisListType

P = 128
T = 256
TH = T // P
D = 1024
KT = D // P
D_FF = 3584
FT = D_FF // P
E = 8
CAP = 128
PASSES = -(-T // CAP)
EPS = 1e-6
RW_LN_EPS = 64e-5
BIG = 1e30
GC = 16
GN = T // GC
RC = 64
RN = T // RC
CH = 512
SLOTS = 3
MF = CH // P
FC = D_FF // CH
LEVELS = (1, 2, 4, 8, 16, 32)

CONST_COLS = [
    ("ident", P), ("ones", P), ("head_ones", P), ("head_mean", P), ("mean", P), ("future", T),
    ("reset16", T), ("gla_block", P), ("parity", 2), ("select", 4 * P),
    ("before", P), ("slots", CAP), ("earlier", E * E), ("chunk_of16", 8),
]
RET_COLS = [("rot", P), ("cos", T), ("sin", T), ("decay", 4 * T), ("reset64", T)]
RW_COLS = [("strict", P), ("upto", P), ("levels", len(LEVELS) * P), ("head_cols", 2 * P)]
PARAM_COLS = [
    ("norm1_e", 8), ("conv_w", 32), ("conv_b", 8), ("ml_norm", 4), ("gla_b", 2), ("gla_norm", 4), ("norm2_e", 8),
    ("norm1_o", 8), ("ret_norm", 4), ("mu", 14), ("w0", 4), ("a0", 4), ("k_k", 4), ("k_a", 4), ("r_k", 4),
    ("ln_g", 4), ("ln_b", 4), ("norm2_o", 8), ("final", 8), ("gate_b", 2),
]


FFN_ORDER = [("gate", 0), ("up", 0)]
for _c in range(1, FC):
    FFN_ORDER += [("gate", _c), ("down", _c - 1), ("up", _c)]
FFN_ORDER += [("down", FC - 1)]


def column_ranges(cols):
    at, out = 0, {}
    for name, n in cols:
        out[name] = (at, at + n)
        at += n
    return out, at


CONST_AT, CONST_N = column_ranges(CONST_COLS)
RET_AT, RET_N = column_ranges(RET_COLS)
RW_AT, RW_N = column_ranges(RW_COLS)
PARAM_AT, PARAM_N = column_ranges(PARAM_COLS)


def constants():
    c = {}
    r, t = np.arange(P)[:, None], np.arange(T)[None, :]
    s = t[:, :P]
    c["ident"] = r == s
    c["ones"] = np.ones((P, P))
    c["mean"] = np.full((P, P), 1.0 / P)
    c["head_ones"] = r // 64 == s // 64
    c["head_mean"] = (r // 64 == s // 64) / 64.0
    c["future"] = np.where(t >= r, 0.0, BIG)
    c["rot"] = 1.0 * (s == r + 64) - 1.0 * (s == r - 64)
    inv = np.float32(10000.0) ** (-np.arange(0, P, 2, dtype=np.float32) / np.float32(P))
    ang = np.arange(T, dtype=np.float32)[None, :] * inv[:, None]
    c["cos"] = np.tile(np.cos(ang), (2, 1))
    c["sin"] = np.tile(np.sin(ang), (2, 1))
    gamma = np.log1p(-np.exp2(-5.0 - np.arange(4)))
    c["decay"] = np.concatenate(
        [np.where(t >= r, np.exp(g * (t - r)), 0.0) * P ** -0.5 for g in gamma], axis=1)
    c["reset16"] = np.broadcast_to(t % GC != 0, (P, T))
    c["reset64"] = np.broadcast_to(t % RC != 0, (P, T))
    c["gla_block"] = (r // GC == s // GC) & (r % GC <= s % GC)
    c["parity"] = r // 64 == np.arange(2)[None, :]
    c["chunk_of16"] = r // GC == np.arange(8)[None, :]
    c["select"] = np.repeat(np.arange(4), P)[None, :] == r
    block = r // RC == s // RC
    c["strict"] = block & (r < s)
    c["upto"] = block & (r <= s)
    c["levels"] = np.concatenate([(r // (2 * m) == s // (2 * m)) & (r // m < s // m) for m in LEVELS], axis=1)
    c["before"] = r < s
    c["head_cols"] = np.broadcast_to(np.arange(2 * P)[None, :] // 64 % 2 == np.arange(2 * P)[None, :] // P, (P, 2 * P))
    c["slots"] = np.broadcast_to(np.arange(CAP)[None, :], (P, CAP))
    e = np.arange(E)
    c["earlier"] = np.broadcast_to((e[None, :] < e[:, None]).reshape(1, E * E), (P, E * E))
    pack = lambda cols: np.concatenate([np.asarray(c[n], np.float32) for n, _ in cols], axis=1)
    return pack(CONST_COLS), pack(RET_COLS), pack(RW_COLS)


def Names(**named):
    return namedtuple("Names", named)(**named)


def bc(ap, axis, n):
    a = ap.unsqueeze(axis)
    return a.broadcast_to([*a.shape[:axis], n, *a.shape[axis + 1:]])


def counted(engine, sem):
    n = [0]

    def after(ins):
        n[0] += 1
        ins.then_inc(sem, 1)
        engine.wait_ge(sem, n[0])

    return after


def weight_chunks(g):
    def cols(w, c0, n=CH):
        return w[:, c0:c0 + n].rearrange("(k p) c -> p k c", p=P)

    def rows(w, r0):
        return w[r0:r0 + CH, :].rearrange("(k p) c -> p k c", p=P)

    e_in, o_in = g.e_w_in[0], g.o_w_in[0]
    out = [cols(e_in, c) for c in (2056, 0, 512, 1024, 1536, 2568, 3080)]
    out += [cols(g.e_w_out[0], c) for c in (0, 512)]
    for kind, c in FFN_ORDER:
        out.append({"gate": lambda: cols(g.e_ffn_w_gate[0], c * CH), "up": lambda: cols(g.e_ffn_w_up[0], c * CH),
                    "down": lambda: rows(g.e_ffn_w_down[0], c * CH)}[kind]())
    out += [cols(o_in, c, min(CH, 3840 - c)) for c in (3584, 2560, 2048, 3072, 0, 512, 1024, 1536)]
    out += [cols(g.o_w_out[0], c) for c in (0, 512)]
    return out


E_IN, E_OUT, FFN, O_IN, O_OUT, DENSE = 0, 7, 9, 30, 38, 40


class Program:
    def __init__(self, nc, g, ctx):
        self.nc, self.g, self.ctx = nc, g, ctx
        self.loads = weight_chunks(g)
        self.issued = 0
        self.stage_sems = []
        sb = self.sb
        self.ps = ctx.enter_context(nc.psum_tensor("ps", [P, 8, 512], F32))
        self.ring = sb("ring", [P, SLOTS, 8 * CH])
        self.consts = sb("consts", [P, CONST_N])
        self.params = sb("params", [P, PARAM_N])
        self.res = sb("res", [P, KT, T])
        self.h = sb("h", [P, KT, T])
        self.narrow = sb("narrow", [P, KT, 24])
        self.gate_up = sb("gate_up", [16, T])
        self.slot_filled = [self.sem(f"slot_filled{i}") for i in range(SLOTS)]
        self.chunk_used = self.sem("chunk_used")
        self.stage_sems = []

    def sb(self, name, shape, ctx=None, dt=F32):
        return (ctx or self.ctx).enter_context(self.nc.sbuf_tensor(name, shape, dt))

    def sem(self, name):
        self.stage_sems.append(self.nc.alloc_semaphore(name))
        return self.stage_sems[-1]

    def recycle(self):
        self.nc.clear_and_free_semaphores(self.stage_sems)
        self.nc.all_engine_barrier()
        self.stage_sems = []

    def c(self, name, rows=P):
        a, b = CONST_AT[name]
        return self.consts[0:rows, a:b]

    def p(self, name, i=None, rows=P):
        a, b = PARAM_AT[name]
        return self.params[0:rows, a:b] if i is None else self.params[0:rows, a + i:a + i + 1]

    def bank(self, b, n=1):
        return self.ps[:, b:b + n, :].rearrange("p b c -> p (b c)")

    def chunk(self, n):
        w = self.ring[:, n % SLOTS, :]
        if tuple(self.loads[n].shape) == (P, MF, D):
            return w.rearrange("p (k c) -> p k c", k=MF)
        return w.rearrange("p (k c) -> p k c", k=KT)[:, :, 0:self.loads[n].shape[2]]

    def load_chunks(self, sp, end):
        for n in range(self.issued, min(end, DENSE)):
            if n >= SLOTS:
                sp.wait_ge(self.chunk_used, n - SLOTS + 1)
            sp.dma_start(self.chunk(n), self.loads[n]).then_inc(self.slot_filled[n % SLOTS], 16)
        self.issued = max(self.issued, min(end, DENSE))

    def wait_chunk(self, pe, n):
        pe.wait_ge(self.slot_filled[n % SLOTS], 16 * (n // SLOTS + 1))


def embed(k):
    nc, g = k.nc, k.g
    loaded, rest_loaded, turned, kept = k.sem("x_loaded"), k.sem("rest_loaded"), k.sem("x_turned"), k.sem("x_kept")
    with ExitStack() as own:
        x = k.sb("x_rows", [P, TH, D], own)
        block = own.enter_context(nc.Block())

        @block.sync
        def _(sp):
            sp.dma_start(k.consts[:, 0:2 * P], g.consts[:, 0:2 * P]).then_inc(loaded, 16)
            sp.dma_start(x[:, :, :], g.x[0].rearrange("(a p) d -> p a d", p=P)).then_inc(loaded, 16)
            sp.dma_start(k.params[:, :], g.params).then_inc(rest_loaded, 16)
            sp.dma_start(k.consts[:, 2 * P:], g.consts[:, 2 * P:]).then_inc(rest_loaded, 16)
            w = g.e_w_in[0]
            sp.dma_start(k.narrow[:, :, 0:8], w[:, 2048:2056].rearrange("(k p) c -> p k c", p=P)).then_inc(rest_loaded, 16)
            sp.dma_start(k.narrow[:, :, 8:24], w[:, 3592:3608].rearrange("(k p) c -> p k c", p=P)).then_inc(rest_loaded, 16)
            sp.dma_start(k.gate_up[:, :], g.e_gla_gate_up[0]).then_inc(rest_loaded, 16)
            k.load_chunks(sp, SLOTS)

        @block.tensor
        def _(pe):
            pe.wait_ge(loaded, 32)
            for kt in range(KT):
                for a in range(TH):
                    ins = pe.transpose(k.bank(kt)[:, a * P:(a + 1) * P], x[:, a, kt * P:(kt + 1) * P], k.c("ident"))
                ins.then_inc(turned, 1)

        @block.vector
        def _(dve):
            for kt in range(KT):
                dve.wait_ge(turned, kt + 1)
                dve.tensor_copy(k.res[:, kt, :], k.bank(kt)[:, 0:T]).then_inc(kept, 1)
            dve.wait_ge(kept, KT)
            dve.wait_ge(rest_loaded, 16 * 5)


def rms_norm(k, name, gain, end, out=None):
    nc = k.nc
    squared, summed, scaled = k.sem(name + "_squared"), k.sem(name + "_summed"), k.sem(name + "_scaled")
    rooted = k.sem(name + "_rooted")
    with ExitStack() as own:
        sq = k.sb(name + "_sq", [P, KT, T], own)
        rstd = k.sb(name + "_rstd", [P, T], own)
        mean = k.sb(name + "_mean", [P, T], own)
        block = own.enter_context(nc.Block())

        @block.sync
        def _(sp):
            k.load_chunks(sp, end)

        @block.scalar
        def _(act):
            for kt in range(0, KT, 2):
                act.activation(sq[:, kt:kt + 2, :], k.res[:, kt:kt + 2, :], ACT.Square).then_inc(squared, 1)
            act.wait_ge(rooted, 2)
            act.activation(rstd[:, :], mean[:, :], ACT.Sqrt).then_inc(rooted, 1)

        @block.tensor
        def _(pe):
            for kt in range(KT):
                pe.wait_ge(squared, kt // 2 + 1)
                ins = pe.matmul(k.bank(0)[:, 0:T], k.c("ones"), sq[:, kt, :], start=kt == 0, stop=kt == KT - 1)
            ins.then_inc(summed, 1)

        @block.vector
        def _(dve):
            dve.wait_ge(summed, 1)
            dve.tensor_scalar(mean[:, :], k.bank(0)[:, 0:T], 1.0 / D, EPS, ALU.mult, ALU.add).then_inc(rooted, 1)
            dve.wait_ge(rooted, 1)
            dve.reciprocal(mean[:, :], mean[:, :]).then_inc(rooted, 1)
            dve.wait_ge(rooted, 3)
            for kt in range(KT):
                dve.scalar_tensor_tensor(out=(out or k.h)[:, kt, :], in0=k.res[:, kt, :], scalar=k.p(gain, kt),
                                         in1=rstd[:, :], op0=ALU.mult, op1=ALU.mult).then_inc(scaled, 1)
            dve.wait_ge(scaled, KT)


PIECE = KT * CH // 4
DENSE_SPLIT = 3


class SplitWeights:

    def __init__(self, k, name, first, own):
        self.k, self.first = k, first
        self.w_hi, self.w_lo = (k.sb(f"{name}_w_{n}", [P, DENSE_SPLIT, PIECE], own, F32R) for n in ("hi", "lo"))
        self.hi_ready, self.lo_ready, self.used = (k.sem(f"{name}_w_{n}") for n in ("hi_ready", "lo_ready", "used"))

    def piece(self, j):
        n = self.first + j // 4
        w = self.k.chunk(n)
        if w.shape[1] == MF:
            return w[:, j % 4, :], lambda part: part[:, j % DENSE_SPLIT, :]
        c = w.shape[2]
        return w[:, 2 * (j % 4):2 * (j % 4) + 2, :], lambda part: part[:, j % DENSE_SPLIT, 0:2 * c].rearrange("p (k c) -> p k c", k=2)

    def hi_of(self, j):
        return self.w_hi[:, j % DENSE_SPLIT, :]

    def lo_of(self, j):
        return self.w_lo[:, j % DENSE_SPLIT, :]

    def hi(self, act, j):
        src, part = self.piece(j)
        if j % 4 == 0:
            self.k.wait_chunk(act, self.first + j // 4)
        if j >= DENSE_SPLIT:
            act.wait_ge(self.used, j - DENSE_SPLIT + 1)
        act.copy(part(self.w_hi), src).then_inc(self.hi_ready, 1)

    def lo(self, engine, j):
        src, part = self.piece(j)
        engine.wait_ge(self.hi_ready, j + 1)
        engine.tensor_tensor(part(self.w_lo), src, part(self.w_hi).bitcast(F32), ALU.subtract).then_inc(self.lo_ready, 1)


class SplitStream:

    def __init__(self, k, name, own):
        self.k = k
        self.x_hi, self.x_lo = (k.sb(f"{name}_h_{n}", [P, KT, T], own, F32R) for n in ("hi", "lo"))
        self.hi_ready, self.ready = k.sem(name + "_h_hi"), k.sem(name + "_h_ready")

    def hi(self, act, i):
        act.copy(self.x_hi[:, 2 * i:2 * i + 2, :], self.k.h[:, 2 * i:2 * i + 2, :]).then_inc(self.hi_ready, 1)

    def lo(self, engine, i):
        engine.wait_ge(self.hi_ready, i + 1)
        engine.tensor_tensor(self.x_lo[:, 2 * i:2 * i + 2, :], self.k.h[:, 2 * i:2 * i + 2, :],
                             self.x_hi[:, 2 * i:2 * i + 2, :].bitcast(F32), ALU.subtract).then_inc(self.ready, 1)


def three(pe, out, a_hi, a_lo, b_hi, b_lo, start):
    pe.matmul(out, a_hi, b_hi, start=start, stop=False, skip_group_check=True)
    pe.matmul(out, a_hi, b_lo, start=False, stop=False, skip_group_check=True)
    return pe.matmul(out, a_lo, b_hi, start=False, stop=True, skip_group_check=True)


def product_tokens(pe, out, w, x, j):
    for a in range(TH):
        for i in range(2):
            kt = 2 * (j % 4) + i
            cols, toks = slice(i * CH, (i + 1) * CH), slice(a * P, (a + 1) * P)
            ins = three(pe, out[:, a * CH:(a + 1) * CH], x.x_hi[:, kt, toks], x.x_lo[:, kt, toks], w.hi_of(j)[:, cols],
                        w.lo_of(j)[:, cols], kt == 0)
    return ins


def product(pe, out, w, x, j, m_tiles=MF):
    hi, lo = w.hi_of(j), w.lo_of(j)
    for m in range(m_tiles):
        for i in range(2):
            kt = 2 * (j % 4) + i
            cols = slice((i * m_tiles + m) * P, (i * m_tiles + m + 1) * P)
            ins = three(pe, out[:, m * T:(m + 1) * T], hi[:, cols], lo[:, cols], x.x_hi[:, kt, :], x.x_lo[:, kt, :],
                        kt == 0 and m % 2 == 0)
    return ins


def project(pe, k, w, x, i, out, tokens_out=False, m_tiles=MF):
    for j in range(4 * i, 4 * i + 4):
        if j < 4:
            pe.wait_ge(x.ready, j + 1)
        pe.wait_ge(w.lo_ready, j + 1)
        ins = product_tokens(pe, out, w, x, j) if tokens_out else product(pe, out, w, x, j, m_tiles)
        ins.then_inc(w.used, 1)
    pe.sem_inc(k.chunk_used, 1)


def out_project(k, name, n, end, after=None):
    added = k.sem(name + "_added")
    with ExitStack() as own:
        w, x = SplitWeights(k, name, n, own), SplitStream(k, name, own)
        block = own.enter_context(k.nc.Block())

        @block.sync
        def _(sp):
            k.load_chunks(sp, end)
            if after:
                after(sp)

        @block.tensor
        def _(pe):
            for i in range(2):
                project(pe, k, w, x, i, k.bank(4 * i, 2))

        @block.scalar
        def _(act):
            for j in range(8):
                if j < 4:
                    x.hi(act, j)
                w.hi(act, j)

        @block.vector
        def _(dve):
            for j in range(8):
                if j < 4:
                    x.lo(dve, j)
                w.lo(dve, j)
            for i in range(2):
                dve.wait_ge(w.used, 4 * i + 4)
                r = k.res[:, 4 * i:4 * i + 4, :]
                dve.tensor_tensor(r, r, k.bank(4 * i, 2).rearrange("p (m t) -> p m t", m=4), ALU.add).then_inc(added, 1)
            dve.wait_ge(added, 2)


def even_mixer(k):
    with ExitStack() as own:
        sb = lambda n, shape: k.sb("e_" + n, shape, own)
        m = Names(
            gqk=sb("gqk", [P, 4, T]),
            gv=sb("gv", [P, TH, CH]), gr=sb("gr", [P, 4, T]),
            qk=sb("qk", [P, 8, T]),
            v=sb("v", [P, TH, CH]), o=sb("o", [P, 4, T]),
            gates=sb("gates", [4, 10, T]),
            la=sb("la", [P, 4, 2, T]),
            expb=sb("expb", [P, 2, T]),
            kdec=sb("kdec", [P, 2, T]),
            qe=sb("qe", [P, 2, 2, T]),
            pair=sb("pair", [P, 16 * GC * GC]),
            pads=sb("pads", [P, 2, 4, T + 3]),
            att=sb("att", [P, 8, P]),
            tmp=sb("tmp", [P, 4, T]),
        )
        even_project(k, m)
        even_attend(k, m, sb)


(LOG_I, ABS_F, EXP_F, LN_F, NEG_F, LOG_F, SUM_F, U, MAX_U, MAX_M) = range(10)


def even_project(k, m):
    nc, g = k.nc, k.g
    s = Names(**{n: k.sem("ep_" + n) for n in (
        "small_done", "small_kept", "proj_kept", "low_done", "gates_split", "gates_exp", "gates_ln",
        "decay_summed", "decay_exp", "diff_ready", "pair_exp", "pair_ready", "att_done", "dve_chain", "act_chain",
        "zeroed", "conv_done", "qk_done", "gated")})
    with ExitStack() as own:
        w, x = SplitWeights(k, "ep", E_IN, own), SplitStream(k, "ep", own)
        wsm, gup = k.narrow, k.gate_up
        low = k.sb("ep_low", [16, T], own)
        attc = k.sb("ep_attc", [P, 8, GC], own)
        block = own.enter_context(nc.Block())
        icj = m.pair[:, :].rearrange("p (i c j) -> p i c j", i=GC, j=GC)
        flat = m.pair[:, :].rearrange("p (i t) -> p i t", i=GC)

        @block.sync
        def _(sp):
            k.load_chunks(sp, E_OUT + SLOTS)

        @block.gpsimd
        def _(pool):
            pool.memset(m.pads[:, :, :, 0:3], 0.0).then_inc(s.zeroed, 1)
            pool.memset(m.qe[:, :, :, :], 0.0).then_inc(s.zeroed, 1)
            for j in range(4 * 7):
                w.lo(pool, j)

        @block.tensor
        def _(pe):
            for a, b, out in ((0, 4, k.bank(6)[0:4, 0:T]), (4, 8, k.bank(6)[0:4, T:2 * T]), (8, 24, k.bank(7)[0:16, 0:T])):
                for kt in range(KT):
                    ins = pe.matmul(out, wsm[:, kt, a:b], k.h[:, kt, :], start=kt == 0, stop=kt == KT - 1)
            ins.then_inc(s.small_done, 1)
            project(pe, k, w, x, 0, k.bank(0, 2))
            pe.wait_ge(s.small_kept, 1)
            for i in range(2):
                ins = pe.matmul(k.bank(7)[:, i * T:(i + 1) * T], gup[:, i * P:(i + 1) * P], low[:, :], start=True, stop=True)
            ins.then_inc(s.low_done, 1)
            for n in range(1, 7):
                if n >= 3:
                    pe.wait_ge(s.proj_kept, n - 2)
                project(pe, k, w, x, n, k.bank(2 * (n % 3), 2), tokens_out=n in (3, 5))
                if n in (4, 6):
                    hp = n // 2 - 2
                    pe.wait_ge(s.pair_ready, hp + 1)
                    for a in range(TH):
                        for i in range(GC):
                            at = (hp * TH + a) * 2
                            ins = pe.matmul(k.bank(6)[:, 0:P].rearrange("p (g i) -> p g i", i=GC)[:, at:at + 2, i],
                                            flat[:, i, a * P:(a + 1) * P], k.c("parity"), start=True, stop=True)
                    ins.then_inc(s.att_done, 1)

        @block.scalar
        def _(act):
            for j in range(3):
                x.hi(act, j)
                w.hi(act, j)
            x.hi(act, 3)
            act.wait_ge(s.small_done, 1)
            act.copy(low[:, :], k.bank(7)[0:16, 0:T]).then_inc(s.small_kept, 1)
            for j in range(3, 7):
                w.hi(act, j)
            act.wait_ge(w.used, 4)
            act.mul(m.gqk[:, 0:2, :].rearrange("p a t -> p (a t)"), k.bank(0), 64 ** -0.5).then_inc(s.gated, 1)
            act.copy(m.gqk[:, 2:4, :].rearrange("p a t -> p (a t)"), k.bank(1)).then_inc(s.proj_kept, 1)
            act.wait_ge(s.gates_split, 2)
            act.activation(m.gates[:, EXP_F, :], m.gates[:, ABS_F, :], ACT.Exp, scale=-1.0).then_inc(s.gates_exp, 1)
            act.activation(m.la[:, 1, :, :], m.la[:, 0, :, :], ACT.Exp, scale=-1.0).then_inc(s.gates_exp, 1)
            act.wait_ge(s.gates_exp, 2)
            act.activation(m.gates[:, LN_F, :], m.gates[:, EXP_F, :], ACT.Ln, bias=1.0).then_inc(s.gates_ln, 1)
            act.activation(m.la[:, 2, :, :], m.la[:, 1, :, :], ACT.Ln, bias=1.0).then_inc(s.gates_ln, 1)
            act.wait_ge(s.decay_summed, 1)
            act.activation(m.expb[:, :, :], m.la[:, 0, :, :], ACT.Exp).then_inc(s.decay_exp, 1)
            act.activation(m.la[:, 3, :, :], m.la[:, 1, :, :], ACT.Exp).then_inc(s.decay_exp, 1)
            act.wait_ge(s.diff_ready, 1)
            act.activation(m.pair[:, :], m.pair[:, :], ACT.Exp).then_inc(s.pair_exp, 1)
            act.wait_ge(s.zeroed, 1)
            for n in range(1, 7):
                for j in range(4 * n + 3, min(4 * n + 7, 28)):
                    w.hi(act, j)
                act.wait_ge(w.used, 4 * n + 4)
                if n in (1, 2):
                    act.copy(m.pads[:, n - 1, :, 3:], k.bank(2 * (n % 3), 2).rearrange("p (m t) -> p m t", m=4)).then_inc(s.proj_kept, 1)
                else:
                    dst = (m.v, m.o, m.gv, m.gr)[n - 3]
                    act.copy(dst[:, :, :].rearrange("p a b -> p (a b)"), k.bank(2 * (n % 3), 2)).then_inc(s.proj_kept, 1)
                if n == 5:
                    act.wait_ge(s.diff_ready, 2)
                    act.activation(m.pair[:, :], m.pair[:, :], ACT.Exp).then_inc(s.pair_exp, 1)
            act.wait_ge(s.conv_done, 2)
            act.wait_ge(s.proj_kept, 7)
            act.activation(m.qk[:, :, :], m.qk[:, :, :], ACT.Silu).then_inc(s.gated, 1)
            act.activation(m.gr[:, :, :], m.gr[:, :, :], ACT.Silu).then_inc(s.gated, 1)
            act.activation(m.o[:, :, :], m.o[:, :, :], ACT.Sigmoid).then_inc(s.gated, 1)
            act.wait_ge(s.gated, 4)

        @block.vector
        def _(dve):
            for i in range(4):
                x.lo(dve, i)
            step = counted(dve, s.dve_chain)
            gt = m.gates
            dve.wait_ge(s.small_done, 1)
            step(dve.tensor_scalar(gt[:, LOG_I, :], k.bank(6)[0:4, 0:T], k.p("gate_b", 0, 4), None, ALU.add))
            step(dve.tensor_scalar(gt[:, LOG_F, :], k.bank(6)[0:4, T:2 * T], k.p("gate_b", 1, 4), None, ALU.add))
            step(dve.tensor_scalar(gt[:, NEG_F, :], gt[:, LOG_F, :], 0.0, None, ALU.min))
            step(dve.scalar_tensor_tensor(out=gt[:, ABS_F, :], in0=gt[:, LOG_F, :], scalar=-1.0, in1=gt[:, LOG_F, :],
                                          op0=ALU.mult, op1=ALU.max))
            dve.wait_ge(s.low_done, 1)
            for i in range(2):
                step(dve.tensor_scalar(m.la[:, 2, i, :], k.bank(7)[:, i * T:(i + 1) * T], k.p("gla_b", i), None, ALU.add))
                step(dve.tensor_scalar(m.la[:, 3, i, :], m.la[:, 2, i, :], 0.0, None, ALU.min))
                dve.scalar_tensor_tensor(out=m.la[:, 0, i, :], in0=m.la[:, 2, i, :], scalar=-1.0, in1=m.la[:, 2, i, :],
                                         op0=ALU.mult, op1=ALU.max).then_inc(s.gates_split, 1)
            dve.wait_ge(s.gates_ln, 2)
            step(dve.tensor_tensor(m.la[:, 0, :, :], m.la[:, 3, :, :], m.la[:, 2, :, :], ALU.subtract))
            step(dve.tensor_scalar(m.la[:, 2, :, :], m.la[:, 0, :, :], 1.0 / 16.0, None, ALU.mult))
            for hp in range(2):
                step(dve.tensor_tensor_scan(m.la[:, 0, hp, :], k.c("reset16"), m.la[:, 2, hp, :], 0.0, ALU.mult, ALU.add))
            b = m.la[:, 0, :, :].rearrange("p h (c t) -> p (h c) t", t=GC)
            dve.tensor_tensor(m.la[:, 1, :, :].rearrange("p h (c t) -> p (h c) t", t=GC),
                              b[:, :, GC - 1:GC].broadcast_to([P, 2 * GN, GC]), b, ALU.subtract).then_inc(s.decay_summed, 1)

            def pair_diff(hp):
                bb = m.la[:, 0, hp, :].rearrange("p (c t) -> p c t", t=GC)
                dve.tensor_tensor(icj, bc(bb.rearrange("p c i -> p i c"), 3, GC), bc(bb, 1, GC), ALU.subtract).then_inc(s.diff_ready, 1)

            def pair_product(hp):
                dve.wait_ge(s.pair_exp, hp + 1)
                step(dve.scalar_tensor_tensor(out=flat, in0=flat, scalar=1.0, in1=bc(m.gqk[:, 2 + hp, :], 1, GC),
                                              op0=ALU.min, op1=ALU.mult))
                q = m.gqk[:, hp, :].rearrange("p (c i) -> p i c", i=GC)
                dve.tensor_tensor(icj, icj, bc(q, 3, GC), ALU.mult).then_inc(s.pair_ready, 1)

            def conv(n):
                dve.wait_ge(s.proj_kept, n + 1)
                for i in range(4):
                    ch = (n - 1) * 4 + i
                    step(dve.tensor_scalar(m.tmp[:, i, :], m.pads[:, n - 1, i, 3:], k.p("conv_w", 24 + ch),
                                           k.p("conv_b", ch), ALU.mult, ALU.add))
                    for tap in (2, 1, 0):
                        out = m.tmp[:, i, :] if tap else m.qk[:, ch, :]
                        step(dve.scalar_tensor_tensor(out=out, in0=m.pads[:, n - 1, i, tap:tap + T],
                                                      scalar=k.p("conv_w", tap * 8 + ch), in1=m.tmp[:, i, :],
                                                      op0=ALU.mult, op1=ALU.add))
                dve.sem_inc(s.conv_done, 1)

            pair_diff(0)
            step(dve.tensor_tensor(gt[:, LOG_F, :], gt[:, NEG_F, :], gt[:, LN_F, :], ALU.subtract))
            step(dve.tensor_tensor_scan(gt[:, SUM_F, :], k.c("ones", 4)[:, 0:1].broadcast_to([4, T]), gt[:, LOG_F, :], 0.0,
                                        ALU.mult, ALU.add))
            step(dve.tensor_tensor(gt[:, U, :], gt[:, LOG_I, :], gt[:, SUM_F, :], ALU.subtract))
            step(dve.tensor_tensor_scan(gt[:, MAX_U, :], gt[:, U, :], gt[:, U, :], 0.0, ALU.max, ALU.max))
            step(dve.tensor_tensor(gt[:, MAX_M, :], gt[:, MAX_U, :], gt[:, SUM_F, :], ALU.add))
            dve.wait_ge(s.decay_exp, 2)
            dve.wait_ge(s.zeroed, 2)
            dve.wait_ge(s.proj_kept, 1)
            dve.wait_ge(s.gated, 1)
            for hd in range(2):
                r = slice(64 * hd, 64 * hd + 64)
                step(dve.tensor_tensor(m.qe[r, :, hd, :], m.gqk[r, 0:2, :], m.expb[r, :, :], ALU.mult))
            step(dve.tensor_tensor(m.kdec[:, :, :], m.gqk[:, 2:4, :], m.la[:, 3, :, :], ALU.mult))
            pair_product(0)
            conv(1)
            conv(2)
            dve.wait_ge(s.att_done, 1)
            pair_diff(1)
            pair_product(1)
            dve.wait_ge(s.att_done, 2)
            step(dve.tensor_copy(attc[:, :, :], k.bank(6)[:, 0:P].rearrange("p (g i) -> p g i", i=GC)))
            blocks = k.c("gla_block").rearrange("p (c i) -> p c i", i=GC)
            step(dve.tensor_tensor(m.att[:, :, :].rearrange("p g (c i) -> p g c i", i=GC), bc(attc[:, :, :], 2, 8),
                                   bc(blocks, 1, 8), ALU.mult))


def even_attend(k, m, sb):
    nc = k.nc
    s = Names(**{n: k.sem("ea_" + n) for n in (
        "turned", "turned_kept", "spread", "spread_kept", "spread_exp", "limited", "weighted", "scored", "p_ready",
        "num_done", "gated", "mean_done", "centred", "squared", "var_done", "mixed", "u_done", "state_ready",
        "inter_done", "dve_chain", "inverted", "rooted", "gla_squared", "gla_var_done", "gla_mixed")})
    with ExitStack() as own:
        ucol = k.sb("ea_u_cols", [P, TH, 4], own)
        wts = k.sb("ea_wts", [P, 4, T + P], own)
        ot = m.gqk
        spread = m.la[:, :, :, :].rearrange("p a b t -> p a (b t)")
        kex = m.pair[:, :].rearrange("p (g c f) -> p g c f", c=8, f=P)
        pads = m.pads[:, :, :, :].rearrange("p a b t -> p (a b t)")
        state = pads[:, 0:8 * T].rearrange("p (c a t) -> p c a t", c=4, a=2)
        tmp = m.tmp
        block = own.enter_context(nc.Block())

        @block.sync
        def _(sp):
            k.load_chunks(sp, E_OUT + SLOTS)

        def inter(pe, c):
            pe.wait_ge(s.state_ready, c + 1)
            for hd in range(4):
                b = k.bank(4 + hd // 2)[:, (hd % 2) * T + c * GC:(hd % 2) * T + (c + 1) * GC]
                ins = pe.matmul(b, state[:, c % 4, hd // 2, (hd % 2) * P:(hd % 2 + 1) * P],
                                m.qe[:, hd // 2, hd % 2, c * GC:(c + 1) * GC], start=False, stop=False, skip_group_check=True)
            return ins.then_inc(s.inter_done, 1)

        @block.tensor
        def _(pe):
            for a in range(TH):
                pe.transpose(k.bank(6)[:, a * 4:a * 4 + 4], m.gates[:, U, a * P:(a + 1) * P], k.c("ident", 4)[:, 0:4])
            for gi in range(4):
                ins = pe.transpose(k.bank(7)[:, gi * P:(gi + 1) * P], m.kdec[:, gi // 2, (gi % 2) * P:(gi % 2 + 1) * P], k.c("ident"))
            ins.then_inc(s.turned, 1)
            for hd in range(4):
                ins = pe.matmul(k.bank(hd), k.c("select", 4)[:, hd * P:(hd + 1) * P], m.gates[:, MAX_U:MAX_U + 2, :],
                                start=True, stop=True)
            ins.then_inc(s.spread, 1)
            pe.wait_ge(s.turned_kept, 2)
            for hd in range(4):
                b = k.bank(4 + hd)
                pe.matmul(b[:, 0:T], m.qk[:, 4 + hd, 0:P], m.qk[:, hd, :], start=True, stop=True)
                pe.matmul(b[:, T:T + P], m.qk[:, 4 + hd, P:T], m.qk[:, hd, P:T], start=True, stop=True).then_inc(s.scored, 1)
            pe.wait_ge(s.spread_kept, 1)
            for hd in range(4):
                pe.wait_ge(s.p_ready, hd + 1)
                b = k.bank(hd)
                cols = slice(hd * P, (hd + 1) * P)
                for w0, w1, at in ((m.v[:, 0, cols], m.v[:, 1, cols], 0), (k.c("ones"), k.c("ones"), T)):
                    pe.matmul(b[:, at:at + T], w0, wts[:, hd, 0:T], start=True, stop=False, skip_group_check=True)
                    ins = pe.matmul(b[:, at + P:at + T], w1, wts[:, hd, T:T + P], start=False, stop=True, skip_group_check=True)
                ins.then_inc(s.num_done, 1)
            for hd in range(4):
                for a in range(TH):
                    b = k.bank(4 + hd // 2)[:, (hd % 2) * T + a * P:(hd % 2) * T + (a + 1) * P]
                    pe.matmul(b, m.gv[:, a, hd * P:(hd + 1) * P], m.att[:, ((hd // 2) * TH + a) * 2 + hd % 2, :],
                              start=hd % 2 == 0 and a == 0, stop=False, skip_group_check=True)
            for ready, sums, done in ((s.gated, 0, s.mean_done), (s.squared, 2, s.var_done)):
                pe.wait_ge(ready, 4 if ready is s.gated else 1)
                src = ot if ready is s.gated else tmp
                for i in range(2):
                    ins = pe.matmul(k.bank(sums + i), k.c("mean"), src[:, 2 * i:2 * i + 2, :], start=True, stop=True)
                ins.then_inc(done, 1)
            for c in range(GN - 1):
                if c >= 2:
                    pe.wait_ge(s.state_ready, c)
                for hp in range(2):
                    ins = pe.matmul(k.bank(6 + c % 2)[:, hp * T:(hp + 1) * T], kex[:, hp * 2 + c // 8, c % 8, :],
                                    m.gv[:, c // 8, hp * T:(hp + 1) * T], start=True, stop=True)
                ins.then_inc(s.u_done, 1)
                if c >= 1:
                    inter(pe, c)
            inter(pe, GN - 1)
            pe.wait_ge(s.gla_squared, 1)
            for i in range(2):
                ins = pe.matmul(k.bank(6 + i), k.c("mean"), tmp[:, 2 * i:2 * i + 2, :], start=True, stop=True)
            ins.then_inc(s.gla_var_done, 1)

        @block.scalar
        def _(act):
            act.wait_ge(s.spread, 1)
            act.copy(spread.rearrange("p h c -> p (h c)"), k.bank(0, 4)).then_inc(s.spread_kept, 1)
            act.wait_ge(s.spread_kept, 1)
            act.activation(spread[:, :, T:2 * T], spread[:, :, T:2 * T], ACT.Exp, scale=-1.0).then_inc(s.spread_exp, 1)
            for hd in range(4):
                act.wait_ge(s.limited, 2 * hd + 2)
                act.activation(wts[:, hd, :], wts[:, hd, :], ACT.Exp, scale=-1.0).then_inc(s.weighted, 1)
            act.wait_ge(s.centred, 1)
            act.activation(tmp[:, :, :], ot[:, :, :], ACT.Square).then_inc(s.squared, 1)
            act.wait_ge(s.inverted, 1)
            act.activation(tmp[:, :, :], tmp[:, :, :], ACT.Sqrt).then_inc(s.rooted, 1)
            act.wait_ge(s.inter_done, GN - 1)
            act.wait_ge(s.mixed, 1)
            act.activation(tmp[:, :, :].rearrange("p h t -> p (h t)"), k.bank(4, 2), ACT.Square).then_inc(s.gla_squared, 1)
            act.wait_ge(s.inverted, 2)
            act.activation(tmp[:, :, :], tmp[:, :, :], ACT.Sqrt).then_inc(s.rooted, 1)

        @block.vector
        def _(dve):
            step = counted(dve, s.dve_chain)
            dve.wait_ge(s.turned, 1)
            dve.tensor_copy(ucol[:, :, :], k.bank(6)[:, 0:8].rearrange("p (a h) -> p a h", a=TH)).then_inc(s.turned_kept, 1)
            kt = k.bank(7).rearrange("p (g f) -> p g f", f=P)
            in_chunk = bc(k.c("chunk_of16"), 2, P)
            for gi in range(4):
                ins = dve.tensor_tensor(kex[:, gi, :, :], bc(kt[:, gi, :], 1, 8), in_chunk, ALU.mult)
                if gi < 3:
                    step(ins)
            ins.then_inc(s.turned_kept, 1)
            dve.wait_ge(s.spread_kept, 1)
            dve.wait_ge(s.turned_kept, 1)
            for hd in range(4):
                dve.scalar_tensor_tensor(out=wts[:, hd, 0:T], in0=spread[:, hd, 0:T], scalar=ucol[:, 0, hd:hd + 1],
                                         in1=k.c("future"), op0=ALU.subtract, op1=ALU.max).then_inc(s.limited, 1)
                dve.scalar_tensor_tensor(out=wts[:, hd, T:T + P], in0=spread[:, hd, P:T], scalar=ucol[:, 1, hd:hd + 1],
                                         in1=k.c("future")[:, 0:P], op0=ALU.subtract, op1=ALU.max).then_inc(s.limited, 1)
            for hd in range(4):
                dve.wait_ge(s.weighted, hd + 1)
                dve.wait_ge(s.scored, hd + 1)
                dve.scalar_tensor_tensor(out=wts[:, hd, :], in0=k.bank(4 + hd)[:, 0:T + P], scalar=P ** -0.5,
                                         in1=wts[:, hd, :], op0=ALU.mult, op1=ALU.mult).then_inc(s.p_ready, 1)
            dve.wait_ge(s.spread_exp, 1)
            for hd in range(4):
                dve.wait_ge(s.num_done, hd + 1)
                step(dve.tensor_copy(tmp[:, hd, :], k.bank(hd)[:, T:2 * T]))
                step(dve.scalar_tensor_tensor(out=tmp[:, hd, :], in0=tmp[:, hd, :], scalar=-1.0, in1=tmp[:, hd, :],
                                              op0=ALU.mult, op1=ALU.max))
                step(dve.tensor_tensor(tmp[:, hd, :], tmp[:, hd, :], spread[:, hd, T:2 * T], ALU.max))
                step(dve.reciprocal(tmp[:, hd, :], tmp[:, hd, :]))
                step(dve.tensor_tensor(ot[:, hd, :], k.bank(hd)[:, 0:T], tmp[:, hd, :], ALU.mult))
                dve.tensor_tensor(ot[:, hd, :], ot[:, hd, :], m.o[:, hd, :], ALU.mult).then_inc(s.gated, 1)
            dve.wait_ge(s.gated, 4)
            dve.wait_ge(s.mean_done, 1)
            flat = lambda a: a.rearrange("p h t -> p (h t)")
            dve.tensor_tensor(flat(ot[:, :, :]), flat(ot[:, :, :]), k.bank(0, 2), ALU.subtract).then_inc(s.centred, 1)
            dve.wait_ge(s.centred, 1)
            dve.wait_ge(s.var_done, 1)
            step(dve.tensor_scalar(flat(tmp[:, :, :]), k.bank(2, 2), EPS, None, ALU.add))
            dve.reciprocal(tmp[:, :, :], tmp[:, :, :]).then_inc(s.inverted, 1)
            dve.wait_ge(s.rooted, 1)
            for hd in range(4):
                ins = dve.scalar_tensor_tensor(out=k.h[:, hd, :], in0=ot[:, hd, :], scalar=k.p("ml_norm", hd),
                                               in1=tmp[:, hd, :], op0=ALU.mult, op1=ALU.mult)
                if hd < 3:
                    step(ins)
            ins.then_inc(s.mixed, 1)
            for c in range(GN - 1):
                dve.wait_ge(s.u_done, c + 1)
                if c == 0:
                    dve.memset(state[:, 0, :, :], 0.0).then_inc(s.state_ready, 1)
                    dve.wait_ge(s.state_ready, 1)
                if c >= 4:
                    dve.wait_ge(s.inter_done, c - 3)
                for hp in range(2):
                    ins = dve.scalar_tensor_tensor(out=state[:, (c + 1) % 4, hp, :], in0=state[:, c % 4, hp, :],
                                                   scalar=m.expb[:, hp, c * GC + GC - 1:c * GC + GC],
                                                   in1=k.bank(6 + c % 2)[:, hp * T:(hp + 1) * T], op0=ALU.mult, op1=ALU.add)
                    if hp == 0:
                        step(ins)
                ins.then_inc(s.state_ready, 1)
                dve.wait_ge(s.state_ready, c + 2)
            dve.wait_ge(s.gla_var_done, 1)
            step(dve.tensor_scalar(flat(tmp[:, :, :]), k.bank(6, 2), EPS, None, ALU.add))
            dve.reciprocal(tmp[:, :, :], tmp[:, :, :]).then_inc(s.inverted, 1)
            dve.wait_ge(s.rooted, 2)
            step(dve.tensor_tensor(flat(tmp[:, :, :]), flat(tmp[:, :, :]), k.bank(4, 2), ALU.mult))
            for hd in range(4):
                step(dve.scalar_tensor_tensor(out=k.h[:, 4 + hd, :], in0=tmp[:, hd, :], scalar=k.p("gla_norm", hd),
                                              in1=m.gr[:, hd, :], op0=ALU.mult, op1=ALU.mult))


def dense_ffn(k):
    with ExitStack() as own:
        s = Names(**{n: k.sem("ffn_" + n) for n in ("gate_kept", "multiplied", "hid_hi", "hid_ready", "added")})
        w, x = SplitWeights(k, "ffn", FFN, own), SplitStream(k, "ffn", own)
        gate, hid = k.sb("ffn_gate", [P, MF, T], own), k.sb("ffn_hidden", [P, MF, T], own)
        hid_hi, hid_lo = k.sb("ffn_hid_hi", [P, MF, T], own, F32R), k.sb("ffn_hid_lo", [P, MF, T], own, F32R)
        block = own.enter_context(k.nc.Block())
        flat = lambda a: a.rearrange("p m t -> p (m t)")
        pieces = 4 * len(FFN_ORDER)

        @block.sync
        def _(sp):
            k.load_chunks(sp, O_IN + SLOTS)

        @block.tensor
        def _(pe):
            for j in range(pieces):
                kind, c = FFN_ORDER[j // 4]
                if j % 4 == 0 and kind == "down":
                    pe.wait_ge(s.hid_ready, c + 1)
                elif j % 4 == 0 and c >= 1:
                    pe.wait_ge(s.gate_kept if kind == "gate" else s.multiplied, c)
                if j < 4:
                    pe.wait_ge(x.ready, j + 1)
                pe.wait_ge(w.lo_ready, j + 1)
                if kind == "down":
                    f = j % 4
                    for m in range(KT):
                        ins = three(pe, k.bank(4 + m // 2)[:, (m % 2) * T:(m % 2 + 1) * T], w.hi_of(j)[:, m * P:(m + 1) * P],
                                    w.lo_of(j)[:, m * P:(m + 1) * P], hid_hi[:, f, :], hid_lo[:, f, :], c == 0 and f == 0 and m % 2 == 0)
                else:
                    ins = product(pe, k.bank(0 if kind == "gate" else 2, 2), w, x, j)
                ins.then_inc(w.used, 1)
                if j % 4 == 3:
                    pe.sem_inc(k.chunk_used, 1)

        @block.scalar
        def _(act):
            for j in range(pieces + 1):
                for c in range(FC):
                    if j == last_piece("gate", c) + DENSE_SPLIT:
                        act.wait_ge(w.used, last_piece("gate", c) + 1)
                        if c >= 1:
                            act.wait_ge(s.multiplied, c)
                        act.activation(flat(gate[:, :, :]), k.bank(0, 2), ACT.Silu).then_inc(s.gate_kept, 1)
                    if j == min(last_piece("up", c) + DENSE_SPLIT + 1, pieces):
                        act.wait_ge(s.multiplied, c + 1)
                        act.copy(hid_hi[:, :, :], hid[:, :, :]).then_inc(s.hid_hi, 1)
                if j < 4:
                    x.hi(act, j)
                if j < pieces:
                    w.hi(act, j)

        @block.vector
        def _(dve):
            for j in range(pieces + 1):
                for c in range(FC):
                    if j == last_piece("up", c) + DENSE_SPLIT:
                        dve.wait_ge(w.used, last_piece("up", c) + 1)
                        dve.wait_ge(s.gate_kept, c + 1)
                        if c >= 1:
                            dve.wait_ge(s.hid_ready, c)
                        dve.tensor_tensor(flat(hid[:, :, :]), flat(gate[:, :, :]), k.bank(2, 2), ALU.mult).then_inc(s.multiplied, 1)
                    if j == min(last_piece("up", c) + DENSE_SPLIT + 1, pieces):
                        dve.wait_ge(s.hid_hi, c + 1)
                        dve.tensor_tensor(hid_lo[:, :, :], hid[:, :, :], hid_hi[:, :, :].bitcast(F32), ALU.subtract).then_inc(s.hid_ready, 1)
                if j < 4:
                    x.lo(dve, j)
                if j < pieces:
                    w.lo(dve, j)
            dve.wait_ge(w.used, pieces)
            for i in range(2):
                r = flat(k.res[:, 4 * i:4 * i + 4, :])
                dve.tensor_tensor(r, r, k.bank(4 + 2 * i, 2), ALU.add).then_inc(s.added, 1)
            dve.wait_ge(s.added, 2)


def odd_mixer(k):
    with ExitStack() as own:
        m = Names(**{n: k.sb("o_" + n, [P, 4, T], own) for n in (
            "r",
            "kh",
            "a",
            "kk",
            "v", "g",
            "bonus")},
            chunk_decay=k.sb("o_chunk_decay", [P, 4, RN], own))
        with ExitStack() as early:
            e = Names(**{n: k.sb("o_" + n, [P, 4, T], early) for n in ("ret_q", "ret_k", "ret_g")},
                      ret_v=k.sb("o_ret_v", [P, TH, CH], early), consts=k.sb("o_ret_consts", [P, RET_N], early))
            odd_project(k, m, e)
            retention(k, e)
        rwkv(k, m)


def odd_project(k, m, e):
    nc, g = k.nc, k.g
    s = Names(**{n: k.sem("op_" + n) for n in (
        "loaded", "zeroed", "proj_kept", "mixed_low", "low_ready", "up_done", "extra_kept", "decay_summed", "exp_ready",
        "kk_squared", "bonus_ready", "dve_chain", "chunk_read", "act_chain")})
    rc = lambda n: e.consts[:, RET_AT[n][0]:RET_AT[n][1]]
    with ExitStack() as own:
        sb = lambda n, shape: k.sb("op_" + n, shape, own)
        w, x = SplitWeights(k, "op", O_IN, own), SplitStream(k, "op", own)
        ups = sb("ups", [P, 3, CH])
        pads = sb("pads", [P, 2, 4, T + 1])
        lowp = sb("low_pads", [P, 2, T + 1])
        low = sb("low", [P, 2, T])
        lw, b, en = sb("log_w", [P, 4, T]), sb("sum_w", [P, 4, T]), sb("exp_minus", [P, 4, T])
        block = own.enter_context(nc.Block())
        flat = lambda a: a.rearrange("p m t -> p (m t)")

        @block.sync
        def _(sp):
            sp.dma_start(e.consts[:, :], g.ret_consts).then_inc(s.loaded, 16)
            sp.wait_ge(s.zeroed, 1)
            sp.dma_start(ups[0:64, 0, :], g.o_rw_w_up[0]).then_inc(s.loaded, 16)
            sp.dma_start(ups[64:P, 1, :], g.o_rw_a_up[0]).then_inc(s.loaded, 16)
            sp.dma_start(ups[:, 2, :], g.o_rw_g_up[0]).then_inc(s.loaded, 16)
            k.load_chunks(sp, O_OUT + SLOTS)

        @block.gpsimd
        def _(pool):
            pool.memset(ups[:, :, :], 0.0).then_inc(s.zeroed, 1)
            pool.memset(pads[:, :, :, 0:1], 0.0).then_inc(s.zeroed, 1)
            pool.memset(lowp[:, :, 0:1], 0.0).then_inc(s.zeroed, 1)
            for j in range(4 * 8):
                w.lo(pool, j)

        @block.tensor
        def _(pe):
            def extra(i, lhsT, rhs, ready, value, tiles=4):
                pe.wait_ge(ready, value)
                if i:
                    pe.wait_ge(s.extra_kept, i)
                for t in range(tiles):
                    ins = pe.matmul(k.bank(6, 2)[:, t * T:(t + 1) * T], lhsT(t), rhs(t), start=True, stop=True)
                ins.then_inc(s.up_done, 1)

            head = lambda t: k.c("head_ones")
            up = lambda i: lambda t: ups[:, i, t * P:(t + 1) * P]
            for i in range(8):
                if i >= 3:
                    pe.wait_ge(s.proj_kept, i - 2)
                project(pe, k, w, x, i, k.bank(2 * (i % 3), 2), tokens_out=i == 6, m_tiles=2 if i == 0 else 4)
                if i == 1:
                    pe.wait_ge(s.loaded, 64)
                    extra(0, up(0), lambda t: low[:, 0, :], s.low_ready, 3)
                if i == 2:
                    extra(1, up(1), lambda t: low[:, 0, :], s.low_ready, 3)
                if i == 3:
                    extra(2, head, lambda t: en[:, t, :], s.kk_squared, 1)
                if i == 4:
                    extra(3, up(2), lambda t: low[:, 1, :], s.low_ready, 3)
                if i == 5:
                    extra(4, head, lambda t: m.bonus[:, t, :], s.bonus_ready, 1)

        @block.scalar
        def _(act):
            def keep(i, dst):
                for j in range(4 * i + 3, min(4 * i + 7, 32)):
                    w.hi(act, j)
                act.wait_ge(w.used, 4 * i + 4)
                act.copy(dst, k.bank(2 * (i % 3), 2).rearrange("p (m t) -> p m t", t=dst.shape[2])[:, 0:dst.shape[1], :])\
                   .then_inc(s.proj_kept, 1)

            for j in range(4):
                x.hi(act, j)
                if j < 3:
                    w.hi(act, j)
            act.wait_ge(s.zeroed, 3)
            keep(0, lowp[:, :, 1:])
            act.wait_ge(s.mixed_low, 1)
            act.activation(low[0:64, 0, :], low[0:64, 0, :], ACT.Tanh).then_inc(s.low_ready, 2)
            act.activation(low[:, 1, :], low[:, 1, :], ACT.Sigmoid).then_inc(s.low_ready, 1)
            keep(1, pads[:, 0, :, 1:])
            act.wait_ge(s.up_done, 1)
            for t in range(4):
                ins = act.activation(lw[:, t, :], k.bank(6, 2)[:, t * T:(t + 1) * T], ACT.Sigmoid, bias=k.p("w0", t))
            ins.then_inc(s.extra_kept, 1)
            keep(2, pads[:, 1, :, 1:])
            act.wait_ge(s.up_done, 2)
            for t in range(4):
                ins = act.activation(m.a[:, t, :], k.bank(6, 2)[:, t * T:(t + 1) * T], ACT.Sigmoid, bias=k.p("a0", t))
            ins.then_inc(s.extra_kept, 1)
            act.wait_ge(s.chunk_read, 1)
            keep(3, pads[:, 0, :, 1:])
            act.wait_ge(s.up_done, 3)
            act.activation(flat(en[:, :, :]), k.bank(6, 2), ACT.Sqrt).then_inc(s.extra_kept, 1)
            keep(4, e.ret_q[:, :, :])
            act.wait_ge(s.up_done, 4)
            act.copy(flat(m.g[:, :, :]), k.bank(6, 2)).then_inc(s.extra_kept, 1)
            keep(5, e.ret_k[:, :, :])
            act.wait_ge(s.decay_summed, 2)
            act.activation(en[:, :, :], b[:, :, :], ACT.Exp, scale=-1.0).then_inc(s.exp_ready, 1)
            act.wait_ge(s.exp_ready, 1)
            act.activation(b[:, :, :], b[:, :, :], ACT.Exp).then_inc(s.exp_ready, 1)
            act.activation(lw[:, :, :], lw[:, :, :], ACT.Exp).then_inc(s.exp_ready, 1)
            keep(6, e.ret_v[:, :, :])
            keep(7, e.ret_g[:, :, :])
            act.wait_ge(s.proj_kept, 8)
            act.activation(e.ret_g[:, :, :], e.ret_g[:, :, :], ACT.Silu).then_inc(s.act_chain, 1)
            act.wait_ge(s.act_chain, 1)

        @block.vector
        def _(dve):
            step = counted(dve, s.dve_chain)

            def shift_mix(dst, src, mu, tiles):
                step(dve.tensor_tensor(dst, src[:, :, 0:T], src[:, :, 1:], ALU.subtract))
                for t in range(tiles):
                    ins = dve.scalar_tensor_tensor(out=dst[:, t, :], in0=dst[:, t, :], scalar=k.p("mu", mu + t),
                                                   in1=src[:, t, 1:], op0=ALU.mult, op1=ALU.add)
                    if t < tiles - 1:
                        step(ins)
                return ins

            for i in range(4):
                x.lo(dve, i)
            dve.wait_ge(s.proj_kept, 1)
            shift_mix(low[:, :, :], lowp[:, :, :], 12, 2).then_inc(s.mixed_low, 1)
            dve.wait_ge(s.proj_kept, 2)
            shift_mix(m.kh[:, :, :], pads[:, 0, :, :], 4, 4).then_inc(s.chunk_read, 1)
            dve.wait_ge(s.chunk_read, 1)
            for t in range(4):
                step(dve.tensor_scalar(m.kk[:, t, :], m.kh[:, t, :], k.p("k_k", t), None, ALU.mult))
            dve.tensor_tensor(en[:, :, :], m.kk[:, :, :], m.kk[:, :, :], ALU.mult).then_inc(s.kk_squared, 1)
            dve.wait_ge(s.extra_kept, 1)
            step(dve.tensor_scalar(lw[:, :, :], lw[:, :, :], -float(np.exp(-0.5)), None, ALU.mult))
            for t in range(4):
                step(dve.tensor_tensor_scan(b[:, t, :], rc("reset64"), lw[:, t, :], 0.0, ALU.mult, ALU.add))
            step(dve.tensor_tensor(lw[:, :, :], b[:, :, :], lw[:, :, :], ALU.subtract))
            dve.wait_ge(s.proj_kept, 3)
            step(shift_mix(m.r[:, :, :], pads[:, 1, :, :], 0, 4))
            dve.wait_ge(s.extra_kept, 2)
            for t in range(4):
                step(dve.tensor_scalar(m.bonus[:, t, :], m.a[:, t, :], -1.0, k.p("k_a", t), ALU.add, ALU.mult))
            step(dve.scalar_tensor_tensor(out=flat(m.kh[:, :, :]), in0=flat(m.bonus[:, :, :]), scalar=1.0, in1=flat(m.kh[:, :, :]),
                                          op0=ALU.add, op1=ALU.mult))
            for t in range(4):
                ins = dve.scalar_tensor_tensor(out=m.bonus[:, t, :], in0=m.r[:, t, :], scalar=k.p("r_k", t),
                                               in1=m.kh[:, t, :], op0=ALU.mult, op1=ALU.mult)
                if t < 3:
                    step(ins)
            ins.then_inc(s.bonus_ready, 1)
            dve.wait_ge(s.proj_kept, 4)
            step(shift_mix(m.v[:, :, :], pads[:, 0, :, :], 8, 4))
            dve.wait_ge(s.extra_kept, 3)
            step(dve.tensor_scalar(en[:, :, :], en[:, :, :], 1e-12, None, ALU.max))
            step(dve.reciprocal(en[:, :, :], en[:, :, :]))
            dve.tensor_tensor(m.kk[:, :, :], m.kk[:, :, :], en[:, :, :], ALU.mult).then_inc(s.decay_summed, 2)
            dve.wait_ge(s.decay_summed, 2)
            step(dve.tensor_tensor(m.a[:, :, :], m.a[:, :, :], m.kk[:, :, :], ALU.mult))
            dve.wait_ge(s.up_done, 5)
            step(dve.tensor_tensor(flat(m.bonus[:, :, :]), k.bank(6, 2), flat(m.v[:, :, :]), ALU.mult))
            dve.wait_ge(s.exp_ready, 3)
            step(dve.tensor_tensor(m.r[:, :, :], m.r[:, :, :], b[:, :, :], ALU.mult))
            step(dve.scalar_tensor_tensor(out=flat(m.kk[:, :, :]), in0=flat(m.kk[:, :, :]), scalar=-1.0, in1=flat(lw[:, :, :]),
                                          op0=ALU.mult, op1=ALU.mult))
            step(dve.tensor_tensor(m.kh[:, :, :], m.kh[:, :, :], en[:, :, :], ALU.mult))
            step(dve.tensor_tensor(m.a[:, :, :], m.a[:, :, :], en[:, :, :], ALU.mult))
            step(dve.tensor_copy(m.chunk_decay[:, :, :], b[:, :, RC - 1::RC]))


def retention(k, e):
    nc = k.nc
    s = Names(**{n: k.sem("rt_" + n) for n in (
        "turned", "rotated", "scored", "p_ready", "o_done", "o_kept", "mean_done", "centred", "squared", "var_done",
        "inverted", "rooted", "dve_chain")})
    rc = lambda n: e.consts[:, RET_AT[n][0]:RET_AT[n][1]]
    with ExitStack() as own:
        wts = k.sb("rt_wts", [P, 4, T + P], own)
        ot, tmp = (k.sb("rt_" + n, [P, 4, T], own) for n in ("ot", "tmp"))
        block = own.enter_context(nc.Block())
        flat = lambda a: a.rearrange("p m t -> p (m t)")

        @block.sync
        def _(sp):
            k.load_chunks(sp, O_OUT + SLOTS)

        @block.tensor
        def _(pe):
            for i, src in enumerate((e.ret_q, e.ret_k)):
                for j in range(2):
                    ins = pe.matmul(k.bank(2 * i + j), rc("rot"), src[:, 2 * j:2 * j + 2, :], start=True, stop=True)
                ins.then_inc(s.turned, 1)
            pe.wait_ge(s.rotated, 2)
            for hd in range(4):
                b = k.bank(4 + hd)
                pe.matmul(b[:, 0:T], e.ret_k[:, hd, 0:P], e.ret_q[:, hd, :], start=True, stop=True)
                pe.matmul(b[:, T:T + P], e.ret_k[:, hd, P:T], e.ret_q[:, hd, P:T], start=True, stop=True).then_inc(s.scored, 1)
            for hd in range(4):
                pe.wait_ge(s.p_ready, hd + 1)
                cols = slice(hd * P, (hd + 1) * P)
                b = k.bank(hd)
                pe.matmul(b[:, 0:T], e.ret_v[:, 0, cols], wts[:, hd, 0:T], start=True, stop=False, skip_group_check=True)
                pe.matmul(b[:, P:T], e.ret_v[:, 1, cols], wts[:, hd, T:T + P], start=False, stop=True,
                          skip_group_check=True).then_inc(s.o_done, 1)
            pe.wait_ge(s.o_kept, 4)
            for i in range(2):
                ins = pe.matmul(k.bank(4 + i), k.c("mean"), ot[:, 2 * i:2 * i + 2, :], start=True, stop=True)
            ins.then_inc(s.mean_done, 1)
            pe.wait_ge(s.squared, 1)
            for i in range(2):
                ins = pe.matmul(k.bank(6 + i), k.c("mean"), tmp[:, 2 * i:2 * i + 2, :], start=True, stop=True)
            ins.then_inc(s.var_done, 1)

        @block.scalar
        def _(act):
            for hd in range(4):
                act.wait_ge(s.o_done, hd + 1)
                act.copy(ot[:, hd, :], k.bank(hd)[:, 0:T]).then_inc(s.o_kept, 1)
            act.wait_ge(s.centred, 1)
            act.activation(tmp[:, :, :], ot[:, :, :], ACT.Square).then_inc(s.squared, 1)
            act.wait_ge(s.inverted, 1)
            act.activation(tmp[:, :, :], tmp[:, :, :], ACT.Sqrt).then_inc(s.rooted, 1)

        @block.vector
        def _(dve):
            step = counted(dve, s.dve_chain)
            for i, x in enumerate((e.ret_q, e.ret_k)):
                dve.wait_ge(s.turned, i + 1)
                step(dve.tensor_tensor(tmp[:, :, :], k.bank(2 * i, 2).rearrange("p (m t) -> p m t", m=4), bc(rc("sin"), 1, 4), ALU.mult))
                step(dve.tensor_tensor(x[:, :, :], x[:, :, :], bc(rc("cos"), 1, 4), ALU.mult))
                dve.tensor_tensor(x[:, :, :], x[:, :, :], tmp[:, :, :], ALU.add).then_inc(s.rotated, 1)
                dve.wait_ge(s.rotated, i + 1)
            decay = rc("decay").rearrange("p (h t) -> p h t", h=4)
            for hd in range(4):
                dve.wait_ge(s.scored, hd + 1)
                step(dve.tensor_tensor(wts[:, hd, 0:T], k.bank(4 + hd)[:, 0:T], decay[:, hd, :], ALU.mult))
                dve.tensor_tensor(wts[:, hd, T:T + P], k.bank(4 + hd)[:, T:T + P], decay[:, hd, 0:P], ALU.mult).then_inc(s.p_ready, 1)
            dve.wait_ge(s.mean_done, 1)
            dve.wait_ge(s.o_kept, 4)
            dve.tensor_tensor(flat(ot[:, :, :]), flat(ot[:, :, :]), k.bank(4, 2), ALU.subtract).then_inc(s.centred, 1)
            dve.wait_ge(s.var_done, 1)
            step(dve.tensor_scalar(flat(tmp[:, :, :]), k.bank(6, 2), EPS, None, ALU.add))
            dve.reciprocal(tmp[:, :, :], tmp[:, :, :]).then_inc(s.inverted, 1)
            dve.wait_ge(s.rooted, 1)
            step(dve.tensor_tensor(tmp[:, :, :], tmp[:, :, :], ot[:, :, :], ALU.mult))
            for hd in range(4):
                step(dve.scalar_tensor_tensor(out=k.h[:, hd, :], in0=tmp[:, hd, :], scalar=k.p("ret_norm", hd),
                                              in1=e.ret_g[:, hd, :], op0=ALU.mult, op1=ALU.mult))


def rwkv(k, m):
    nc, g = k.nc, k.g
    s = Names(**{n: k.sem("rw_" + n) for n in (
        "loaded", "gram_done", "gram_kept", "padded", "turned", "v_kept", "rows_kept", "w1_done", "w1_kept", "off_ready",
        "u_done", "u_kept", "dx_done", "x_ready", "xa_done", "xa_kept", "q_done", "q_kept", "m_kept", "state_done",
        "state_ready", "y_done", "y_kept", "dve_chain", "act_chain", "pool_chain", "mean_done", "centred", "squared",
        "var_done", "inverted", "rooted")})
    HD = 8
    with ExitStack() as own:
        sb = lambda n, shape: k.sb("rw_" + n, shape, own)
        consts = sb("consts", [P, RW_N])
        gram = sb("gram", [P, HD, 4, P])
        ar = sb("ar", [P, HD, 2, P])
        vp = sb("vp", [P, HD, P])
        aw = sb("aw", [P, HD, 2, 64])
        bk = sb("bk", [P, 2, 2, CH])
        x, xt = sb("x", [P, HD, P]), sb("xt", [P, HD, P])
        u, off = sb("u", [P, HD, P]), sb("off", [P, HD, P])
        xa, xw, mt = u, off, x
        q = sb("q", [P, 4, P])
        grown = sb("grown", [P, 4, P])
        state = sb("state", [P, 3, 4, P])
        wc = lambda n: consts[:, RW_AT[n][0]:RW_AT[n][1]]
        block = own.enter_context(nc.Block())
        L = len(LEVELS)
        pair_cols = lambda t, p: t[:, 2 * p:2 * p + 2, :].rearrange("p h c -> p (h c)")[:, 0:T].rearrange(
            "p (a c) -> p a c", c=64)[:, 0::3, :]

        @block.sync
        def _(sp):
            sp.dma_start(consts[:, :], g.rw_consts).then_inc(s.loaded, 16)
            k.load_chunks(sp, O_OUT + SLOTS)

        @block.gpsimd
        def _(pool):
            pool.memset(ar[:, :, :, :], 0.0).then_inc(s.padded, 1)
            pool.memset(state[:, 0, :, :], 0.0).then_inc(s.state_ready, 1)
            pool.wait_ge(s.loaded, 16)
            pool.wait_ge(s.padded, 1)
            pool.wait_ge(s.state_ready, 1)
            for a in range(TH):
                half = slice(a * P, (a + 1) * P)
                if a:
                    pool.wait_ge(s.gram_done, HD)
                for hd in range(2):
                    rows = slice(64 * hd, 64 * hd + 64)
                    for i, src in enumerate((m.kk, m.r)):
                        pool.tensor_copy(ar[rows, hd::2, i, :], src[rows, :, half]).then_inc(s.padded, 1)
                        pool.wait_ge(s.padded, 2 + 4 * a + 2 * hd + i)
                for lv in range(L):
                    for grp in range(2):
                        hs = slice(4 * grp, 4 * grp + 4)
                        if lv == 0:
                            pool.wait_ge(s.gram_kept, HD * a + 4 * grp + 4)
                            if a:
                                pool.wait_ge(s.y_done, 1)
                        else:
                            pool.wait_ge(s.u_done, 2 * (L * a + lv - 1) + grp + 1)
                            if lv == 1:
                                pool.wait_ge(s.x_ready, 2 * L * a + grp + 1)
                        pool.tensor_tensor(off[:, hs, :], gram[:, hs, 0, :], bc(wc("levels")[:, lv * P:(lv + 1) * P], 1, 4),
                                           ALU.mult).then_inc(s.off_ready, 1)
                pool.wait_ge(s.off_ready, 2 * L * (a + 1))

        @block.tensor
        def _(pe):
            for a in range(TH):
                half = slice(a * P, (a + 1) * P)
                pe.wait_ge(s.padded, 5 + 4 * a)
                if a:
                    pe.wait_ge(s.y_kept, 1)
                    pe.wait_ge(s.state_ready, 3)
                for h in range(HD):
                    pe.matmul(k.bank(h)[:, 0:T], m.a[:, h // 2, half], ar[:, h, :, :], start=True, stop=True)
                    pe.matmul(k.bank(h)[:, T:2 * T], m.kh[:, h // 2, half], ar[:, h, :, :], start=True, stop=True).then_inc(s.gram_done, 1)
                pe.wait_ge(s.gram_kept, HD * (a + 1))
                for i, src in enumerate((m.v, m.kk, m.a, m.kh)):
                    for p in range(4):
                        ins = pe.transpose(k.bank(i)[:, p * P:(p + 1) * P], src[:, p, half], k.c("ident"))
                    ins.then_inc(s.turned, 1)
                pe.wait_ge(s.v_kept, a + 1)
                for h in range(HD):
                    ins = pe.matmul(k.bank(4)[:, h * 64:(h + 1) * 64], gram[:, h, 2, :], vp[:, h, (h % 2) * 64:(h % 2) * 64 + 64],
                                    start=True, stop=True)
                ins.then_inc(s.w1_done, 1)
                for lv in range(L):
                    for grp in range(2):
                        pe.wait_ge(s.off_ready, 2 * (L * a + lv) + grp + 1)
                        if lv or a:
                            pe.wait_ge(s.x_ready, 2 * (L * a + lv - 1) + grp + 1)
                        if a == 1 and lv == 0:
                            pe.wait_ge(s.y_done, 1)
                        for h in range(4 * grp, 4 * grp + 4):
                            ins = pe.matmul(k.bank(6 + grp)[:, (h % 4) * P:(h % 4 + 1) * P], off[:, h, :],
                                            x[:, h, :] if lv else k.c("ident"), start=True, stop=True)
                        ins.then_inc(s.u_done, 1)
                    if lv == 0:
                        continue
                    for grp in range(2):
                        pe.wait_ge(s.u_kept, 2 * ((L - 1) * a + lv - 1) + grp + 1)
                        if lv == 1:
                            pe.wait_ge(s.rows_kept, a + 1)
                        for h in range(4 * grp, 4 * grp + 4):
                            cols = slice((h % 4) * P, (h % 4 + 1) * P)
                            if lv < L - 1:
                                pe.matmul(k.bank(2 * grp)[:, cols], xt[:, h, :], u[:, h, :], start=True, stop=True)
                            ins = pe.matmul(k.bank(2 * grp + 1)[:, cols], u[:, h, :], xt[:, h, :], start=True, stop=True)
                        ins.then_inc(s.dx_done, 1)
                pe.wait_ge(s.w1_kept, a + 1)
                pe.wait_ge(s.x_ready, 2 * L * (a + 1))
                for h in range(HD):
                    ins = pe.matmul(k.bank(4 + h // 4)[:, (h % 4) * P:(h % 4 + 1) * P], xt[:, h, :], aw[:, h, :, :], start=True, stop=True)
                ins.then_inc(s.xa_done, 1)
                pe.wait_ge(s.xa_kept, a + 1)
                for p in range(4):
                    for h in (2 * p, 2 * p + 1):
                        ins = pe.matmul(k.bank(6)[:, p * P:(p + 1) * P], xa[:, h, :], gram[:, h, 1, :], start=h % 2 == 0, stop=h % 2 == 1)
                for p in range(4):
                    for c in range(2):
                        for h in (2 * p, 2 * p + 1):
                            ins = pe.matmul(k.bank(c)[:, p * P:(p + 1) * P], xa[:, h, :], bk[:, 0, c, p * P:(p + 1) * P],
                                            start=h % 2 == 0, stop=h % 2 == 1)
                ins.then_inc(s.q_done, 1)
                pe.wait_ge(s.m_kept, a + 1)
                for n in range(2 * a, min(2 * a + 2, RN - 1)):
                    c = n - 2 * a
                    pe.wait_ge(s.state_ready, n + 1)
                    for p in range(4):
                        out = k.bank(2 + c)[:, p * P:(p + 1) * P]
                        cols = slice(p * P, (p + 1) * P)
                        pe.matmul(out, bk[:, 0, c, cols], pair_cols(xw, p), start=True, stop=False)
                        pe.matmul(out, bk[:, 1, c, cols], pair_cols(vp, p), start=False, stop=False)
                        ins = pe.matmul(out, mt[:, 4 * c + p, :], state[:, n % 3, p, :], start=False, stop=True)
                    ins.then_inc(s.state_done, 1)
                pe.wait_ge(s.q_kept, a + 1)
                pe.wait_ge(s.state_ready, 2 * a + 2)
                for p in range(4):
                    out = k.bank(7)[:, p * P:(p + 1) * P]
                    for h in (2 * p, 2 * p + 1):
                        pe.matmul(out, xw[:, h, :], gram[:, h, 1, :], start=h % 2 == 0, stop=False, skip_group_check=True)
                        pe.matmul(out, vp[:, h, :], gram[:, h, 3, :], start=False, stop=False, skip_group_check=True)
                    for c in range(2):
                        ins = pe.matmul(out[:, c * 64:(c + 1) * 64], state[:, (2 * a + c) % 3, p, :], q[:, p, c * 64:(c + 1) * 64],
                                        start=False, stop=True, skip_group_check=True)
                ins.then_inc(s.y_done, 1)
            pe.wait_ge(s.y_kept, 2)
            for i in range(2):
                ins = pe.matmul(k.bank(i), k.c("head_mean"), k.h[:, 4 + 2 * i:6 + 2 * i, :], start=True, stop=True)
            ins.then_inc(s.mean_done, 1)
            pe.wait_ge(s.squared, 1)
            for i in range(2):
                ins = pe.matmul(k.bank(2 + i), k.c("head_mean"), gram[:, i, :, :], start=True, stop=True)
            ins.then_inc(s.var_done, 1)

        @block.scalar
        def _(act):
            astep = counted(act, s.act_chain)
            for a in range(TH):
                act.wait_ge(s.turned, 4 * a + 4)
                astep(act.copy(aw[:, :, 0, :], k.bank(1).rearrange("p (h c) -> p h c", c=64)))
                for i in range(2):
                    for c in range(2):
                        ins = act.activation(bk[:, i, c, :], k.bank(2 + i), ACT.Copy, scale=k.c("parity")[:, c:c + 1])
                        if (i, c) != (1, 1):
                            astep(ins)
                ins.then_inc(s.rows_kept, 1)
                act.wait_ge(s.w1_done, a + 1)
                act.copy(aw[:, :, 1, :], k.bank(4).rearrange("p (h c) -> p h c", c=64)).then_inc(s.w1_kept, 1)
                for lv in range(1, L):
                    for grp in range(2):
                        act.wait_ge(s.u_done, 2 * (L * a + lv) + grp + 1)
                        act.copy(u[:, 4 * grp:4 * grp + 4, :], k.bank(6 + grp).rearrange("p (h c) -> p h c", c=P)).then_inc(s.u_kept, 1)
                act.wait_ge(s.y_done, a + 1)
                act.copy(k.h[:, 4:8, a * P:(a + 1) * P], k.bank(7).rearrange("p (h c) -> p h c", c=P)).then_inc(s.y_kept, 1)
            act.wait_ge(s.centred, 1)
            act.activation(gram[:, :, :, :].rearrange("p a b c -> p (a b c)")[:, 0:4 * T], k.h[:, 4:8, :].rearrange("p a t -> p (a t)"), ACT.Square).then_inc(s.squared, 1)
            act.wait_ge(s.inverted, 1)
            act.activation(gram[:, 0:2, :, :], gram[:, 0:2, :, :], ACT.Sqrt).then_inc(s.rooted, 1)

        @block.vector
        def _(dve):
            step = counted(dve, s.dve_chain)
            dve.wait_ge(s.loaded, 16)
            masks = consts[:, RW_AT["strict"][0]:RW_AT["upto"][1]].rearrange("p (b c) -> p b c", b=2)
            cols = wc("head_cols").rearrange("p (h c) -> p h c", h=2)
            for a in range(TH):
                for h in range(HD):
                    dve.wait_ge(s.gram_done, HD * a + h + 1)
                    dve.tensor_tensor(gram[:, h, :, :].rearrange("p (x y) c -> p x y c", x=2),
                                      k.bank(h).rearrange("p (x y c) -> p x y c", x=2, y=2), bc(masks, 1, 2), ALU.mult).then_inc(s.gram_kept, 1)
                dve.wait_ge(s.turned, 4 * a + 1)
                dve.tensor_tensor(vp[:, :, :].rearrange("p (q h) c -> p q h c", h=2),
                                  bc(k.bank(0).rearrange("p (q c) -> p q c", c=P), 2, 2), bc(cols, 1, 4), ALU.mult).then_inc(s.v_kept, 1)
                for lv in range(L):
                    for grp in range(2):
                        hs = slice(4 * grp, 4 * grp + 4)
                        n = 2 * (L * a + lv) + grp + 1
                        if lv == 0:
                            ident = bc(k.c("ident"), 1, 4)
                            dve.wait_ge(s.off_ready, n)
                            step(dve.tensor_tensor(xt[:, hs, :], off[:, hs, :], ident, ALU.add))
                            dve.wait_ge(s.u_done, n)
                            dve.tensor_tensor(x[:, hs, :], k.bank(6 + grp).rearrange("p (h c) -> p h c", c=P), ident, ALU.add).then_inc(s.x_ready, 1)
                            continue
                        dve.wait_ge(s.dx_done, 2 * ((L - 1) * a + lv - 1) + grp + 1)
                        if lv < L - 1:
                            step(dve.tensor_tensor(x[:, hs, :], x[:, hs, :], k.bank(2 * grp).rearrange("p (h c) -> p h c", c=P), ALU.add))
                        dve.tensor_tensor(xt[:, hs, :], xt[:, hs, :], k.bank(2 * grp + 1).rearrange("p (h c) -> p h c", c=P), ALU.add).then_inc(s.x_ready, 1)
                dve.wait_ge(s.xa_done, a + 1)
                for hd in range(2):
                    for i, dst in enumerate((xa, xw)):
                        src = k.bank(4, 2).rearrange("p (q h i c) -> p q h i c", q=4, h=2, i=2)[:, :, hd, i, :]
                        ins = dve.tensor_tensor(dst[:, hd::2, :].rearrange("p q (r c) -> p q r c", r=2), bc(src, 2, 2),
                                                bc(cols[:, hd, :].rearrange("p (r c) -> p r c", r=2), 1, 4), ALU.mult)
                        if (hd, i) != (1, 1):
                            step(ins)
                ins.then_inc(s.xa_kept, 1)
                dve.wait_ge(s.q_done, a + 1)
                dve.tensor_tensor(mt[:, :, :].rearrange("p n c -> p (n c)").rearrange("p (n c) -> p n c", c=P),
                                  k.bank(0, 2).rearrange("p (n c) -> p n c", c=P), bc(k.c("head_ones"), 1, 8), ALU.mult).then_inc(s.m_kept, 1)
                dve.tensor_tensor(q[:, :, :], k.bank(6).rearrange("p (n c) -> p n c", c=P), m.r[:, :, a * P:(a + 1) * P], ALU.add).then_inc(s.q_kept, 1)
                for n in range(2 * a, min(2 * a + 2, RN - 1)):
                    c = n - 2 * a
                    dve.wait_ge(s.state_done, n + 1)
                    if n == 2:
                        dve.wait_ge(s.y_done, 1)
                    step(dve.tensor_tensor(grown[:, :, :], k.bank(2 + c).rearrange("p (n c) -> p n c", c=P), state[:, n % 3, :, :], ALU.add))
                    step(dve.tensor_tensor(grown[:, :, :], grown[:, :, :], m.chunk_decay[:, :, n:n + 1].broadcast_to([P, 4, P]), ALU.mult))
                    dve.tensor_tensor(state[:, (n + 1) % 3, :, :], grown[:, :, :], bc(k.c("head_ones"), 1, 4), ALU.mult).then_inc(s.state_ready, 1)
            y = k.h[:, 4:8, :]
            flat = lambda t: t.rearrange("p m t -> p (m t)")
            tmp = gram[:, 0:2, :, :].rearrange("p a b c -> p (a b c)").rearrange("p (m t) -> p m t", m=4)
            dve.wait_ge(s.mean_done, 1)
            dve.tensor_tensor(flat(y), flat(y), k.bank(0, 2), ALU.subtract).then_inc(s.centred, 1)
            dve.wait_ge(s.centred, 1)
            dve.wait_ge(s.var_done, 1)
            step(dve.tensor_scalar(flat(tmp), k.bank(2, 2), RW_LN_EPS, None, ALU.add))
            dve.reciprocal(flat(tmp), flat(tmp)).then_inc(s.inverted, 1)
            dve.wait_ge(s.rooted, 1)
            step(dve.tensor_tensor(y, y, tmp, ALU.mult))
            for t in range(4):
                step(dve.tensor_scalar(y[:, t, :], y[:, t, :], k.p("ln_g", t), k.p("ln_b", t), ALU.mult, ALU.add))
            step(dve.tensor_tensor(y, y, m.bonus[:, :, :], ALU.add))
            step(dve.tensor_tensor(y, y, m.g[:, :, :], ALU.mult))


def route(k, x):
    nc, g = k.nc, k.g
    s = Names(**{n: k.sem("ro_" + n) for n in (
        "loaded", "logits_done", "rows_done", "rows_kept", "chosen", "places_done", "shifted", "exp_ready", "dve_chain")})
    with ExitStack() as own:
        sb = lambda n, shape: k.sb("ro_" + n, shape, own)
        router = sb("router", [P, KT, E])
        lg, ez, w = sb("logits", [P, TH, E]), sb("exp", [P, TH, E]), sb("weights", [P, TH, E])
        above, same = sb("above", [P, E, E]), sb("same", [P, E, E])
        rank, top, total = sb("rank", [P, TH, E]), sb("top", [P, TH]), sb("total", [P, TH])
        most = sb("most", [P, 1])
        block = own.enter_context(nc.Block())

        @block.sync
        def _(sp):
            sp.dma_start(router[:, :, :], g.o_moe_router[0].rearrange("(k p) e -> p k e", p=P)).then_inc(s.loaded, 16)

        @block.tensor
        def _(pe):
            pe.wait_ge(s.loaded, 16)
            for a in range(TH):
                for kt in range(KT):
                    ins = pe.matmul(k.bank(4)[:, a * E:(a + 1) * E], k.h[:, kt, a * P:(a + 1) * P], router[:, kt, :],
                                    start=kt == 0, stop=kt == KT - 1)
            ins.then_inc(s.logits_done, 1)
            for a in range(TH):
                for kt in range(KT):
                    ins = pe.transpose(k.bank(2 * a + kt // 4)[:, (kt % 4) * P:(kt % 4 + 1) * P], k.h[:, kt, a * P:(a + 1) * P], k.c("ident"))
                ins.then_inc(s.rows_done, 1)
            pe.wait_ge(s.chosen, 1)
            pe.matmul(k.bank(5)[:, 0:E], k.c("before"), x.chosen[:, 0, :], start=True, stop=True)
            pe.matmul(k.bank(5)[:, E:2 * E], k.c("ones"), x.chosen[:, 0, :], start=True, stop=False)
            pe.matmul(k.bank(5)[:, E:2 * E], k.c("before"), x.chosen[:, 1, :], start=False, stop=True)
            for a in range(TH):
                ins = pe.matmul(k.bank(5)[:, 2 * E:3 * E], k.c("ones"), x.chosen[:, a, :], start=a == 0, stop=a == 1)
            ins.then_inc(s.places_done, 1)

        @block.scalar
        def _(act):
            for a in range(TH):
                act.wait_ge(s.rows_done, a + 1)
                act.copy(x.rows[:, a, :], k.bank(2 * a, 2)).then_inc(s.rows_kept, 1)
            act.wait_ge(s.shifted, 1)
            act.activation(ez[:, :, :], ez[:, :, :], ACT.Exp).then_inc(s.exp_ready, 1)

        @block.vector
        def _(dve):
            step = counted(dve, s.dve_chain)
            dve.wait_ge(s.logits_done, 1)
            step(dve.tensor_copy(lg[:, :, :], k.bank(4)[:, 0:TH * E].rearrange("p (a e) -> p a e", a=TH)))
            step(dve.tensor_reduce(top[:, :], lg[:, :, :], AX.X, ALU.max))
            dve.tensor_tensor(ez[:, :, :], lg[:, :, :], bc(top[:, :], 2, E), ALU.subtract).then_inc(s.shifted, 1)
            for a in range(TH):
                mine, other = bc(lg[:, a, :], 2, E), bc(lg[:, a, :], 1, E)
                step(dve.tensor_tensor(above[:, :, :], other, mine, ALU.is_gt))
                step(dve.tensor_tensor(same[:, :, :], other, mine, ALU.is_equal))
                step(dve.tensor_tensor(same[:, :, :], same[:, :, :], k.c("earlier").rearrange("p (e f) -> p e f", e=E), ALU.mult))
                step(dve.tensor_tensor(above[:, :, :], above[:, :, :], same[:, :, :], ALU.add))
                step(dve.tensor_reduce(rank[:, a, :], above[:, :, :], AX.X, ALU.add))
            dve.tensor_scalar(x.chosen[:, :, :], rank[:, :, :], float(TOP_K), None, ALU.is_lt).then_inc(s.chosen, 1)
            dve.wait_ge(s.chosen, 1)
            dve.wait_ge(s.exp_ready, 1)
            step(dve.tensor_tensor(w[:, :, :], ez[:, :, :], x.chosen[:, :, :], ALU.mult))
            step(dve.tensor_reduce(total[:, :], w[:, :, :], AX.X, ALU.add))
            step(dve.reciprocal(total[:, :], total[:, :]))
            step(dve.tensor_tensor(x.gate[:, :, :], w[:, :, :], bc(total[:, :], 2, E), ALU.mult))
            dve.wait_ge(s.places_done, 1)
            step(dve.tensor_copy(x.place[:, :, :], k.bank(5)[:, 0:2 * E].rearrange("p (a e) -> p a e", a=TH)))
            step(dve.tensor_reduce(most[:, :], k.bank(5)[:, 2 * E:3 * E], AX.X, ALU.max))
            step(dve.tensor_copy(x.most[:, :], most[:, :]))
            dve.wait_ge(s.rows_kept, TH)


TOP_K = 2
FREE = 1
X_RING = 7
X_SPLIT = 6
HALVES = 2 * len(FFN_ORDER)
PIECES = 2 * HALVES


def expert_half(k, e, i):
    g = k.g
    kind, c = FFN_ORDER[i // 2]
    w = {"gate": g.o_moe_w_gate, "up": g.o_moe_w_up, "down": g.o_moe_w_down}[kind][0]
    if kind == "down":
        r0 = c * CH + (i % 2) * CH // 2
        return w[bass.ds(e, 1), r0:r0 + CH // 2, :].rearrange("o (k p) c -> p (o k) c", p=P)
    r0 = (i % 2) * D // 2
    return w[bass.ds(e, 1), r0:r0 + D // 2, c * CH:(c + 1) * CH].rearrange("o (k p) c -> p (o k) c", p=P)


def expert_slot(k, i):
    j = i % X_RING
    if j < 2 * SLOTS:
        return k.ring[:, j // 2, (j % 2) * 2 * PIECE:(j % 2 + 1) * 2 * PIECE]
    return k.ring_more[:, j - 2 * SLOTS, :]


def load_expert_half(k, sp, e, i, before):
    if before + i >= X_RING:
        sp.wait_ge(k.lo_ready, 2 * (before + i - X_RING + 1) + PIECES * e)
    else:
        if i // 2 < SLOTS:
            sp.wait_ge(k.chunk_used, DENSE - (DENSE - 1 - i // 2) % SLOTS)
    w = expert_slot(k, i).rearrange("p (k c) -> p k c", k=2 if FFN_ORDER[i // 2][0] == "down" else 4)
    sp.dma_start(w, expert_half(k, e, i)).then_inc(k.half_filled[i % X_RING], 16)


def last_piece(kind, c):
    return 4 * FFN_ORDER.index((kind, c)) + 3


def turn_after(c):
    return last_piece("gate", c + 1) - 2 if c < FC - 1 else last_piece("up", c)


def guarded(k, x, p, engine, program):
    if p == 0:
        return program()
    most = engine.value_load(x.most[0:1, 0:1], min_val=0, max_val=T)
    with engine.If(most > CAP * p):
        program()


def expert_tables(k, x, s, p):
    with ExitStack() as own:
        weighted = k.sb(f"expert_weighted{p}", [P, E, TH, CAP], own)
        block = own.enter_context(k.nc.Block())

        @block.vector
        def _(dve):
            def program():
                if p == 0:
                    dve.memset(x.hot[:, E, :, :], 0.0).then_inc(s.zeroed, 1)
                    dve.wait_ge(s.zeroed, 1)
                dve.tensor_scalar(x.here[:, :, :], x.place[:, :, :], -float(CAP * p), None, ALU.add).then_inc(s.hot, 1)
                dve.wait_ge(s.hot, (2 * E + 2) * p + 1)
                for e in range(E):
                    for a in range(TH):
                        dve.tensor_scalar(x.hot[:, e, a, :], k.c("slots"), x.here[:, a, e:e + 1], x.chosen[:, a, e:e + 1],
                                          ALU.is_equal, ALU.mult).then_inc(s.hot, 1)
                dve.wait_ge(s.hot, (2 * E + 2) * p + 2 * E + 1)
                for a in range(TH):
                    ins = dve.tensor_tensor(weighted[:, :, a, :], x.hot[:, 0:E, a, :], bc(x.gate[:, a, :], 2, CAP), ALU.mult)
                ins.then_inc(s.hot, 1)
                for b in range(4):
                    dve.wait_ge(s.scatter_turned, 4 * p + b + 1)
                    dve.tensor_copy(x.scatter[:, 2 * b:2 * b + 2, :], k.bank(b)[0:CAP, :].rearrange("p (e t) -> p e t", e=2)).then_inc(s.scatter_kept, 1)
                dve.wait_ge(s.scatter_kept, 4 * (p + 1))
            guarded(k, x, p, dve, program)

        @block.tensor
        def _(pe):
            def program():
                pe.wait_ge(s.hot, (2 * E + 2) * (p + 1))
                for b in range(4):
                    for i in range(4):
                        ins = pe.transpose(k.bank(b)[0:CAP, i * P:(i + 1) * P], weighted[:, 2 * b + i // 2, i % 2, :], k.c("ident"))
                    ins.then_inc(s.scatter_turned, 1)
            guarded(k, x, p, pe, program)


def expert_pass(k, x, s, p):
    with ExitStack() as own:
        tile = lambda n, cols, dt: k.sb(f"expert_{n}{p}", [P, *cols], own, dt)
        w_hi, w_lo = tile("w_hi", [X_SPLIT, PIECE], F32R), tile("w_lo", [X_SPLIT, PIECE], F32R)
        tok_hi, tok_lo = tile("tok_hi", [KT, CAP], F32R), tile("tok_lo", [KT, CAP], F32R)
        hid_hi, hid_lo = tile("hid_hi", [MF, CAP], F32R), tile("hid_lo", [MF, CAP], F32R)
        hid, gated = tile("hid", [MF * CAP], F32), tile("gated", [MF * CAP], F32)
        y = tile("y", [D], F32)
        hot_now, scatter_now = tile("hot_now", [TH, CAP], F32), tile("scatter_now", [T], F32)
        block = own.enter_context(k.nc.Block())
        x0 = E * p
        flat = lambda a: a.rearrange("p a b -> p (a b)")
        run = lambda engine, program: guarded(k, x, p, engine, program)

        @block.sync
        def _(sp):
            def program():
                if p:
                    for i in range(X_RING):
                        load_expert_half(k, sp, 0, i, HALVES * x0)
                with sp.Fori(0, E - 1) as e:
                    for i in range(X_RING, HALVES):
                        load_expert_half(k, sp, e, i, HALVES * x0)
                    for i in range(X_RING):
                        sp.wait_ge(k.lo_ready, 2 * (HALVES * (x0 + 1) + i - X_RING + 1) + PIECES * e)
                        w = expert_slot(k, i).rearrange("p (k c) -> p k c", k=2 if FFN_ORDER[i // 2][0] == "down" else 4)
                        sp.dma_start(w, expert_half(k, e + 1, i)).then_inc(k.half_filled[i], 16)
                for i in range(X_RING, HALVES):
                    load_expert_half(k, sp, E - 1, i, HALVES * x0)
            run(sp, program)

        @block.scalar
        def _(act):
            def keep_tokens(n, half):
                act.wait_ge(s.gathered, 2 * n - 1 + half)
                act.copy(flat(tok_hi[:, 4 * half:4 * half + 4, :]), k.bank(0)).then_inc(s.tokens_hi, 1)

            def keep_hidden(n):
                act.wait_ge(s.turned, n)
                act.copy(flat(hid_hi[:, :, :]), k.bank(1)).then_inc(s.hid_hi, 1)

            def program():
                if p == 0:
                    act.sem_inc(s.gate_kept, FREE)
                    act.sem_inc(s.y_kept, FREE)
                for half in range(2):
                    keep_tokens((E + 1) * p + 1, half)
                with act.Fori(0, E) as e:
                    for j in range(PIECES + 1):
                        if j == PIECES:
                            act.wait_ge(s.piece_used, X_SPLIT + PIECES * (x0 + 1) + PIECES * e)
                            act.wait_ge(s.out_done, FREE + x0 + e)
                            act.copy(y[:, :], k.bank(2, 2)).then_inc(s.y_kept, 1)
                            continue
                        for c in range(FC):
                            if j == last_piece("gate", c) + X_SPLIT:
                                act.wait_ge(s.piece_used, X_SPLIT + PIECES * x0 + last_piece("gate", c) + 1 + PIECES * e)
                                act.wait_ge(s.multiplied, FREE + FC * x0 + c + FC * e)
                                act.activation(gated[:, :], k.bank(0), ACT.Silu).then_inc(s.gate_kept, 1)
                            if c < FC - 1 and j == turn_after(c) + X_SPLIT:
                                if c == 0:
                                    act.wait_ge(s.piece_used, X_SPLIT + PIECES * x0 + PIECES * e)
                                keep_hidden(FC * x0 + c + 1 + FC * e)
                        if j == PIECES - 1:
                            keep_tokens((E + 1) * p + 2 + e, 0)
                            keep_hidden(FC * x0 + FC + FC * e)
                            keep_tokens((E + 1) * p + 2 + e, 1)
                        if j % 2 == 0:
                            act.wait_ge(k.half_filled[j // 2 % X_RING], 16 * (HALVES // X_RING * x0 + j // 2 // X_RING + 1) + 16 * (HALVES // X_RING) * e)
                        act.wait_ge(s.piece_used, PIECES * x0 + j + 1 + PIECES * e)
                        act.copy(w_hi[:, j % X_SPLIT, :], expert_slot(k, j // 2)[:, j % 2 * PIECE:(j % 2 + 1) * PIECE]).then_inc(s.hi_ready, 1)
            run(act, program)

        @block.vector
        def _(dve):
            def rest_of_tokens(n, half):
                dve.wait_ge(s.tokens_hi, 2 * n - 1 + half)
                dve.tensor_tensor(flat(tok_lo[:, 4 * half:4 * half + 4, :]), k.bank(0), flat(tok_hi[:, 4 * half:4 * half + 4, :]).bitcast(F32),
                                  ALU.subtract).then_inc(s.tokens_ready, 1)

            def rest_of_hidden(n):
                dve.wait_ge(s.hid_hi, n)
                dve.tensor_tensor(flat(hid_lo[:, :, :]), k.bank(1), flat(hid_hi[:, :, :]).bitcast(F32), ALU.subtract).then_inc(s.hid_ready, 1)

            def program():
                if p == 0:
                    dve.sem_inc(s.multiplied, FREE)
                    dve.sem_inc(s.hid_ready, FREE)
                for half in range(2):
                    rest_of_tokens((E + 1) * p + 1, half)
                with dve.Fori(0, E) as e:
                    for j in range(PIECES):
                        for c in range(FC):
                            if j == min(last_piece("up", c) + X_SPLIT, PIECES - 1):
                                dve.wait_ge(s.piece_used, X_SPLIT + PIECES * x0 + last_piece("up", c) + 1 + PIECES * e)
                                dve.wait_ge(s.gate_kept, FREE + FC * x0 + c + 1 + FC * e)
                                dve.tensor_tensor(hid[:, :], gated[:, :], k.bank(1), ALU.mult).then_inc(s.multiplied, 1)
                            if c < FC - 1 and j == turn_after(c) + X_SPLIT:
                                rest_of_hidden(FC * x0 + c + 1 + FC * e)
                        if j == PIECES - 1:
                            rest_of_tokens((E + 1) * p + 2 + e, 0)
                            rest_of_hidden(FC * x0 + FC + FC * e)
                            rest_of_tokens((E + 1) * p + 2 + e, 1)
                        dve.wait_ge(s.hi_ready, PIECES * x0 + j + 1 + PIECES * e)
                        dve.tensor_tensor(w_lo[:, j % X_SPLIT, :], expert_slot(k, j // 2)[:, j % 2 * PIECE:(j % 2 + 1) * PIECE],
                                          w_hi[:, j % X_SPLIT, :].bitcast(F32), ALU.subtract).then_inc(k.lo_ready, 1)
                dve.wait_ge(s.out_done, FREE + E * (p + 1))
                for i in range(2):
                    r = flat(k.res[:, 4 * i:4 * i + 4, :])
                    dve.tensor_tensor(r, r, k.bank(4 + 2 * i, 2), ALU.add).then_inc(s.added, 1)
                dve.wait_ge(s.added, 2 * (p + 1))
            run(dve, program)

        @block.gpsimd
        def _(pool):
            def program():
                pool.tensor_copy(flat(hot_now[:, :, :]), flat(x.hot[:, 0, :, :])).then_inc(s.hot_ready, 1)
                with pool.Fori(0, E) as e:
                    pool.wait_ge(s.gathered, 2 * (E + 1) * p + 2 + 2 * e)
                    pool.tensor_copy(hot_now[:, :, :], x.hot[:, bass.ds(e + 1, 1), :, :].rearrange("p o a c -> p (o a) c")).then_inc(s.hot_ready, 1)
                    pool.wait_ge(s.out_done, FREE + x0 + e)
                    pool.tensor_copy(scatter_now[:, :], x.scatter[:, bass.ds(e, 1), :].rearrange("p o c -> p (o c)")).then_inc(s.scatter_ready, 1)
            run(pool, program)

        @block.tensor
        def _(pe):
            def gather(n, half):
                if half:
                    pe.wait_ge(s.tokens_ready, 2 * n - 1)
                else:
                    pe.wait_ge(s.hot_ready, n)
                for kt in range(4):
                    for a in range(TH):
                        ins = pe.matmul(k.bank(0)[:, kt * CAP:(kt + 1) * CAP], x.rows[:, a, (4 * half + kt) * P:(4 * half + kt + 1) * P],
                                        hot_now[:, a, :], start=a == 0, stop=a == 1)
                ins.then_inc(s.gathered, 1)

            def three(out, x_hi, x_lo, hi, lo, start, stop):
                pe.matmul(out, x_hi, hi, start=start, stop=False)
                pe.matmul(out, x_lo, hi, start=False, stop=False)
                return pe.matmul(out, x_hi, lo, start=False, stop=stop)

            def program():
                if p == 0:
                    pe.sem_inc(s.piece_used, X_SPLIT)
                    pe.sem_inc(s.out_done, FREE)
                for b in range(4, 8):
                    pe.matmul(k.bank(b), x.hot[:, E, 0, :], k.consts[:, 0:512], start=True, stop=False, skip_group_check=True)
                for half in range(2):
                    gather((E + 1) * p + 1, half)
                with pe.Fori(0, E) as e:
                    pe.wait_ge(s.tokens_ready, 2 * (E + 1) * p + 2 + 2 * e)
                    for j in range(PIECES):
                        kind, c = FFN_ORDER[j // 4]
                        if j % 4 == 0 and kind == "down":
                            pe.wait_ge(s.hid_ready, FREE + FC * x0 + c + 1 + FC * e)
                            if c == 0:
                                pe.wait_ge(s.y_kept, FREE + x0 + e)
                        elif j % 4 == 0 and (c or kind == "up"):
                            pe.wait_ge(s.gate_kept if kind == "gate" else s.hid_ready, FREE + FC * x0 + c + FC * e)
                        pe.wait_ge(k.lo_ready, PIECES * x0 + j + 1 + PIECES * e)
                        hi, lo = w_hi[:, j % X_SPLIT, :], w_lo[:, j % X_SPLIT, :]
                        for n in range(2):
                            cols = slice(n * CH, (n + 1) * CH)
                            if kind == "down":
                                f = j % 4
                                ins = three(k.bank(2 + n), hid_hi[:, f, :], hid_lo[:, f, :], hi[:, cols], lo[:, cols],
                                            c == 0 and f == 0, c == FC - 1 and f == MF - 1)
                            else:
                                kt = 2 * (j % 4) + n
                                ins = three(k.bank(0 if kind == "gate" else 1), tok_hi[:, kt, :], tok_lo[:, kt, :], hi[:, cols], lo[:, cols],
                                            kt == 0, kt == KT - 1)
                        ins.then_inc(s.piece_used, 1)
                        if j == last_piece("up", FC - 1):
                            pe.wait_ge(s.gate_kept, FREE + FC * (x0 + 1) + FC * e)
                            gather((E + 1) * p + 2 + e, 0)
                        for c in range(FC):
                            if j == turn_after(c):
                                pe.wait_ge(s.multiplied, FREE + FC * x0 + c + 1 + FC * e)
                                for f in range(MF):
                                    ins = pe.transpose(k.bank(1)[:, f * CAP:(f + 1) * CAP], hid[:, f * P:(f + 1) * P], k.c("ident"))
                                ins.then_inc(s.turned, 1)
                        if j == last_piece("up", FC - 1):
                            gather((E + 1) * p + 2 + e, 1)
                    pe.wait_ge(s.y_kept, FREE + x0 + 1 + e)
                    pe.wait_ge(s.scatter_ready, x0 + 1 + e)
                    for m in range(KT):
                        ins = pe.matmul(k.bank(4 + m // 2)[:, (m % 2) * T:(m % 2 + 1) * T], y[:, m * P:(m + 1) * P], scatter_now[:, :],
                                        start=False, stop=False, skip_group_check=True)
                    ins.then_inc(s.out_done, 1)
            run(pe, program)


def experts(k):
    with ExitStack() as own:
        k.ring_more = k.sb("ring_more", [P, X_RING - 2 * SLOTS, 2 * PIECE], own)
        k.lo_ready = k.sem("expert_lo_ready")
        k.half_filled = [k.sem(f"expert_half_filled{i}") for i in range(X_RING)]

        def first_loads(sp):
            for i in range(X_RING):
                load_expert_half(k, sp, 0, i, 0)

        out_project(k, "odd_out", O_OUT, DENSE, after=first_loads)
        rms_norm(k, "norm4", "norm2_o", DENSE)
        sb = lambda n, shape, dt=F32: k.sb("expert_" + n, shape, own, dt)
        x = Names(
            rows=sb("rows", [P, TH, D]),
            chosen=sb("chosen", [P, TH, E]), gate=sb("gate", [P, TH, E]), place=sb("place", [P, TH, E]),
            here=sb("here", [P, TH, E]), most=sb("most", [P, 1], I32),
            hot=sb("hot", [P, E + 1, TH, CAP]),
            scatter=sb("scatter", [CAP, E, T]))
        route(k, x)
        s = Names(**{n: k.sem("expert_" + n) for n in (
            "zeroed", "hot", "scatter_turned", "scatter_kept", "hot_ready", "gathered", "tokens_hi", "tokens_ready", "hi_ready",
            "turned", "piece_used", "gate_kept", "multiplied", "hid_hi", "hid_ready", "y_kept", "scatter_ready", "out_done", "added")})
        for p in range(PASSES):
            expert_tables(k, x, s, p)
            expert_pass(k, x, s, p)


def emit(k):
    turned, kept, stored = k.sem("out_turned"), k.sem("out_kept"), k.sem("out_stored")
    with ExitStack() as own:
        y = k.sb("out_rows", [P, TH, D], own)
        block = own.enter_context(k.nc.Block())

        @block.tensor
        def _(pe):
            for a in range(TH):
                for kt in range(KT):
                    ins = pe.transpose(k.bank(2 * a + kt // 4)[:, (kt % 4) * P:(kt % 4 + 1) * P], k.h[:, kt, a * P:(a + 1) * P], k.c("ident"))
                ins.then_inc(turned, 1)

        @block.vector
        def _(dve):
            for a in range(TH):
                dve.wait_ge(turned, a + 1)
                dve.tensor_copy(y[:, a, :], k.bank(2 * a, 2)).then_inc(kept, 1)

        @block.sync
        def _(sp):
            for a in range(TH):
                sp.wait_ge(kept, a + 1)
                sp.dma_start(k.g.out[0, a * P:(a + 1) * P, :], y[:, a, :]).then_inc(stored, 16)
            sp.wait_ge(stored, 16 * TH)


def build(nc, g):
    with ExitStack() as ctx:
        k = Program(nc, g, ctx)
        embed(k)
        rms_norm(k, "norm1", "norm1_e", SLOTS)
        even_mixer(k)
        out_project(k, "even_out", E_OUT, FFN + SLOTS)
        rms_norm(k, "norm2", "norm2_e", FFN + SLOTS)
        dense_ffn(k)
        k.recycle()
        rms_norm(k, "norm3", "norm1_o", O_IN + SLOTS)
        odd_mixer(k)
        k.recycle()
        experts(k)
        rms_norm(k, "norm5", "final", DENSE)
        emit(k)


INPUTS = ["x", "e_w_in", "e_gla_gate_up", "e_w_out", "e_ffn_w_gate", "e_ffn_w_up", "e_ffn_w_down", "o_w_in",
          "o_rw_w_up", "o_rw_a_up", "o_rw_g_up", "o_w_out", "o_moe_router", "o_moe_w_gate", "o_moe_w_up",
          "o_moe_w_down"]


def packed_params(i):
    cols = lambda a: np.asarray(a).reshape(-1, P).T
    gate_b = np.zeros((P, 2), np.float32)
    gate_b[0:4, :] = np.asarray(i["e_ml_gate_b"]).reshape(2, 4).T
    v = {
        "norm1_e": i["e_norm1_g"], "conv_w": i["e_ml_conv_w"], "conv_b": i["e_ml_conv_b"], "ml_norm": i["e_ml_norm_g"],
        "gla_b": i["e_gla_gate_b"], "gla_norm": i["e_gla_norm_g"], "norm2_e": i["e_norm2_g"], "norm1_o": i["o_norm1_g"],
        "ret_norm": i["o_ret_norm_g"], "mu": i["o_rw_mu"], "w0": i["o_rw_w0"], "a0": i["o_rw_a0"], "k_k": i["o_rw_k_k"],
        "k_a": i["o_rw_k_a"], "r_k": i["o_rw_r_k"], "ln_g": i["o_rw_ln_g"], "ln_b": i["o_rw_ln_b"],
        "norm2_o": i["o_norm2_g"], "final": i["final_norm_g"],
    }
    return np.concatenate([gate_b if n == "gate_b" else cols(v[n]) for n, _ in PARAM_COLS], axis=1)


def kernel(**inputs):
    import concourse.bacc as bacc
    from concourse.bass_utils import run_bass_kernel_spmd as run
    nc = bacc.Bacc("TRN2", target_bir_lowering=False, num_devices=1)
    arrays = {n: np.ascontiguousarray(inputs[n]) for n in INPUTS}
    arrays["params"] = np.ascontiguousarray(packed_params(inputs))
    arrays["consts"], arrays["ret_consts"], arrays["rw_consts"] = constants()
    sent = {f"in_{n}_dram": a for n, a in arrays.items()}
    g = Names(**{n: nc.dram_tensor(f"in_{n}_dram", a.shape, mybir.dt.from_np(a.dtype), kind="ExternalInput").ap()
                 for n, a in arrays.items()}, out=nc.dram_tensor("out_0_dram", (1, T, D), F32, kind="ExternalOutput").ap())
    build(nc, g)
    r = run(nc, [sent], core_ids=[0])
    return r.results[0]["out_0_dram"]
```

```python
from collections import namedtuple
from contextlib import ExitStack

import numpy as np
import concourse.bass as bass
from concourse import mybir

F32 = mybir.dt.float32
F32R = mybir.dt.float32r
I32 = mybir.dt.int32
ALU = mybir.AluOpType
ACT = mybir.ActivationFunctionType
AX = mybir.AxisListType

P = 128
T = 256
TH = T // P
D = 1024
KT = D // P
D_FF = 3584
FT = D_FF // P
E = 8
CAP = 128
PASSES = -(-T // CAP)
EPS = 1e-6
RW_LN_EPS = 64e-5
BIG = 1e30
GC = 16
GN = T // GC
RC = 64
RN = T // RC
CH = 512
SLOTS = 3
MF = CH // P
FC = D_FF // CH
LEVELS = (1, 2, 4, 8, 16, 32)

CONST_COLS = [
    ("ident", P), ("ones", P), ("head_ones", P), ("head_mean", P), ("mean", P), ("future", T),
    ("reset16", T), ("gla_block", P), ("parity", 2), ("select", 4 * P),
    ("before", P), ("slots", CAP), ("earlier", E * E), ("chunk_of16", 8),
]
RET_COLS = [("rot", P), ("cos", T), ("sin", T), ("decay", 4 * T), ("reset64", T)]
RW_COLS = [("strict", P), ("upto", P), ("levels", len(LEVELS) * P), ("head_cols", 2 * P)]
PARAM_COLS = [
    ("norm1_e", 8), ("conv_w", 32), ("conv_b", 8), ("ml_norm", 4), ("gla_b", 2), ("gla_norm", 4), ("norm2_e", 8),
    ("norm1_o", 8), ("ret_norm", 4), ("mu", 14), ("w0", 4), ("a0", 4), ("k_k", 4), ("k_a", 4), ("r_k", 4),
    ("ln_g", 4), ("ln_b", 4), ("norm2_o", 8), ("gate_b", 2), ("eps", 1), ("rw_eps", 1),
]


FFN_ORDER = [("gate", 0), ("up", 0)]
for _c in range(1, FC):
    FFN_ORDER += [("gate", _c), ("down", _c - 1), ("up", _c)]
FFN_ORDER += [("down", FC - 1)]
DENSE_ORDER = FFN_ORDER[:-4] + [("gate", FC - 1), ("up", FC - 1), ("down", FC - 2), ("down", FC - 1)]


def column_ranges(cols):
    at, out = 0, {}
    for name, n in cols:
        out[name] = (at, at + n)
        at += n
    return out, at


CONST_AT, CONST_N = column_ranges(CONST_COLS)
RET_AT, RET_N = column_ranges(RET_COLS)
RW_AT, RW_N = column_ranges(RW_COLS)
PARAM_AT, PARAM_N = column_ranges(PARAM_COLS)


def constants():
    c = {}
    r, t = np.arange(P)[:, None], np.arange(T)[None, :]
    s = t[:, :P]
    c["ident"] = r == s
    c["ones"] = np.ones((P, P))
    c["mean"] = np.full((P, P), 1.0 / P)
    c["head_ones"] = r // 64 == s // 64
    c["head_mean"] = (r // 64 == s // 64) / 64.0
    c["future"] = np.where(t >= r, 0.0, BIG)
    c["rot"] = 1.0 * (s == r + 64) - 1.0 * (s == r - 64)
    inv = np.float32(10000.0) ** (-np.arange(0, P, 2, dtype=np.float32) / np.float32(P))
    ang = np.arange(T, dtype=np.float32)[None, :] * inv[:, None]
    c["cos"] = np.tile(np.cos(ang), (2, 1))
    c["sin"] = np.tile(np.sin(ang), (2, 1))
    gamma = np.log1p(-np.exp2(-5.0 - np.arange(4)))
    c["decay"] = np.concatenate(
        [np.where(t >= r, np.exp(g * (t - r)), 0.0) * P ** -0.5 for g in gamma], axis=1)
    c["reset16"] = np.broadcast_to(t % GC != 0, (P, T))
    c["reset64"] = np.broadcast_to(t % RC != 0, (P, T))
    c["gla_block"] = (r // GC == s // GC) & (r % GC <= s % GC)
    c["parity"] = r // 64 == np.arange(2)[None, :]
    c["chunk_of16"] = r // GC == np.arange(8)[None, :]
    c["select"] = np.repeat(np.arange(4), P)[None, :] == r
    block = r // RC == s // RC
    c["strict"] = block & (r < s)
    c["upto"] = block & (r <= s)
    c["levels"] = np.concatenate([(r // (2 * m) == s // (2 * m)) & (r // m < s // m) for m in LEVELS], axis=1)
    c["before"] = r < s
    c["head_cols"] = np.broadcast_to(np.arange(2 * P)[None, :] // 64 % 2 == np.arange(2 * P)[None, :] // P, (P, 2 * P))
    c["slots"] = np.broadcast_to(np.arange(CAP)[None, :], (P, CAP))
    e = np.arange(E)
    c["earlier"] = np.broadcast_to((e[None, :] < e[:, None]).reshape(1, E * E), (P, E * E))
    pack = lambda cols: np.concatenate([np.asarray(c[n], np.float32) for n, _ in cols], axis=1)
    return pack(CONST_COLS), pack(RET_COLS), pack(RW_COLS)


def Names(**named):
    return namedtuple("Names", named)(**named)


def bc(ap, axis, n):
    a = ap.unsqueeze(axis)
    return a.broadcast_to([*a.shape[:axis], n, *a.shape[axis + 1:]])


def counted(engine, sem):
    n = [0]

    def after(ins):
        n[0] += 1
        ins.then_inc(sem, 1)
        engine.wait_ge(sem, n[0])

    return after


def weight_chunks(g):
    def cols(w, c0, n=CH):
        return w[:, c0:c0 + n].rearrange("(k p) c -> p k c", p=P)

    def rows(w, r0):
        return w[r0:r0 + CH, :].rearrange("(k p) c -> p k c", p=P)

    e_in, o_in = g.e_w_in[0], g.o_w_in[0]
    out = [cols(e_in, c) for c in (2056, 0, 512, 1024, 1536, 2568, 3080)]
    out += [cols(g.e_w_out[0], c) for c in (0, 512)]
    for kind, c in DENSE_ORDER:
        out.append({"gate": lambda: cols(g.e_ffn_w_gate[0], c * CH), "up": lambda: cols(g.e_ffn_w_up[0], c * CH),
                    "down": lambda: rows(g.e_ffn_w_down[0], c * CH)}[kind]())
    out += [cols(o_in, c, min(CH, 3840 - c)) for c in (3584, 2560, 2048, 3072, 0, 512, 1024, 1536)]
    out += [cols(g.o_w_out[0], c) for c in (0, 512)]
    return out


E_IN, E_OUT, FFN, O_IN, O_OUT, DENSE = 0, 7, 9, 30, 38, 40


class Program:
    def __init__(self, nc, g, ctx):
        self.nc, self.g, self.ctx = nc, g, ctx
        self.loads = weight_chunks(g)
        self.issued = 0
        self.stage_sems = []
        sb = self.sb
        self.ps = ctx.enter_context(nc.psum_tensor("ps", [P, 8, 512], F32))
        self.ring = sb("ring", [P, SLOTS, 8 * CH])
        self.consts = sb("consts", [P, CONST_N])
        self.params = sb("params", [P, PARAM_N])
        self.res = sb("res", [P, KT, T])
        self.h = sb("h", [P, KT, T])
        self.rstd = sb("rstd", [P, T])
        self.narrow = sb("narrow", [P, KT, 80])
        self.gate_up = sb("gate_up", [16, T])
        self.router = sb("router", [P, KT, E])
        self.slot_filled = [self.sem(f"slot_filled{i}") for i in range(SLOTS)]
        self.chunk_used = self.sem("chunk_used")
        self.stage_sems = []

    def sb(self, name, shape, ctx=None, dt=F32):
        return (ctx or self.ctx).enter_context(self.nc.sbuf_tensor(name, shape, dt))

    def sem(self, name):
        self.stage_sems.append(self.nc.alloc_semaphore(name))
        return self.stage_sems[-1]

    def recycle(self):
        self.nc.clear_and_free_semaphores(self.stage_sems)
        self.nc.all_engine_barrier()
        self.stage_sems = []

    def c(self, name, rows=P):
        a, b = CONST_AT[name]
        return self.consts[0:rows, a:b]

    def p(self, name, i=None, rows=P):
        a, b = PARAM_AT[name]
        return self.params[0:rows, a:b] if i is None else self.params[0:rows, a + i:a + i + 1]

    def bank(self, b, n=1):
        return self.ps[:, b:b + n, :].rearrange("p b c -> p (b c)")

    def chunk(self, n):
        w = self.ring[:, n % SLOTS, :]
        if tuple(self.loads[n].shape) == (P, MF, D):
            return w.rearrange("p (k c) -> p k c", k=MF)
        return w.rearrange("p (k c) -> p k c", k=KT)[:, :, 0:self.loads[n].shape[2]]

    def load_chunks(self, sp, end):
        for n in range(self.issued, min(end, DENSE)):
            if n >= SLOTS:
                sp.wait_ge(self.chunk_used, n - SLOTS + 1)
            sp.dma_start(self.chunk(n), self.loads[n]).then_inc(self.slot_filled[n % SLOTS], 16)
        self.issued = max(self.issued, min(end, DENSE))

    def wait_chunk(self, pe, n):
        pe.wait_ge(self.slot_filled[n % SLOTS], 16 * (n // SLOTS + 1))


def embed(k):
    nc, g = k.nc, k.g
    loaded, rest_loaded, turned, kept = k.sem("x_loaded"), k.sem("rest_loaded"), k.sem("x_turned"), k.sem("x_kept")
    zeroed = k.sem("narrow_zeroed")
    with ExitStack() as own:
        x = k.sb("x_rows", [P, TH, D], own)
        block = own.enter_context(nc.Block())

        @block.sync
        def _(sp):
            sp.dma_start(k.consts[:, 0:2 * P], g.consts[:, 0:2 * P]).then_inc(loaded, 16)
            sp.dma_start(x[:, :, :], g.x[0].rearrange("(a p) d -> p a d", p=P)).then_inc(loaded, 16)
            sp.dma_start(k.params[:, :], g.params).then_inc(rest_loaded, 16)
            sp.dma_start(k.consts[:, 2 * P:], g.consts[:, 2 * P:]).then_inc(rest_loaded, 16)
            w = g.e_w_in[0]
            sp.wait_ge(zeroed, 1)
            for at, c0, n in ((0, 2048, 4), (32, 2052, 4), (64, 3592, 16)):
                sp.dma_start(k.narrow[:, :, at:at + n], w[:, c0:c0 + n].rearrange("(k p) c -> p k c", p=P)).then_inc(rest_loaded, 16)
            sp.dma_start(k.gate_up[:, :], g.e_gla_gate_up[0]).then_inc(rest_loaded, 16)
            sp.dma_start(k.router[:, :, :], g.o_moe_router[0].rearrange("(k p) e -> p k e", p=P)).then_inc(rest_loaded, 16)
            k.load_chunks(sp, SLOTS)

        @block.gpsimd
        def _(pool):
            pool.memset(k.narrow[:, :, :], 0.0).then_inc(zeroed, 1)

        @block.tensor
        def _(pe):
            pe.wait_ge(loaded, 32)
            for kt in range(KT):
                for a in range(TH):
                    ins = pe.transpose(k.bank(kt)[:, a * P:(a + 1) * P], x[:, a, kt * P:(kt + 1) * P], k.c("ident"))
                ins.then_inc(turned, 1)

        @block.vector
        def _(dve):
            for kt in range(KT):
                dve.wait_ge(turned, kt + 1)
                dve.tensor_copy(k.res[:, kt, :], k.bank(kt)[:, 0:T]).then_inc(kept, 1)
            dve.wait_ge(kept, KT)
            dve.wait_ge(rest_loaded, 16 * 7)


def rms_norm(k, name, end, after=None):
    nc = k.nc
    squared, summed = k.sem(name + "_squared"), k.sem(name + "_summed")
    rooted, folded = k.sem(name + "_rooted"), k.sem(name + "_folded")
    with ExitStack() as own:
        sq = k.sb(name + "_sq", [P, KT, T], own)
        block = own.enter_context(nc.Block())

        @block.sync
        def _(sp):
            k.load_chunks(sp, end)
            if after:
                after(sp)

        @block.scalar
        def _(act):
            act.activation(sq[:, 0:4, :], k.res[:, 0:4, :], ACT.Square).then_inc(squared, 1)
            act.wait_ge(summed, 1)
            act.activation(k.rstd[:, :], k.bank(0)[:, 0:T], ACT.Ln, bias=k.p("eps"), scale=1.0 / D).then_inc(rooted, 1)
            act.wait_ge(rooted, 1)
            act.activation(k.rstd[:, :], k.rstd[:, :], ACT.Exp, scale=-0.5).then_inc(rooted, 1)
            act.wait_ge(rooted, 2)

        @block.tensor
        def _(pe):
            pe.wait_ge(folded, 4)
            pe.matmul(k.bank(0)[:, 0:T], k.c("ones"), sq[:, 0, :], start=True, stop=True).then_inc(summed, 1)

        @block.vector
        def _(dve):
            dve.tensor_tensor(sq[:, 4:8, :], k.res[:, 4:8, :], k.res[:, 4:8, :], ALU.mult).then_inc(folded, 1)
            dve.wait_ge(squared, 1)
            for i, n in enumerate((4, 2, 1)):
                dve.wait_ge(folded, i + 1)
                dve.tensor_tensor(sq[:, 0:n, :], sq[:, 0:n, :], sq[:, n:2 * n, :], ALU.add).then_inc(folded, 1)


PIECE = KT * CH // 4
DENSE_SPLIT = 3


class SplitWeights:

    def __init__(self, k, name, first, own):
        self.k, self.first = k, first
        self.w_hi, self.w_lo = (k.sb(f"{name}_w_{n}", [P, DENSE_SPLIT, PIECE], own, F32R) for n in ("hi", "lo"))
        self.hi_ready, self.lo_ready, self.used = (k.sem(f"{name}_w_{n}") for n in ("hi_ready", "lo_ready", "used"))

    def piece(self, j):
        n = self.first + j // 4
        w = self.k.chunk(n)
        if w.shape[1] == MF:
            return w[:, j % 4, :], lambda part: part[:, j % DENSE_SPLIT, :]
        c = w.shape[2]
        return w[:, 2 * (j % 4):2 * (j % 4) + 2, :], lambda part: part[:, j % DENSE_SPLIT, 0:2 * c].rearrange("p (k c) -> p k c", k=2)

    def hi_of(self, j):
        return self.w_hi[:, j % DENSE_SPLIT, :]

    def lo_of(self, j):
        return self.w_lo[:, j % DENSE_SPLIT, :]

    def hi(self, act, j):
        src, part = self.piece(j)
        if j % 4 == 0:
            self.k.wait_chunk(act, self.first + j // 4)
        if j >= DENSE_SPLIT:
            act.wait_ge(self.used, j - DENSE_SPLIT + 1)
        act.copy(part(self.w_hi), src).then_inc(self.hi_ready, 1)

    def lo(self, engine, j):
        src, part = self.piece(j)
        engine.wait_ge(self.hi_ready, j + 1)
        engine.tensor_tensor(part(self.w_lo), src, part(self.w_hi).bitcast(F32), ALU.subtract).then_inc(self.lo_ready, 1)


class SplitStream:

    def __init__(self, k, name, own, gain=None):
        self.k, self.gain = k, gain
        if gain:
            self.normalised = k.sem(name + "_h_normalised")
        self.x_hi, self.x_lo = (k.sb(f"{name}_h_{n}", [P, KT, T], own, F32R) for n in ("hi", "lo"))
        self.hi_ready, self.ready = k.sem(name + "_h_hi"), k.sem(name + "_h_ready")

    def normalise(self, dve, i):
        for kt in (2 * i, 2 * i + 1):
            dve.scalar_tensor_tensor(out=self.k.h[:, kt, :], in0=self.k.res[:, kt, :], scalar=self.k.p(self.gain, kt),
                                     in1=self.k.rstd[:, :], op0=ALU.mult, op1=ALU.mult).then_inc(self.normalised, 1)

    def normalise_and_lo(self, dve):
        self.normalise(dve, 0)
        for i in range(4):
            if i < 3:
                self.normalise(dve, i + 1)
            self.lo(dve, i)

    def hi(self, act, i):
        if self.gain:
            act.wait_ge(self.normalised, 2 * i + 2)
        act.copy(self.x_hi[:, 2 * i:2 * i + 2, :], self.k.h[:, 2 * i:2 * i + 2, :]).then_inc(self.hi_ready, 1)

    def lo(self, engine, i):
        engine.wait_ge(self.hi_ready, i + 1)
        engine.tensor_tensor(self.x_lo[:, 2 * i:2 * i + 2, :], self.k.h[:, 2 * i:2 * i + 2, :],
                             self.x_hi[:, 2 * i:2 * i + 2, :].bitcast(F32), ALU.subtract).then_inc(self.ready, 1)


def three(pe, out, a_hi, a_lo, b_hi, b_lo, start):
    pe.matmul(out, a_hi, b_hi, start=start, stop=False, skip_group_check=True)
    pe.matmul(out, a_hi, b_lo, start=False, stop=False, skip_group_check=True)
    return pe.matmul(out, a_lo, b_hi, start=False, stop=True, skip_group_check=True)


def product_tokens(pe, out, w, x, j):
    for a in range(TH):
        for i in range(2):
            kt = 2 * (j % 4) + i
            cols, toks = slice(i * CH, (i + 1) * CH), slice(a * P, (a + 1) * P)
            ins = three(pe, out[:, a * CH:(a + 1) * CH], x.x_hi[:, kt, toks], x.x_lo[:, kt, toks], w.hi_of(j)[:, cols],
                        w.lo_of(j)[:, cols], kt == 0)
    return ins


def product(pe, out, w, x, j, m_tiles=MF):
    hi, lo = w.hi_of(j), w.lo_of(j)
    for m in range(m_tiles):
        for i in range(2):
            kt = 2 * (j % 4) + i
            cols = slice((i * m_tiles + m) * P, (i * m_tiles + m + 1) * P)
            ins = three(pe, out[:, m * T:(m + 1) * T], hi[:, cols], lo[:, cols], x.x_hi[:, kt, :], x.x_lo[:, kt, :],
                        kt == 0 and m % 2 == 0)
    return ins


def project(pe, k, w, x, i, out, tokens_out=False, m_tiles=MF):
    for j in range(4 * i, 4 * i + 4):
        if j < 4:
            pe.wait_ge(x.ready, j + 1)
        pe.wait_ge(w.lo_ready, j + 1)
        ins = product_tokens(pe, out, w, x, j) if tokens_out else product(pe, out, w, x, j, m_tiles)
        ins.then_inc(w.used, 1)
    pe.sem_inc(k.chunk_used, 1)


def out_project(k, name, n, end, after=None):
    added = k.sem(name + "_added")
    with ExitStack() as own:
        w, x = SplitWeights(k, name, n, own), SplitStream(k, name, own)
        block = own.enter_context(k.nc.Block())

        @block.sync
        def _(sp):
            k.load_chunks(sp, end)
            if after:
                after(sp)

        @block.tensor
        def _(pe):
            for i in range(2):
                project(pe, k, w, x, i, k.bank(4 * i, 2))

        @block.scalar
        def _(act):
            for j in range(8):
                if j < 4:
                    x.hi(act, j)
                w.hi(act, j)

        @block.vector
        def _(dve):
            for j in range(8):
                if j < 4:
                    x.lo(dve, j)
                w.lo(dve, j)
            for i in range(2):
                dve.wait_ge(w.used, 4 * i + 4)
                r = k.res[:, 4 * i:4 * i + 4, :]
                dve.tensor_tensor(r, r, k.bank(4 * i, 2).rearrange("p (m t) -> p m t", m=4), ALU.add).then_inc(added, 1)
            dve.wait_ge(added, 2)


def even_mixer(k):
    with ExitStack() as own:
        sb = lambda n, shape: k.sb("e_" + n, shape, own)
        m = Names(
            gqk=sb("gqk", [P, 4, T]),
            gv=sb("gv", [P, TH, CH]), gr=sb("gr", [P, 4, T]),
            qk=sb("qk", [P, 8, T]),
            v=sb("v", [P, TH, CH]), o=sb("o", [P, 4, T]),
            gates=sb("gates", [4, 10, T]),
            la=sb("la", [P, 4, 2, T]),
            expb=sb("expb", [P, 2, T]),
            kdec=sb("kdec", [P, 2, T]),
            qe=sb("qe", [P, 2, 2, T]),
            pair=sb("pair", [P, 16 * GC * GC]),
            pads=sb("pads", [P, 2, 4, T + 3]),
            att=sb("att", [P, 8, P]),
            tmp=sb("tmp", [P, 4, T]),
        )
        even_project(k, m)
        even_attend(k, m, sb)


(LOG_I, ABS_F, EXP_F, LN_F, NEG_F, LOG_F, SUM_F, U, MAX_U, MAX_M) = range(10)


def even_project(k, m):
    nc, g = k.nc, k.g
    s = Names(**{n: k.sem("ep_" + n) for n in (
        "small_done", "small_kept", "proj_kept", "low_done", "gates_split", "gates_exp", "gates_ln",
        "decay_summed", "decay_exp", "diff_ready", "pair_exp", "pair_ready", "att_done", "dve_chain",
        "zeroed", "conv_done", "gated")})
    with ExitStack() as own:
        w, x = SplitWeights(k, "ep", E_IN, own), SplitStream(k, "ep", own, "norm1_e")
        low = k.sb("ep_low", [16, T], own)
        attc = k.sb("ep_attc", [P, 8, GC], own)
        block = own.enter_context(nc.Block())
        icj = m.pair[:, :].rearrange("p (i c j) -> p i c j", i=GC, j=GC)
        flat = m.pair[:, :].rearrange("p (i t) -> p i t", i=GC)

        @block.sync
        def _(sp):
            k.load_chunks(sp, E_OUT + SLOTS)

        @block.gpsimd
        def _(pool):
            pool.memset(m.pads[:, :, :, 0:3], 0.0).then_inc(s.zeroed, 1)
            pool.memset(m.qe[:, :, :, :], 0.0).then_inc(s.zeroed, 1)
            for j in range(4 * 7):
                w.lo(pool, j)

        @block.tensor
        def _(pe):
            for kt in range(KT):
                pe.wait_ge(x.normalised, kt + 1)
                ins = pe.matmul(k.bank(6)[0:80, 0:T], k.narrow[:, kt, :], k.h[:, kt, :], start=kt == 0, stop=kt == KT - 1)
            ins.then_inc(s.small_done, 1)
            project(pe, k, w, x, 0, k.bank(0, 2))
            pe.wait_ge(s.small_kept, 1)
            for i in range(2):
                ins = pe.matmul(k.bank(7)[:, i * T:(i + 1) * T], k.gate_up[:, i * P:(i + 1) * P], low[:, :], start=True, stop=True)
            ins.then_inc(s.low_done, 1)
            for n in range(1, 7):
                if n >= 3:
                    pe.wait_ge(s.proj_kept, n - 2)
                project(pe, k, w, x, n, k.bank(2 * (n % 3), 2), tokens_out=n in (3, 5))
                if n in (3, 6):
                    hp = n // 3 - 1
                    pe.wait_ge(s.pair_ready, hp + 1)
                    for a in range(TH):
                        for i in range(GC):
                            at = (hp * TH + a) * 2
                            ins = pe.matmul(k.bank(6)[:, 0:P].rearrange("p (g i) -> p g i", i=GC)[:, at:at + 2, i],
                                            flat[:, i, a * P:(a + 1) * P], k.c("parity"), start=True, stop=True)
                    ins.then_inc(s.att_done, 1)

        @block.scalar
        def _(act):
            for j in range(3):
                w.hi(act, j)
                x.hi(act, j)
            x.hi(act, 3)
            act.wait_ge(s.small_done, 1)
            act.copy(low[:, :], k.bank(6)[64:80, 0:T]).then_inc(s.small_kept, 1)
            for j in range(3, 7):
                w.hi(act, j)
            act.wait_ge(w.used, 4)
            act.mul(m.gqk[:, 0:2, :].rearrange("p a t -> p (a t)"), k.bank(0), 64 ** -0.5).then_inc(s.gated, 1)
            act.copy(m.gqk[:, 2:4, :].rearrange("p a t -> p (a t)"), k.bank(1)).then_inc(s.proj_kept, 1)
            act.wait_ge(s.gates_split, 2)
            act.activation(m.gates[:, EXP_F, :], m.gates[:, ABS_F, :], ACT.Exp, scale=-1.0).then_inc(s.gates_exp, 1)
            act.activation(m.la[:, 1, :, :], m.la[:, 0, :, :], ACT.Exp, scale=-1.0).then_inc(s.gates_exp, 1)
            w.hi(act, 7)
            act.wait_ge(s.gates_exp, 2)
            act.activation(m.gates[:, LN_F, :], m.gates[:, EXP_F, :], ACT.Ln, bias=1.0).then_inc(s.gates_ln, 1)
            act.activation(m.la[:, 2, :, :], m.la[:, 1, :, :], ACT.Ln, bias=1.0).then_inc(s.gates_ln, 1)
            w.hi(act, 8)
            act.wait_ge(s.decay_summed, 1)
            act.activation(m.expb[:, :, :], m.la[:, 0, :, :], ACT.Exp).then_inc(s.decay_exp, 1)
            act.activation(m.la[:, 3, :, :], m.la[:, 1, :, :], ACT.Exp).then_inc(s.decay_exp, 1)
            w.hi(act, 9)
            act.wait_ge(s.diff_ready, 1)
            w.hi(act, 10)
            act.activation(m.pair[:, :], m.pair[:, :], ACT.Exp).then_inc(s.pair_exp, 1)
            act.wait_ge(s.zeroed, 1)
            for n in range(1, 7):
                for j in range(4 * n + 3 if n > 1 else 11, min(4 * n + 7, 28)):
                    w.hi(act, j)
                act.wait_ge(w.used, 4 * n + 4)
                if n in (1, 2):
                    act.copy(m.pads[:, n - 1, :, 3:], k.bank(2 * (n % 3), 2).rearrange("p (m t) -> p m t", m=4)).then_inc(s.proj_kept, 1)
                else:
                    dst = (m.v, m.o, m.gv, m.gr)[n - 3]
                    act.copy(dst[:, :, :].rearrange("p a b -> p (a b)"), k.bank(2 * (n % 3), 2)).then_inc(s.proj_kept, 1)
                if n == 4:
                    act.wait_ge(s.diff_ready, 2)
                    act.activation(m.pair[:, :], m.pair[:, :], ACT.Exp).then_inc(s.pair_exp, 1)
            act.wait_ge(s.conv_done, 2)
            act.wait_ge(s.proj_kept, 7)
            act.activation(m.qk[:, :, :], m.qk[:, :, :], ACT.Silu).then_inc(s.gated, 1)
            act.activation(m.gr[:, :, :], m.gr[:, :, :], ACT.Silu).then_inc(s.gated, 1)
            act.activation(m.o[:, :, :], m.o[:, :, :], ACT.Sigmoid).then_inc(s.gated, 1)
            act.wait_ge(s.gated, 4)

        @block.vector
        def _(dve):
            x.normalise_and_lo(dve)
            step = counted(dve, s.dve_chain)
            gt = m.gates
            dve.wait_ge(s.small_done, 1)
            step(dve.tensor_scalar(gt[:, LOG_I, :], k.bank(6)[0:4, 0:T], k.p("gate_b", 0, 4), None, ALU.add))
            step(dve.tensor_scalar(gt[:, LOG_F, :], k.bank(6)[32:36, 0:T], k.p("gate_b", 1, 4), None, ALU.add))
            step(dve.tensor_scalar(gt[:, NEG_F, :], gt[:, LOG_F, :], 0.0, None, ALU.min))
            step(dve.scalar_tensor_tensor(out=gt[:, ABS_F, :], in0=gt[:, LOG_F, :], scalar=-1.0, in1=gt[:, LOG_F, :],
                                          op0=ALU.mult, op1=ALU.max))
            dve.wait_ge(s.low_done, 1)
            for i in range(2):
                step(dve.tensor_scalar(m.la[:, 2, i, :], k.bank(7)[:, i * T:(i + 1) * T], k.p("gla_b", i), None, ALU.add))
                step(dve.tensor_scalar(m.la[:, 3, i, :], m.la[:, 2, i, :], 0.0, None, ALU.min))
                dve.scalar_tensor_tensor(out=m.la[:, 0, i, :], in0=m.la[:, 2, i, :], scalar=-1.0, in1=m.la[:, 2, i, :],
                                         op0=ALU.mult, op1=ALU.max).then_inc(s.gates_split, 1)
            dve.wait_ge(s.gates_ln, 2)
            step(dve.tensor_tensor(m.la[:, 0, :, :], m.la[:, 3, :, :], m.la[:, 2, :, :], ALU.subtract))
            step(dve.tensor_scalar(m.la[:, 2, :, :], m.la[:, 0, :, :], 1.0 / 16.0, None, ALU.mult))
            for hp in range(2):
                step(dve.tensor_tensor_scan(m.la[:, 0, hp, :], k.c("reset16"), m.la[:, 2, hp, :], 0.0, ALU.mult, ALU.add))
            b = m.la[:, 0, :, :].rearrange("p h (c t) -> p (h c) t", t=GC)
            dve.tensor_tensor(m.la[:, 1, :, :].rearrange("p h (c t) -> p (h c) t", t=GC),
                              b[:, :, GC - 1:GC].broadcast_to([P, 2 * GN, GC]), b, ALU.subtract).then_inc(s.decay_summed, 1)

            def pair_diff(hp):
                bb = m.la[:, 0, hp, :].rearrange("p (c t) -> p c t", t=GC)
                dve.tensor_tensor(icj, bc(bb.rearrange("p c i -> p i c"), 3, GC), bc(bb, 1, GC), ALU.subtract).then_inc(s.diff_ready, 1)

            def pair_product(hp):
                dve.wait_ge(s.pair_exp, hp + 1)
                step(dve.scalar_tensor_tensor(out=flat, in0=flat, scalar=1.0, in1=bc(m.gqk[:, 2 + hp, :], 1, GC),
                                              op0=ALU.min, op1=ALU.mult))
                q = m.gqk[:, hp, :].rearrange("p (c i) -> p i c", i=GC)
                dve.tensor_tensor(icj, icj, bc(q, 3, GC), ALU.mult).then_inc(s.pair_ready, 1)

            def conv(n):
                dve.wait_ge(s.proj_kept, n + 1)
                for i in range(4):
                    ch = (n - 1) * 4 + i
                    step(dve.tensor_scalar(m.tmp[:, i, :], m.pads[:, n - 1, i, 3:], k.p("conv_w", 24 + ch),
                                           k.p("conv_b", ch), ALU.mult, ALU.add))
                    for tap in (2, 1, 0):
                        out = m.tmp[:, i, :] if tap else m.qk[:, ch, :]
                        step(dve.scalar_tensor_tensor(out=out, in0=m.pads[:, n - 1, i, tap:tap + T],
                                                      scalar=k.p("conv_w", tap * 8 + ch), in1=m.tmp[:, i, :],
                                                      op0=ALU.mult, op1=ALU.add))
                dve.sem_inc(s.conv_done, 1)

            pair_diff(0)
            step(dve.tensor_tensor(gt[:, LOG_F, :], gt[:, NEG_F, :], gt[:, LN_F, :], ALU.subtract))
            step(dve.tensor_tensor_scan(gt[:, SUM_F, :], k.c("ones", 4)[:, 0:1].broadcast_to([4, T]), gt[:, LOG_F, :], 0.0,
                                        ALU.mult, ALU.add))
            step(dve.tensor_tensor(gt[:, U, :], gt[:, LOG_I, :], gt[:, SUM_F, :], ALU.subtract))
            step(dve.tensor_tensor_scan(gt[:, MAX_U, :], gt[:, U, :], gt[:, U, :], 0.0, ALU.max, ALU.max))
            step(dve.tensor_tensor(gt[:, MAX_M, :], gt[:, MAX_U, :], gt[:, SUM_F, :], ALU.add))
            dve.wait_ge(s.decay_exp, 2)
            dve.wait_ge(s.zeroed, 2)
            dve.wait_ge(s.proj_kept, 1)
            dve.wait_ge(s.gated, 1)
            for hd in range(2):
                r = slice(64 * hd, 64 * hd + 64)
                step(dve.tensor_tensor(m.qe[r, :, hd, :], m.gqk[r, 0:2, :], m.expb[r, :, :], ALU.mult))
            step(dve.tensor_tensor(m.kdec[:, :, :], m.gqk[:, 2:4, :], m.la[:, 3, :, :], ALU.mult))
            pair_product(0)
            conv(1)
            conv(2)
            dve.wait_ge(s.att_done, 1)
            pair_diff(1)
            pair_product(1)
            dve.wait_ge(s.att_done, 2)
            step(dve.tensor_copy(attc[:, :, :], k.bank(6)[:, 0:P].rearrange("p (g i) -> p g i", i=GC)))
            blocks = k.c("gla_block").rearrange("p (c i) -> p c i", i=GC)
            step(dve.tensor_tensor(m.att[:, :, :].rearrange("p g (c i) -> p g c i", i=GC), bc(attc[:, :, :], 2, 8),
                                   bc(blocks, 1, 8), ALU.mult))


def even_attend(k, m, sb):
    nc = k.nc
    s = Names(**{n: k.sem("ea_" + n) for n in (
        "turned", "turned_kept", "spread", "spread_kept", "spread_exp", "limited", "weighted", "scored", "p_ready",
        "num_done", "gated", "mean_done", "centred", "squared", "var_done", "mixed", "u_done", "state_ready",
        "inter_done", "dve_chain", "rooted", "gla_squared", "gla_var_done", "den_ready")})
    with ExitStack() as own:
        ucol = k.sb("ea_u_cols", [P, TH, 4], own)
        wts = k.sb("ea_wts", [P, 4, T + P], own)
        ot = m.gqk
        spread = m.la[:, :, :, :].rearrange("p a b t -> p a (b t)")
        kex = m.pair[:, :].rearrange("p (g c f) -> p g c f", c=8, f=P)
        pads = m.pads[:, :, :, :].rearrange("p a b t -> p (a b t)")
        state = pads[:, 0:8 * T].rearrange("p (c a t) -> p c a t", c=4, a=2)
        tmp = m.tmp
        block = own.enter_context(nc.Block())

        @block.sync
        def _(sp):
            k.load_chunks(sp, E_OUT + SLOTS)

        def inter(pe, c):
            pe.wait_ge(s.state_ready, c + 1)
            for hd in range(4):
                b = k.bank(4 + hd // 2)[:, (hd % 2) * T + c * GC:(hd % 2) * T + (c + 1) * GC]
                ins = pe.matmul(b, state[:, c % 4, hd // 2, (hd % 2) * P:(hd % 2 + 1) * P],
                                m.qe[:, hd // 2, hd % 2, c * GC:(c + 1) * GC], start=False, stop=False, skip_group_check=True)
            return ins.then_inc(s.inter_done, 1)

        @block.tensor
        def _(pe):
            for a in range(TH):
                pe.transpose(k.bank(6)[:, a * 4:a * 4 + 4], m.gates[:, U, a * P:(a + 1) * P], k.c("ident", 4)[:, 0:4])
            for gi in range(4):
                ins = pe.transpose(k.bank(7)[:, gi * P:(gi + 1) * P], m.kdec[:, gi // 2, (gi % 2) * P:(gi % 2 + 1) * P], k.c("ident"))
            ins.then_inc(s.turned, 1)
            for hd in range(4):
                ins = pe.matmul(k.bank(hd), k.c("select", 4)[:, hd * P:(hd + 1) * P], m.gates[:, MAX_U:MAX_U + 2, :],
                                start=True, stop=True)
            ins.then_inc(s.spread, 1)
            pe.wait_ge(s.turned_kept, 2)
            for hd in range(4):
                b = k.bank(4 + hd)
                pe.matmul(b[:, 0:T], m.qk[:, 4 + hd, 0:P], m.qk[:, hd, :], start=True, stop=True)
                pe.matmul(b[:, T:T + P], m.qk[:, 4 + hd, P:T], m.qk[:, hd, P:T], start=True, stop=True).then_inc(s.scored, 1)
            pe.wait_ge(s.spread_kept, 1)
            for hd in range(4):
                pe.wait_ge(s.p_ready, hd + 1)
                b = k.bank(hd)
                cols = slice(hd * P, (hd + 1) * P)
                for w0, w1, at in ((m.v[:, 0, cols], m.v[:, 1, cols], 0), (k.c("ones"), k.c("ones"), T)):
                    pe.matmul(b[:, at:at + T], w0, wts[:, hd, 0:T], start=True, stop=False, skip_group_check=True)
                    ins = pe.matmul(b[:, at + P:at + T], w1, wts[:, hd, T:T + P], start=False, stop=True, skip_group_check=True)
                ins.then_inc(s.num_done, 1)
            for hd in range(4):
                for a in range(TH):
                    b = k.bank(4 + hd // 2)[:, (hd % 2) * T + a * P:(hd % 2) * T + (a + 1) * P]
                    pe.matmul(b, m.gv[:, a, hd * P:(hd + 1) * P], m.att[:, ((hd // 2) * TH + a) * 2 + hd % 2, :],
                              start=hd % 2 == 0 and a == 0, stop=False, skip_group_check=True)
            for c in range(GN - 1):
                if c >= 2:
                    pe.wait_ge(s.state_ready, c)
                for hp in range(2):
                    ins = pe.matmul(k.bank(6 + c % 2)[:, hp * T:(hp + 1) * T], kex[:, hp * 2 + c // 8, c % 8, :],
                                    m.gv[:, c // 8, hp * T:(hp + 1) * T], start=True, stop=True)
                ins.then_inc(s.u_done, 1)
                if c >= 1:
                    inter(pe, c)
                if c == 2:
                    pe.wait_ge(s.gated, 4)
                    for i in range(2):
                        ins = pe.matmul(k.bank(i), k.c("mean"), ot[:, 2 * i:2 * i + 2, :], start=True, stop=True)
                    ins.then_inc(s.mean_done, 1)
                if c == 5:
                    pe.wait_ge(s.squared, 1)
                    for i in range(2):
                        ins = pe.matmul(k.bank(2 + i), k.c("mean"), tmp[:, 2 * i:2 * i + 2, :], start=True, stop=True)
                    ins.then_inc(s.var_done, 1)
            inter(pe, GN - 1)
            pe.wait_ge(s.gla_squared, 1)
            for i in range(2):
                ins = pe.matmul(k.bank(6 + i), k.c("mean"), tmp[:, 2 * i:2 * i + 2, :], start=True, stop=True)
            ins.then_inc(s.gla_var_done, 1)

        @block.scalar
        def _(act):
            act.wait_ge(s.spread, 1)
            act.copy(spread.rearrange("p h c -> p (h c)"), k.bank(0, 4)).then_inc(s.spread_kept, 1)
            act.wait_ge(s.spread_kept, 1)
            act.activation(spread[:, :, T:2 * T], spread[:, :, T:2 * T], ACT.Exp, scale=-1.0).then_inc(s.spread_exp, 1)
            for hd in range(4):
                act.wait_ge(s.limited, 2 * hd + 2)
                act.activation(wts[:, hd, :], wts[:, hd, :], ACT.Exp, scale=-1.0).then_inc(s.weighted, 1)
            for hd in range(4):
                act.wait_ge(s.num_done, hd + 1)
                act.activation(tmp[:, hd, :], k.bank(hd)[:, T:2 * T], ACT.Abs).then_inc(s.den_ready, 1)
            act.wait_ge(s.centred, 1)
            act.activation(tmp[:, :, :], ot[:, :, :], ACT.Square).then_inc(s.squared, 1)
            act.wait_ge(s.var_done, 1)
            act.activation(tmp[:, :, :], k.bank(2, 2).rearrange("p (h t) -> p h t", h=4), ACT.Ln, bias=k.p("eps")).then_inc(s.rooted, 1)
            act.wait_ge(s.rooted, 1)
            act.activation(tmp[:, :, :], tmp[:, :, :], ACT.Exp, scale=-0.5).then_inc(s.rooted, 1)
            act.wait_ge(s.inter_done, GN - 1)
            act.wait_ge(s.mixed, 1)
            act.activation(tmp[:, :, :].rearrange("p h t -> p (h t)"), k.bank(4, 2), ACT.Square).then_inc(s.gla_squared, 1)
            act.wait_ge(s.gla_var_done, 1)
            act.activation(tmp[:, :, :], k.bank(6, 2).rearrange("p (h t) -> p h t", h=4), ACT.Ln, bias=k.p("eps")).then_inc(s.rooted, 1)
            act.wait_ge(s.rooted, 3)
            act.activation(tmp[:, :, :], tmp[:, :, :], ACT.Exp, scale=-0.5).then_inc(s.rooted, 1)

        @block.vector
        def _(dve):
            step = counted(dve, s.dve_chain)
            dve.wait_ge(s.turned, 1)
            dve.tensor_copy(ucol[:, :, :], k.bank(6)[:, 0:8].rearrange("p (a h) -> p a h", a=TH)).then_inc(s.turned_kept, 1)
            kt = k.bank(7).rearrange("p (g f) -> p g f", f=P)
            in_chunk = bc(k.c("chunk_of16"), 2, P)
            for gi in range(4):
                ins = dve.tensor_tensor(kex[:, gi, :, :], bc(kt[:, gi, :], 1, 8), in_chunk, ALU.mult)
                if gi < 3:
                    step(ins)
            ins.then_inc(s.turned_kept, 1)
            dve.wait_ge(s.spread_kept, 1)
            dve.wait_ge(s.turned_kept, 1)
            for hd in range(4):
                dve.scalar_tensor_tensor(out=wts[:, hd, 0:T], in0=spread[:, hd, 0:T], scalar=ucol[:, 0, hd:hd + 1],
                                         in1=k.c("future"), op0=ALU.subtract, op1=ALU.max).then_inc(s.limited, 1)
                dve.scalar_tensor_tensor(out=wts[:, hd, T:T + P], in0=spread[:, hd, P:T], scalar=ucol[:, 1, hd:hd + 1],
                                         in1=k.c("future")[:, 0:P], op0=ALU.subtract, op1=ALU.max).then_inc(s.limited, 1)
            for hd in range(4):
                dve.wait_ge(s.weighted, hd + 1)
                dve.wait_ge(s.scored, hd + 1)
                dve.scalar_tensor_tensor(out=wts[:, hd, :], in0=k.bank(4 + hd)[:, 0:T + P], scalar=P ** -0.5,
                                         in1=wts[:, hd, :], op0=ALU.mult, op1=ALU.mult).then_inc(s.p_ready, 1)
            def update_state(c):
                dve.wait_ge(s.u_done, c + 1)
                if c == 0:
                    dve.memset(state[:, 0, :, :], 0.0).then_inc(s.state_ready, 1)
                    dve.wait_ge(s.state_ready, 1)
                if c >= 4:
                    dve.wait_ge(s.inter_done, c - 3)
                for hp in range(2):
                    ins = dve.scalar_tensor_tensor(out=state[:, (c + 1) % 4, hp, :], in0=state[:, c % 4, hp, :],
                                                   scalar=m.expb[:, hp, c * GC + GC - 1:c * GC + GC],
                                                   in1=k.bank(6 + c % 2)[:, hp * T:(hp + 1) * T], op0=ALU.mult, op1=ALU.add)
                    if hp == 0:
                        step(ins)
                ins.then_inc(s.state_ready, 1)
                dve.wait_ge(s.state_ready, c + 2)

            dve.wait_ge(s.spread_exp, 1)
            for hd in range(4):
                dve.wait_ge(s.num_done, hd + 1)
                dve.wait_ge(s.den_ready, hd + 1)
                step(dve.tensor_tensor(tmp[:, hd, :], tmp[:, hd, :], spread[:, hd, T:2 * T], ALU.max))
                step(dve.reciprocal(tmp[:, hd, :], tmp[:, hd, :]))
                step(dve.tensor_tensor(ot[:, hd, :], k.bank(hd)[:, 0:T], tmp[:, hd, :], ALU.mult))
                dve.tensor_tensor(ot[:, hd, :], ot[:, hd, :], m.o[:, hd, :], ALU.mult).then_inc(s.gated, 1)
                if hd >= 2:
                    update_state(hd - 2)
            dve.wait_ge(s.gated, 4)
            update_state(2)
            flat = lambda a: a.rearrange("p h t -> p (h t)")
            dve.wait_ge(s.mean_done, 1)
            dve.tensor_tensor(flat(ot[:, :, :]), flat(ot[:, :, :]), k.bank(0, 2), ALU.subtract).then_inc(s.centred, 1)
            dve.wait_ge(s.centred, 1)
            for c in range(3, 8):
                update_state(c)
            dve.wait_ge(s.rooted, 2)
            for hd in range(4):
                ins = dve.scalar_tensor_tensor(out=k.h[:, hd, :], in0=ot[:, hd, :], scalar=k.p("ml_norm", hd),
                                               in1=tmp[:, hd, :], op0=ALU.mult, op1=ALU.mult)
                if hd < 3:
                    step(ins)
            ins.then_inc(s.mixed, 1)
            for c in range(8, GN - 1):
                update_state(c)
                if 10 <= c < 14:
                    hd = c - 10
                    step(dve.tensor_scalar(m.gr[:, hd, :], m.gr[:, hd, :], k.p("gla_norm", hd), None, ALU.mult))
            dve.wait_ge(s.rooted, 4)
            step(dve.tensor_tensor(flat(tmp[:, :, :]), flat(tmp[:, :, :]), k.bank(4, 2), ALU.mult))
            step(dve.tensor_tensor(k.h[:, 4:8, :], tmp[:, :, :], m.gr[:, :, :], ALU.mult))


def dense_ffn(k):
    with ExitStack() as own:
        s = Names(**{n: k.sem("ffn_" + n) for n in ("gate_kept", "multiplied", "hid_hi", "hid_ready", "added")})
        w, x = SplitWeights(k, "ffn", FFN, own), SplitStream(k, "ffn", own, "norm2_e")
        gate, hid = k.sb("ffn_gate", [P, MF, T], own), k.sb("ffn_hidden", [P, MF, T], own)
        hid_hi, hid_lo = k.sb("ffn_hid_hi", [P, 2, MF, T], own, F32R), k.sb("ffn_hid_lo", [P, 2, MF, T], own, F32R)
        block = own.enter_context(k.nc.Block())
        flat = lambda a: a.rearrange("p m t -> p (m t)")
        pieces = 4 * len(DENSE_ORDER)

        @block.sync
        def _(sp):
            k.load_chunks(sp, O_IN + SLOTS)

        @block.tensor
        def _(pe):
            for j in range(pieces):
                kind, c = DENSE_ORDER[j // 4]
                if j % 4 == 0 and kind == "down":
                    pe.wait_ge(s.hid_ready, c + 1)
                elif j % 4 == 0 and c >= 1:
                    pe.wait_ge(s.gate_kept if kind == "gate" else s.multiplied, c)
                if j < 4:
                    pe.wait_ge(x.ready, j + 1)
                pe.wait_ge(w.lo_ready, j + 1)
                if kind == "down":
                    f = j % 4
                    for m in range(KT):
                        ins = three(pe, k.bank(4 + m // 2)[:, (m % 2) * T:(m % 2 + 1) * T], w.hi_of(j)[:, m * P:(m + 1) * P],
                                    w.lo_of(j)[:, m * P:(m + 1) * P], hid_hi[:, c % 2, f, :], hid_lo[:, c % 2, f, :], c == 0 and f == 0 and m % 2 == 0)
                else:
                    ins = product(pe, k.bank(0 if kind == "gate" else 2, 2), w, x, j)
                ins.then_inc(w.used, 1)
                if j % 4 == 3:
                    pe.sem_inc(k.chunk_used, 1)

        @block.scalar
        def _(act):
            for j in range(pieces + 1):
                for c in range(FC):
                    if j == last_piece("gate", c, DENSE_ORDER) + DENSE_SPLIT:
                        act.wait_ge(w.used, last_piece("gate", c, DENSE_ORDER) + 1)
                        if c >= 1:
                            act.wait_ge(s.multiplied, c)
                        act.activation(flat(gate[:, :, :]), k.bank(0, 2), ACT.Silu).then_inc(s.gate_kept, 1)
                    if j == min(last_piece("up", c, DENSE_ORDER) + DENSE_SPLIT + 1, pieces):
                        act.wait_ge(s.multiplied, c + 1)
                        act.copy(hid_hi[:, c % 2, :, :], hid[:, :, :]).then_inc(s.hid_hi, 1)
                if 1 <= j < 5:
                    x.hi(act, j - 1)
                if j < pieces:
                    w.hi(act, j)

        @block.vector
        def _(dve):
            for i in range(2):
                x.normalise(dve, i)
            for j in range(pieces + 1):
                for c in range(FC):
                    if j == last_piece("up", c, DENSE_ORDER) + DENSE_SPLIT:
                        dve.wait_ge(w.used, last_piece("up", c, DENSE_ORDER) + 1)
                        dve.wait_ge(s.gate_kept, c + 1)
                        if c >= 1:
                            dve.wait_ge(s.hid_ready, c)
                        dve.tensor_tensor(flat(hid[:, :, :]), flat(gate[:, :, :]), k.bank(2, 2), ALU.mult).then_inc(s.multiplied, 1)
                    if j == min(last_piece("up", c, DENSE_ORDER) + DENSE_SPLIT + 1, pieces):
                        dve.wait_ge(s.hid_hi, c + 1)
                        dve.tensor_tensor(hid_lo[:, c % 2, :, :], hid[:, :, :], hid_hi[:, c % 2, :, :].bitcast(F32), ALU.subtract).then_inc(s.hid_ready, 1)
                if j < pieces:
                    w.lo(dve, j)
                if j < 4:
                    x.lo(dve, j)
                if j < 2:
                    x.normalise(dve, j + 2)
            dve.wait_ge(w.used, pieces)
            for i in range(2):
                r = flat(k.res[:, 4 * i:4 * i + 4, :])
                dve.tensor_tensor(r, r, k.bank(4 + 2 * i, 2), ALU.add).then_inc(s.added, 1)
            dve.wait_ge(s.added, 2)


def odd_mixer(k):
    with ExitStack() as own:
        m = Names(**{n: k.sb("o_" + n, [P, 4, T], own) for n in (
            "r",
            "kh",
            "a",
            "kk",
            "v", "g",
            "bonus")},
            chunk_decay=k.sb("o_chunk_decay", [P, 4, RN], own))
        with ExitStack() as early:
            e = Names(**{n: k.sb("o_" + n, [P, 4, T], early) for n in ("ret_q", "ret_k", "ret_g")},
                      ret_v=k.sb("o_ret_v", [P, TH, CH], early), consts=k.sb("o_ret_consts", [P, RET_N], early))
            odd_project(k, m, e)
            retention(k, e)
        rwkv(k, m)


def odd_project(k, m, e):
    nc, g = k.nc, k.g
    s = Names(**{n: k.sem("op_" + n) for n in (
        "loaded", "zeroed", "proj_kept", "mixed_low", "low_ready", "up_done", "extra_kept", "decay_summed", "exp_ready",
        "kk_squared", "bonus_ready", "dve_chain", "chunk_read")})
    rc = lambda n: e.consts[:, RET_AT[n][0]:RET_AT[n][1]]
    with ExitStack() as own:
        sb = lambda n, shape: k.sb("op_" + n, shape, own)
        w, x = SplitWeights(k, "op", O_IN, own), SplitStream(k, "op", own, "norm1_o")
        ups = sb("ups", [P, 3, CH])
        pads = sb("pads", [P, 2, 4, T + 1])
        lowp = sb("low_pads", [P, 2, T + 1])
        low = sb("low", [P, 2, T])
        lw, b, en = sb("log_w", [P, 4, T]), sb("sum_w", [P, 4, T]), sb("exp_minus", [P, 4, T])
        block = own.enter_context(nc.Block())
        flat = lambda a: a.rearrange("p m t -> p (m t)")

        @block.sync
        def _(sp):
            sp.dma_start(e.consts[:, :], g.ret_consts).then_inc(s.loaded, 16)
            sp.wait_ge(s.zeroed, 1)
            sp.dma_start(ups[0:64, 0, :], g.o_rw_w_up[0]).then_inc(s.loaded, 16)
            sp.dma_start(ups[64:P, 1, :], g.o_rw_a_up[0]).then_inc(s.loaded, 16)
            sp.dma_start(ups[:, 2, :], g.o_rw_g_up[0]).then_inc(s.loaded, 16)
            k.load_chunks(sp, O_OUT + SLOTS)

        @block.gpsimd
        def _(pool):
            pool.memset(ups[:, :, :], 0.0).then_inc(s.zeroed, 1)
            pool.memset(pads[:, :, :, 0:1], 0.0).then_inc(s.zeroed, 1)
            pool.memset(lowp[:, :, 0:1], 0.0).then_inc(s.zeroed, 1)
            for j in range(4 * 8):
                w.lo(pool, j)

        @block.tensor
        def _(pe):
            def extra(i, lhsT, rhs, ready, value, tiles=4):
                pe.wait_ge(ready, value)
                if i:
                    pe.wait_ge(s.extra_kept, i)
                for t in range(tiles):
                    ins = pe.matmul(k.bank(6, 2)[:, t * T:(t + 1) * T], lhsT(t), rhs(t), start=True, stop=True)
                ins.then_inc(s.up_done, 1)

            head = lambda t: k.c("head_ones")
            up = lambda i: lambda t: ups[:, i, t * P:(t + 1) * P]
            for i in range(8):
                if i >= 3:
                    pe.wait_ge(s.proj_kept, i - 2)
                project(pe, k, w, x, i, k.bank(2 * (i % 3), 2), tokens_out=i == 6, m_tiles=2 if i == 0 else 4)
                if i == 1:
                    pe.wait_ge(s.loaded, 64)
                    extra(0, up(0), lambda t: low[:, 0, :], s.low_ready, 3)
                if i == 2:
                    extra(1, up(1), lambda t: low[:, 0, :], s.low_ready, 3)
                if i == 3:
                    extra(2, head, lambda t: en[:, t, :], s.kk_squared, 1)
                if i == 4:
                    extra(3, up(2), lambda t: low[:, 1, :], s.low_ready, 3)
                if i == 5:
                    extra(4, head, lambda t: m.bonus[:, t, :], s.bonus_ready, 1)

        @block.scalar
        def _(act):
            def keep(i, dst):
                for j in range(4 * i + 3, min(4 * i + 7, 32)):
                    w.hi(act, j)
                act.wait_ge(w.used, 4 * i + 4)
                act.copy(dst, k.bank(2 * (i % 3), 2).rearrange("p (m t) -> p m t", t=dst.shape[2])[:, 0:dst.shape[1], :])\
                   .then_inc(s.proj_kept, 1)

            for j in range(4):
                if j < 3:
                    w.hi(act, j)
                x.hi(act, j)
            act.wait_ge(s.zeroed, 3)
            keep(0, lowp[:, :, 1:])
            act.wait_ge(s.mixed_low, 1)
            act.activation(low[0:64, 0, :], low[0:64, 0, :], ACT.Tanh).then_inc(s.low_ready, 2)
            act.activation(low[:, 1, :], low[:, 1, :], ACT.Sigmoid).then_inc(s.low_ready, 1)
            keep(1, pads[:, 0, :, 1:])
            act.wait_ge(s.up_done, 1)
            for t in range(4):
                ins = act.activation(lw[:, t, :], k.bank(6, 2)[:, t * T:(t + 1) * T], ACT.Sigmoid, bias=k.p("w0", t))
            ins.then_inc(s.extra_kept, 1)
            keep(2, pads[:, 1, :, 1:])
            act.wait_ge(s.up_done, 2)
            for t in range(4):
                ins = act.activation(m.a[:, t, :], k.bank(6, 2)[:, t * T:(t + 1) * T], ACT.Sigmoid, bias=k.p("a0", t))
            ins.then_inc(s.extra_kept, 1)
            act.wait_ge(s.chunk_read, 1)
            keep(3, pads[:, 0, :, 1:])
            act.wait_ge(s.up_done, 3)
            act.activation(flat(en[:, :, :]), k.bank(6, 2), ACT.Sqrt).then_inc(s.extra_kept, 1)
            keep(4, e.ret_q[:, :, :])
            act.wait_ge(s.up_done, 4)
            act.copy(flat(m.g[:, :, :]), k.bank(6, 2)).then_inc(s.extra_kept, 1)
            keep(5, e.ret_k[:, :, :])
            act.wait_ge(s.decay_summed, 2)
            act.activation(en[:, :, :], b[:, :, :], ACT.Exp, scale=-1.0).then_inc(s.exp_ready, 1)
            act.wait_ge(s.exp_ready, 1)
            act.activation(b[:, :, :], b[:, :, :], ACT.Exp).then_inc(s.exp_ready, 1)
            act.activation(lw[:, :, :], lw[:, :, :], ACT.Exp).then_inc(s.exp_ready, 1)
            keep(6, e.ret_v[:, :, :])
            keep(7, e.ret_g[:, :, :])
            act.wait_ge(s.proj_kept, 8)

        @block.vector
        def _(dve):
            step = counted(dve, s.dve_chain)

            def shift_mix(dst, src, mu, tiles):
                step(dve.tensor_tensor(dst, src[:, :, 0:T], src[:, :, 1:], ALU.subtract))
                for t in range(tiles):
                    ins = dve.scalar_tensor_tensor(out=dst[:, t, :], in0=dst[:, t, :], scalar=k.p("mu", mu + t),
                                                   in1=src[:, t, 1:], op0=ALU.mult, op1=ALU.add)
                    if t < tiles - 1:
                        step(ins)
                return ins

            x.normalise_and_lo(dve)
            dve.wait_ge(s.proj_kept, 1)
            shift_mix(low[:, :, :], lowp[:, :, :], 12, 2).then_inc(s.mixed_low, 1)
            dve.wait_ge(s.proj_kept, 2)
            shift_mix(m.kh[:, :, :], pads[:, 0, :, :], 4, 4).then_inc(s.chunk_read, 1)
            dve.wait_ge(s.chunk_read, 1)
            for t in range(4):
                step(dve.tensor_scalar(m.kk[:, t, :], m.kh[:, t, :], k.p("k_k", t), None, ALU.mult))
            dve.tensor_tensor(en[:, :, :], m.kk[:, :, :], m.kk[:, :, :], ALU.mult).then_inc(s.kk_squared, 1)
            dve.wait_ge(s.extra_kept, 1)
            step(dve.tensor_scalar(lw[:, :, :], lw[:, :, :], -float(np.exp(-0.5)), None, ALU.mult))
            for t in range(4):
                step(dve.tensor_tensor_scan(b[:, t, :], rc("reset64"), lw[:, t, :], 0.0, ALU.mult, ALU.add))
            step(dve.tensor_tensor(lw[:, :, :], b[:, :, :], lw[:, :, :], ALU.subtract))
            dve.wait_ge(s.proj_kept, 3)
            step(shift_mix(m.r[:, :, :], pads[:, 1, :, :], 0, 4))
            dve.wait_ge(s.extra_kept, 2)
            for t in range(4):
                step(dve.tensor_scalar(m.bonus[:, t, :], m.a[:, t, :], -1.0, k.p("k_a", t), ALU.add, ALU.mult))
            step(dve.scalar_tensor_tensor(out=flat(m.kh[:, :, :]), in0=flat(m.bonus[:, :, :]), scalar=1.0, in1=flat(m.kh[:, :, :]),
                                          op0=ALU.add, op1=ALU.mult))
            for t in range(4):
                ins = dve.scalar_tensor_tensor(out=m.bonus[:, t, :], in0=m.r[:, t, :], scalar=k.p("r_k", t),
                                               in1=m.kh[:, t, :], op0=ALU.mult, op1=ALU.mult)
                if t < 3:
                    step(ins)
            ins.then_inc(s.bonus_ready, 1)
            dve.wait_ge(s.proj_kept, 4)
            step(shift_mix(m.v[:, :, :], pads[:, 0, :, :], 8, 4))
            dve.wait_ge(s.extra_kept, 3)
            step(dve.tensor_scalar(en[:, :, :], en[:, :, :], 1e-12, None, ALU.max))
            step(dve.reciprocal(en[:, :, :], en[:, :, :]))
            dve.tensor_tensor(m.kk[:, :, :], m.kk[:, :, :], en[:, :, :], ALU.mult).then_inc(s.decay_summed, 2)
            dve.wait_ge(s.decay_summed, 2)
            step(dve.tensor_tensor(m.a[:, :, :], m.a[:, :, :], m.kk[:, :, :], ALU.mult))
            dve.wait_ge(s.up_done, 5)
            step(dve.tensor_tensor(flat(m.bonus[:, :, :]), k.bank(6, 2), flat(m.v[:, :, :]), ALU.mult))
            dve.wait_ge(s.exp_ready, 3)
            step(dve.tensor_tensor(m.r[:, :, :], m.r[:, :, :], b[:, :, :], ALU.mult))
            step(dve.scalar_tensor_tensor(out=flat(m.kk[:, :, :]), in0=flat(m.kk[:, :, :]), scalar=-1.0, in1=flat(lw[:, :, :]),
                                          op0=ALU.mult, op1=ALU.mult))
            step(dve.tensor_tensor(m.kh[:, :, :], m.kh[:, :, :], en[:, :, :], ALU.mult))
            step(dve.tensor_tensor(m.a[:, :, :], m.a[:, :, :], en[:, :, :], ALU.mult))
            step(dve.tensor_copy(m.chunk_decay[:, :, :], b[:, :, RC - 1::RC]))


def retention(k, e):
    nc = k.nc
    s = Names(**{n: k.sem("rt_" + n) for n in (
        "turned", "rotated", "scored", "p_ready", "o_done", "o_kept", "mean_done", "centred", "squared", "var_done",
        "rooted", "gated", "dve_chain")})
    rc = lambda n: e.consts[:, RET_AT[n][0]:RET_AT[n][1]]
    with ExitStack() as own:
        wts = k.sb("rt_wts", [P, 4, T + P], own)
        ot, tmp = (k.sb("rt_" + n, [P, 4, T], own) for n in ("ot", "tmp"))
        block = own.enter_context(nc.Block())
        flat = lambda a: a.rearrange("p m t -> p (m t)")

        @block.sync
        def _(sp):
            k.load_chunks(sp, O_OUT + SLOTS)

        @block.tensor
        def _(pe):
            for i, src in enumerate((e.ret_q, e.ret_k)):
                for j in range(2):
                    ins = pe.matmul(k.bank(2 * i + j), rc("rot"), src[:, 2 * j:2 * j + 2, :], start=True, stop=True)
                ins.then_inc(s.turned, 1)
            pe.wait_ge(s.rotated, 2)
            for hd in range(4):
                b = k.bank(4 + hd)
                pe.matmul(b[:, 0:T], e.ret_k[:, hd, 0:P], e.ret_q[:, hd, :], start=True, stop=True)
                pe.matmul(b[:, T:T + P], e.ret_k[:, hd, P:T], e.ret_q[:, hd, P:T], start=True, stop=True).then_inc(s.scored, 1)
            for hd in range(4):
                pe.wait_ge(s.p_ready, hd + 1)
                cols = slice(hd * P, (hd + 1) * P)
                b = k.bank(hd)
                pe.matmul(b[:, 0:T], e.ret_v[:, 0, cols], wts[:, hd, 0:T], start=True, stop=False, skip_group_check=True)
                pe.matmul(b[:, P:T], e.ret_v[:, 1, cols], wts[:, hd, T:T + P], start=False, stop=True,
                          skip_group_check=True).then_inc(s.o_done, 1)
            pe.wait_ge(s.o_kept, 4)
            for i in range(2):
                ins = pe.matmul(k.bank(4 + i), k.c("mean"), ot[:, 2 * i:2 * i + 2, :], start=True, stop=True)
            ins.then_inc(s.mean_done, 1)
            pe.wait_ge(s.squared, 1)
            for i in range(2):
                ins = pe.matmul(k.bank(6 + i), k.c("mean"), tmp[:, 2 * i:2 * i + 2, :], start=True, stop=True)
            ins.then_inc(s.var_done, 1)

        @block.scalar
        def _(act):
            act.activation(e.ret_g[:, :, :], e.ret_g[:, :, :], ACT.Silu).then_inc(s.gated, 1)
            for hd in range(4):
                act.wait_ge(s.o_done, hd + 1)
                act.copy(ot[:, hd, :], k.bank(hd)[:, 0:T]).then_inc(s.o_kept, 1)
            act.wait_ge(s.centred, 1)
            act.activation(tmp[:, :, :], ot[:, :, :], ACT.Square).then_inc(s.squared, 1)
            act.wait_ge(s.var_done, 1)
            act.activation(tmp[:, :, :], k.bank(6, 2).rearrange("p (h t) -> p h t", h=4), ACT.Ln, bias=k.p("eps")).then_inc(s.rooted, 1)
            act.wait_ge(s.rooted, 1)
            act.activation(tmp[:, :, :], tmp[:, :, :], ACT.Exp, scale=-0.5).then_inc(s.rooted, 1)

        @block.vector
        def _(dve):
            step = counted(dve, s.dve_chain)
            with_cos = (ot[:, :, :], wts[:, :, 0:T])
            for x, dst in zip((e.ret_q, e.ret_k), with_cos):
                step(dve.tensor_tensor(dst, x[:, :, :], bc(rc("cos"), 1, 4), ALU.mult))
            for i, x in enumerate((e.ret_q, e.ret_k)):
                dve.wait_ge(s.turned, i + 1)
                step(dve.tensor_tensor(tmp[:, :, :], k.bank(2 * i, 2).rearrange("p (m t) -> p m t", m=4), bc(rc("sin"), 1, 4), ALU.mult))
                dve.tensor_tensor(x[:, :, :], with_cos[i], tmp[:, :, :], ALU.add).then_inc(s.rotated, 1)
                dve.wait_ge(s.rotated, i + 1)
            decay = rc("decay").rearrange("p (h t) -> p h t", h=4)
            for hd in range(4):
                dve.wait_ge(s.scored, hd + 1)
                step(dve.tensor_tensor(wts[:, hd, 0:T], k.bank(4 + hd)[:, 0:T], decay[:, hd, :], ALU.mult))
                dve.tensor_tensor(wts[:, hd, T:T + P], k.bank(4 + hd)[:, T:T + P], decay[:, hd, 0:P], ALU.mult).then_inc(s.p_ready, 1)
            dve.wait_ge(s.mean_done, 1)
            dve.wait_ge(s.o_kept, 4)
            dve.tensor_tensor(flat(ot[:, :, :]), flat(ot[:, :, :]), k.bank(4, 2), ALU.subtract).then_inc(s.centred, 1)
            dve.wait_ge(s.centred, 1)
            dve.wait_ge(s.squared, 1)
            dve.wait_ge(s.gated, 1)
            for hd in range(4):
                step(dve.scalar_tensor_tensor(out=ot[:, hd, :], in0=ot[:, hd, :], scalar=k.p("ret_norm", hd),
                                              in1=e.ret_g[:, hd, :], op0=ALU.mult, op1=ALU.mult))
            dve.wait_ge(s.rooted, 2)
            step(dve.tensor_tensor(k.h[:, 0:4, :], tmp[:, :, :], ot[:, :, :], ALU.mult))


def rwkv(k, m):
    nc, g = k.nc, k.g
    s = Names(**{n: k.sem("rw_" + n) for n in (
        "loaded", "gram_done", "gram_kept", "padded", "turned", "v_kept", "rows_kept", "w1_done", "w1_kept", "off_ready",
        "u_done", "u_kept", "dx_done", "x_ready", "xa_done", "xa_kept", "q_done", "q_kept", "m_kept", "state_done",
        "state_ready", "y_done", "y_kept", "dve_chain", "act_chain", "mean_done", "centred", "squared",
        "var_done", "rooted")})
    HD = 8
    with ExitStack() as own:
        sb = lambda n, shape: k.sb("rw_" + n, shape, own)
        consts = sb("consts", [P, RW_N])
        gram = sb("gram", [P, HD, 4, P])
        ar = sb("ar", [P, HD, 2, P])
        vp = sb("vp", [P, HD, P])
        aw = sb("aw", [P, HD, 2, 64])
        bk = sb("bk", [P, 2, 2, CH])
        x, xt = sb("x", [P, HD, P]), sb("xt", [P, HD, P])
        u, off = sb("u", [P, HD, P]), sb("off", [P, HD, P])
        xa, xw, mt = u, off, x
        q = sb("q", [P, 4, P])
        grown = sb("grown", [P, 4, P])
        state = sb("state", [P, 3, 4, P])
        wc = lambda n: consts[:, RW_AT[n][0]:RW_AT[n][1]]
        block = own.enter_context(nc.Block())
        L = len(LEVELS)
        pair_cols = lambda t, p: t[:, 2 * p:2 * p + 2, :].rearrange("p h c -> p (h c)")[:, 0:T].rearrange(
            "p (a c) -> p a c", c=64)[:, 0::3, :]

        @block.sync
        def _(sp):
            sp.dma_start(consts[:, :], g.rw_consts).then_inc(s.loaded, 16)
            k.load_chunks(sp, O_OUT + SLOTS)

        @block.gpsimd
        def _(pool):
            pool.memset(ar[:, 4:8, :, :], 0.0).then_inc(s.padded, 1)
            pool.memset(state[:, 0, :, :], 0.0).then_inc(s.state_ready, 1)
            pool.wait_ge(s.loaded, 16)
            pool.wait_ge(s.state_ready, 1)
            for a in range(TH):
                half = slice(a * P, (a + 1) * P)
                for hd in range(2 if a else 0):
                    pool.wait_ge(s.gram_done, HD)
                    rows = slice(64 * hd, 64 * hd + 64)
                    for i, src in enumerate((m.kk, m.r)):
                        pool.tensor_copy(ar[rows, hd::2, i, :], src[rows, :, half]).then_inc(s.padded, 1)
                        pool.wait_ge(s.padded, 3 + 4 * a + 2 * hd + i)
                for lv in range(L):
                    for grp in range(2):
                        hs = slice(4 * grp, 4 * grp + 4)
                        if lv == 0:
                            pool.wait_ge(s.gram_kept, HD * a + 4 * grp + 4)
                            if a:
                                pool.wait_ge(s.y_done, 1)
                        else:
                            pool.wait_ge(s.u_done, 2 * (L * a + lv - 1) + grp + 1)
                            if lv == 1:
                                pool.wait_ge(s.x_ready, 2 * L * a + grp + 1)
                        pool.tensor_tensor(off[:, hs, :], gram[:, hs, 0, :], bc(wc("levels")[:, lv * P:(lv + 1) * P], 1, 4),
                                           ALU.mult).then_inc(s.off_ready, 1)
                pool.wait_ge(s.off_ready, 2 * L * (a + 1))

        @block.tensor
        def _(pe):
            for a in range(TH):
                half = slice(a * P, (a + 1) * P)
                pe.wait_ge(s.padded, 6 + 4 * a)
                if a:
                    pe.wait_ge(s.y_kept, 1)
                    pe.wait_ge(s.state_ready, 3)
                for h in range(HD):
                    pe.matmul(k.bank(h)[:, 0:T], m.a[:, h // 2, half], ar[:, h, :, :], start=True, stop=True)
                    pe.matmul(k.bank(h)[:, T:2 * T], m.kh[:, h // 2, half], ar[:, h, :, :], start=True, stop=True).then_inc(s.gram_done, 1)
                pe.wait_ge(s.gram_kept, HD * (a + 1))
                for i, src in enumerate((m.v, m.kk, m.a, m.kh)):
                    for p in range(4):
                        ins = pe.transpose(k.bank(i)[:, p * P:(p + 1) * P], src[:, p, half], k.c("ident"))
                    ins.then_inc(s.turned, 1)
                pe.wait_ge(s.v_kept, a + 1)
                for h in range(HD):
                    ins = pe.matmul(k.bank(4)[:, h * 64:(h + 1) * 64], gram[:, h, 2, :], vp[:, h, (h % 2) * 64:(h % 2) * 64 + 64],
                                    start=True, stop=True)
                ins.then_inc(s.w1_done, 1)
                for lv in range(L):
                    for grp in range(2):
                        pe.wait_ge(s.off_ready, 2 * (L * a + lv) + grp + 1)
                        if lv or a:
                            pe.wait_ge(s.x_ready, 2 * (L * a + lv - 1) + grp + 1)
                        if a == 1 and lv == 0:
                            pe.wait_ge(s.y_done, 1)
                        for h in range(4 * grp, 4 * grp + 4):
                            ins = pe.matmul(k.bank(6 + grp)[:, (h % 4) * P:(h % 4 + 1) * P], off[:, h, :],
                                            x[:, h, :] if lv else k.c("ident"), start=True, stop=True)
                        ins.then_inc(s.u_done, 1)
                    if lv == 0:
                        continue
                    for grp in range(2):
                        pe.wait_ge(s.u_kept, 2 * ((L - 1) * a + lv - 1) + grp + 1)
                        if lv == 1:
                            pe.wait_ge(s.rows_kept, a + 1)
                        for h in range(4 * grp, 4 * grp + 4):
                            cols = slice((h % 4) * P, (h % 4 + 1) * P)
                            if lv < L - 1:
                                pe.matmul(k.bank(2 * grp)[:, cols], xt[:, h, :], u[:, h, :], start=True, stop=True)
                            ins = pe.matmul(k.bank(2 * grp + 1)[:, cols], u[:, h, :], xt[:, h, :], start=True, stop=True)
                        ins.then_inc(s.dx_done, 1)
                pe.wait_ge(s.w1_kept, a + 1)
                pe.wait_ge(s.x_ready, 2 * L * (a + 1))
                for h in range(HD):
                    ins = pe.matmul(k.bank(4 + h // 4)[:, (h % 4) * P:(h % 4 + 1) * P], xt[:, h, :], aw[:, h, :, :], start=True, stop=True)
                ins.then_inc(s.xa_done, 1)
                pe.wait_ge(s.xa_kept, a + 1)
                for p in range(4):
                    for h in (2 * p, 2 * p + 1):
                        ins = pe.matmul(k.bank(6)[:, p * P:(p + 1) * P], xa[:, h, :], gram[:, h, 1, :], start=h % 2 == 0, stop=h % 2 == 1)
                for p in range(4):
                    for c in range(2):
                        for h in (2 * p, 2 * p + 1):
                            ins = pe.matmul(k.bank(c)[:, p * P:(p + 1) * P], xa[:, h, :], bk[:, 0, c, p * P:(p + 1) * P],
                                            start=h % 2 == 0, stop=h % 2 == 1)
                ins.then_inc(s.q_done, 1)
                pe.wait_ge(s.m_kept, a + 1)
                for n in range(2 * a, min(2 * a + 2, RN - 1)):
                    c = n - 2 * a
                    pe.wait_ge(s.state_ready, n + 1)
                    for p in range(4):
                        out = k.bank(2 + c)[:, p * P:(p + 1) * P]
                        cols = slice(p * P, (p + 1) * P)
                        pe.matmul(out, bk[:, 0, c, cols], pair_cols(xw, p), start=True, stop=False)
                        pe.matmul(out, bk[:, 1, c, cols], pair_cols(vp, p), start=False, stop=False)
                        ins = pe.matmul(out, mt[:, 4 * c + p, :], state[:, n % 3, p, :], start=False, stop=True)
                    ins.then_inc(s.state_done, 1)
                pe.wait_ge(s.q_kept, a + 1)
                pe.wait_ge(s.state_ready, 2 * a + 2)
                for p in range(4):
                    out = k.bank(7)[:, p * P:(p + 1) * P]
                    for h in (2 * p, 2 * p + 1):
                        pe.matmul(out, xw[:, h, :], gram[:, h, 1, :], start=h % 2 == 0, stop=False, skip_group_check=True)
                        pe.matmul(out, vp[:, h, :], gram[:, h, 3, :], start=False, stop=False, skip_group_check=True)
                    for c in range(2):
                        ins = pe.matmul(out[:, c * 64:(c + 1) * 64], state[:, (2 * a + c) % 3, p, :], q[:, p, c * 64:(c + 1) * 64],
                                        start=False, stop=True, skip_group_check=True)
                ins.then_inc(s.y_done, 1)
            pe.wait_ge(s.y_kept, 2)
            for i in range(2):
                ins = pe.matmul(k.bank(i), k.c("head_mean"), k.h[:, 4 + 2 * i:6 + 2 * i, :], start=True, stop=True)
            ins.then_inc(s.mean_done, 1)
            pe.wait_ge(s.squared, 1)
            for i in range(2):
                ins = pe.matmul(k.bank(2 + i), k.c("head_mean"), gram[:, i, :, :], start=True, stop=True)
            ins.then_inc(s.var_done, 1)

        @block.scalar
        def _(act):
            astep = counted(act, s.act_chain)
            for a in range(TH):
                act.wait_ge(s.turned, 4 * a + 4)
                astep(act.copy(aw[:, :, 0, :], k.bank(1).rearrange("p (h c) -> p h c", c=64)))
                for i in range(2):
                    for c in range(2):
                        ins = act.activation(bk[:, i, c, :], k.bank(2 + i), ACT.Copy, scale=k.c("parity")[:, c:c + 1])
                        if (i, c) != (1, 1):
                            astep(ins)
                ins.then_inc(s.rows_kept, 1)
                act.wait_ge(s.w1_done, a + 1)
                act.copy(aw[:, :, 1, :], k.bank(4).rearrange("p (h c) -> p h c", c=64)).then_inc(s.w1_kept, 1)
                for lv in range(1, L):
                    for grp in range(2):
                        act.wait_ge(s.u_done, 2 * (L * a + lv) + grp + 1)
                        act.copy(u[:, 4 * grp:4 * grp + 4, :], k.bank(6 + grp).rearrange("p (h c) -> p h c", c=P)).then_inc(s.u_kept, 1)
                act.wait_ge(s.y_done, a + 1)
                act.copy(k.h[:, 4:8, a * P:(a + 1) * P], k.bank(7).rearrange("p (h c) -> p h c", c=P)).then_inc(s.y_kept, 1)
            act.wait_ge(s.centred, 1)
            act.activation(gram[:, :, :, :].rearrange("p a b c -> p (a b c)")[:, 0:4 * T], k.h[:, 4:8, :].rearrange("p a t -> p (a t)"), ACT.Square).then_inc(s.squared, 1)
            act.wait_ge(s.var_done, 1)
            rstd = gram[:, 0:2, :, :].rearrange("p a b c -> p (a b c)")
            act.activation(rstd, k.bank(2, 2), ACT.Ln, bias=k.p("rw_eps")).then_inc(s.rooted, 1)
            act.wait_ge(s.rooted, 1)
            act.activation(rstd, rstd, ACT.Exp, scale=-0.5).then_inc(s.rooted, 1)

        @block.vector
        def _(dve):
            step = counted(dve, s.dve_chain)
            dve.memset(ar[:, 0:4, :, :], 0.0).then_inc(s.padded, 1)
            dve.wait_ge(s.padded, 2)
            for hd in range(2):
                rows = slice(64 * hd, 64 * hd + 64)
                for i, src in enumerate((m.kk, m.r)):
                    dve.tensor_copy(ar[rows, hd::2, i, :], src[rows, :, 0:P]).then_inc(s.padded, 1)
            dve.wait_ge(s.loaded, 16)
            masks = consts[:, RW_AT["strict"][0]:RW_AT["upto"][1]].rearrange("p (b c) -> p b c", b=2)
            cols = wc("head_cols").rearrange("p (h c) -> p h c", h=2)
            for a in range(TH):
                for h in range(HD):
                    dve.wait_ge(s.gram_done, HD * a + h + 1)
                    dve.tensor_tensor(gram[:, h, :, :].rearrange("p (x y) c -> p x y c", x=2),
                                      k.bank(h).rearrange("p (x y c) -> p x y c", x=2, y=2), bc(masks, 1, 2), ALU.mult).then_inc(s.gram_kept, 1)
                dve.wait_ge(s.turned, 4 * a + 1)
                dve.tensor_tensor(vp[:, :, :].rearrange("p (q h) c -> p q h c", h=2),
                                  bc(k.bank(0).rearrange("p (q c) -> p q c", c=P), 2, 2), bc(cols, 1, 4), ALU.mult).then_inc(s.v_kept, 1)
                if a == 1:
                    for t in range(4):
                        step(dve.scalar_tensor_tensor(out=m.bonus[:, t, :], in0=m.bonus[:, t, :], scalar=k.p("ln_b", t),
                                                      in1=m.g[:, t, :], op0=ALU.add, op1=ALU.mult))
                        step(dve.tensor_scalar(m.g[:, t, :], m.g[:, t, :], k.p("ln_g", t), None, ALU.mult))
                for lv in range(L):
                    for grp in range(2):
                        hs = slice(4 * grp, 4 * grp + 4)
                        n = 2 * (L * a + lv) + grp + 1
                        if lv == 0:
                            ident = bc(k.c("ident"), 1, 4)
                            dve.wait_ge(s.off_ready, n)
                            step(dve.tensor_tensor(xt[:, hs, :], off[:, hs, :], ident, ALU.add))
                            dve.wait_ge(s.u_done, n)
                            dve.tensor_tensor(x[:, hs, :], k.bank(6 + grp).rearrange("p (h c) -> p h c", c=P), ident, ALU.add).then_inc(s.x_ready, 1)
                            continue
                        dve.wait_ge(s.dx_done, 2 * ((L - 1) * a + lv - 1) + grp + 1)
                        if lv < L - 1:
                            step(dve.tensor_tensor(x[:, hs, :], x[:, hs, :], k.bank(2 * grp).rearrange("p (h c) -> p h c", c=P), ALU.add))
                        dve.tensor_tensor(xt[:, hs, :], xt[:, hs, :], k.bank(2 * grp + 1).rearrange("p (h c) -> p h c", c=P), ALU.add).then_inc(s.x_ready, 1)
                dve.wait_ge(s.xa_done, a + 1)
                for hd in range(2):
                    for i, dst in enumerate((xa, xw)):
                        src = k.bank(4, 2).rearrange("p (q h i c) -> p q h i c", q=4, h=2, i=2)[:, :, hd, i, :]
                        ins = dve.tensor_tensor(dst[:, hd::2, :].rearrange("p q (r c) -> p q r c", r=2), bc(src, 2, 2),
                                                bc(cols[:, hd, :].rearrange("p (r c) -> p r c", r=2), 1, 4), ALU.mult)
                        if (hd, i) != (1, 1):
                            step(ins)
                ins.then_inc(s.xa_kept, 1)
                dve.wait_ge(s.q_done, a + 1)
                dve.tensor_tensor(mt[:, :, :].rearrange("p n c -> p (n c)").rearrange("p (n c) -> p n c", c=P),
                                  k.bank(0, 2).rearrange("p (n c) -> p n c", c=P), bc(k.c("head_ones"), 1, 8), ALU.mult).then_inc(s.m_kept, 1)
                dve.tensor_tensor(q[:, :, :], k.bank(6).rearrange("p (n c) -> p n c", c=P), m.r[:, :, a * P:(a + 1) * P], ALU.add).then_inc(s.q_kept, 1)
                for n in range(2 * a, min(2 * a + 2, RN - 1)):
                    c = n - 2 * a
                    dve.wait_ge(s.state_done, n + 1)
                    if n == 2:
                        dve.wait_ge(s.y_done, 1)
                    step(dve.tensor_tensor(grown[:, :, :], k.bank(2 + c).rearrange("p (n c) -> p n c", c=P), state[:, n % 3, :, :], ALU.add))
                    step(dve.tensor_tensor(grown[:, :, :], grown[:, :, :], m.chunk_decay[:, :, n:n + 1].broadcast_to([P, 4, P]), ALU.mult))
                    dve.tensor_tensor(state[:, (n + 1) % 3, :, :], grown[:, :, :], bc(k.c("head_ones"), 1, 4), ALU.mult).then_inc(s.state_ready, 1)
            y = k.h[:, 4:8, :]
            flat = lambda t: t.rearrange("p m t -> p (m t)")
            tmp = gram[:, 0:2, :, :].rearrange("p a b c -> p (a b c)").rearrange("p (m t) -> p m t", m=4)
            dve.wait_ge(s.mean_done, 1)
            dve.tensor_tensor(flat(y), flat(y), k.bank(0, 2), ALU.subtract).then_inc(s.centred, 1)
            dve.wait_ge(s.centred, 1)
            dve.wait_ge(s.squared, 1)
            step(dve.tensor_tensor(y, y, m.g[:, :, :], ALU.mult))
            dve.wait_ge(s.rooted, 2)
            step(dve.tensor_tensor(y, y, tmp, ALU.mult))
            step(dve.tensor_tensor(y, y, m.bonus[:, :, :], ALU.add))


def route(k, x):
    nc, g = k.nc, k.g
    s = Names(**{n: k.sem("ro_" + n) for n in (
        "normalised", "logits_done", "rows_done", "rows_kept", "chosen", "places_done", "shifted", "exp_ready", "dve_chain")})
    with ExitStack() as own:
        sb = lambda n, shape: k.sb("ro_" + n, shape, own)
        lg, ez, w = sb("logits", [P, TH, E]), sb("exp", [P, TH, E]), sb("weights", [P, TH, E])
        above, same = sb("above", [P, E, E]), sb("same", [P, E, E])
        rank, top, total = sb("rank", [P, TH, E]), sb("top", [P, TH]), sb("total", [P, TH])
        most = sb("most", [P, 1])
        block = own.enter_context(nc.Block())

        @block.tensor
        def _(pe):
            for kt in range(KT):
                pe.wait_ge(s.normalised, kt + 1)
                for a in range(TH):
                    ins = pe.matmul(k.bank(4)[:, a * E:(a + 1) * E], k.h[:, kt, a * P:(a + 1) * P], k.router[:, kt, :],
                                    start=kt == 0 and a == 0, stop=kt == KT - 1, skip_group_check=True)
            ins.then_inc(s.logits_done, 1)
            for a in range(TH):
                for kt in range(KT):
                    ins = pe.transpose(k.bank(2 * a + kt // 4)[:, (kt % 4) * P:(kt % 4 + 1) * P], k.h[:, kt, a * P:(a + 1) * P], k.c("ident"))
                ins.then_inc(s.rows_done, 1)
            pe.wait_ge(s.chosen, 1)
            pe.matmul(k.bank(5)[:, 0:E], k.c("before"), x.chosen[:, 0, :], start=True, stop=True)
            pe.matmul(k.bank(5)[:, E:2 * E], k.c("ones"), x.chosen[:, 0, :], start=True, stop=False)
            pe.matmul(k.bank(5)[:, E:2 * E], k.c("before"), x.chosen[:, 1, :], start=False, stop=True)
            for a in range(TH):
                ins = pe.matmul(k.bank(5)[:, 2 * E:3 * E], k.c("ones"), x.chosen[:, a, :], start=a == 0, stop=a == 1)
            ins.then_inc(s.places_done, 1)

        @block.scalar
        def _(act):
            act.wait_ge(s.shifted, 1)
            act.activation(ez[:, :, :], ez[:, :, :], ACT.Exp).then_inc(s.exp_ready, 1)
            for a in range(TH):
                act.wait_ge(s.rows_done, a + 1)
                act.copy(x.rows[:, a, :], k.bank(2 * a, 2)).then_inc(s.rows_kept, 1)

        @block.vector
        def _(dve):
            step = counted(dve, s.dve_chain)
            for kt in range(KT):
                dve.scalar_tensor_tensor(out=k.h[:, kt, :], in0=k.res[:, kt, :], scalar=k.p("norm2_o", kt),
                                         in1=k.rstd[:, :], op0=ALU.mult, op1=ALU.mult).then_inc(s.normalised, 1)
            dve.wait_ge(s.logits_done, 1)
            step(dve.tensor_copy(lg[:, :, :], k.bank(4)[:, 0:TH * E].rearrange("p (a e) -> p a e", a=TH)))
            step(dve.tensor_reduce(top[:, :], lg[:, :, :], AX.X, ALU.max))
            dve.tensor_tensor(ez[:, :, :], lg[:, :, :], bc(top[:, :], 2, E), ALU.subtract).then_inc(s.shifted, 1)
            for a in range(TH):
                mine, other = bc(lg[:, a, :], 2, E), bc(lg[:, a, :], 1, E)
                step(dve.tensor_tensor(above[:, :, :], other, mine, ALU.is_gt))
                step(dve.tensor_tensor(same[:, :, :], other, mine, ALU.is_equal))
                step(dve.tensor_tensor(same[:, :, :], same[:, :, :], k.c("earlier").rearrange("p (e f) -> p e f", e=E), ALU.mult))
                step(dve.tensor_tensor(above[:, :, :], above[:, :, :], same[:, :, :], ALU.add))
                step(dve.tensor_reduce(rank[:, a, :], above[:, :, :], AX.X, ALU.add))
            dve.tensor_scalar(x.chosen[:, :, :], rank[:, :, :], float(TOP_K), None, ALU.is_lt).then_inc(s.chosen, 1)
            dve.wait_ge(s.chosen, 1)
            dve.wait_ge(s.exp_ready, 1)
            step(dve.tensor_tensor(w[:, :, :], ez[:, :, :], x.chosen[:, :, :], ALU.mult))
            step(dve.tensor_reduce(total[:, :], w[:, :, :], AX.X, ALU.add))
            step(dve.reciprocal(total[:, :], total[:, :]))
            step(dve.tensor_tensor(x.gate[:, :, :], w[:, :, :], bc(total[:, :], 2, E), ALU.mult))
            dve.wait_ge(s.places_done, 1)
            step(dve.tensor_copy(x.place[:, :, :], k.bank(5)[:, 0:2 * E].rearrange("p (a e) -> p a e", a=TH)))
            step(dve.tensor_reduce(most[:, :], k.bank(5)[:, 2 * E:3 * E], AX.X, ALU.max))
            step(dve.tensor_copy(x.most[:, :], most[:, :]))
            dve.wait_ge(s.rows_kept, TH)


TOP_K = 2
HOT_STEPS = 6
FREE = 1
X_RING = 14
X_SPLIT = 4
HALVES = 2 * len(FFN_ORDER)
PIECES = 2 * HALVES


def expert_half(k, e, i):
    g = k.g
    kind, c = FFN_ORDER[i // 2]
    w = {"gate": g.o_moe_w_gate, "up": g.o_moe_w_up, "down": g.o_moe_w_down}[kind][0]
    if kind == "down":
        r0 = c * CH + (i % 2) * CH // 2
        return w[bass.ds(e, 1), r0:r0 + CH // 2, :].rearrange("o (k p) c -> p (o k) c", p=P)
    r0 = (i % 2) * D // 2
    return w[bass.ds(e, 1), r0:r0 + D // 2, c * CH:(c + 1) * CH].rearrange("o (k p) c -> p (o k) c", p=P)


def expert_slot(k, i):
    j = i % X_RING
    if j < 2 * SLOTS:
        return k.ring[:, j // 2, (j % 2) * 2 * PIECE:(j % 2 + 1) * 2 * PIECE]
    return k.ring_more[:, j - 2 * SLOTS, :]


def load_expert_half(k, sp, e, i, before):
    if before + i >= X_RING:
        sp.wait_ge(k.lo_ready, 2 * (before + i - X_RING + 1) + PIECES * e)
    else:
        if i // 2 < SLOTS:
            sp.wait_ge(k.chunk_used, DENSE - (DENSE - 1 - i // 2) % SLOTS)
    w = expert_slot(k, i).rearrange("p (k c) -> p k c", k=2 if FFN_ORDER[i // 2][0] == "down" else 4)
    sp.dma_start(w, expert_half(k, e, i)).then_inc(k.half_filled[i % X_RING], 16)


def last_piece(kind, c, order=FFN_ORDER):
    return 4 * order.index((kind, c)) + 3


def turn_after(c):
    return last_piece("gate", c + 1) - 2 if c < FC - 1 else last_piece("up", c)


def flat2(a):
    return a.rearrange("p a b -> p (a b)")


def guarded(k, x, p, engine, program):
    if p == 0:
        return program()
    most = engine.value_load(x.most[0:1, 0:1], min_val=0, max_val=T)
    with engine.If(most > CAP * p):
        program()


def expert_tables(k, x, s, p):
    with ExitStack() as own:
        weighted = k.sb(f"expert_weighted{p}", [P, E, TH, CAP], own)
        here = x.here[:, :, 0:E]
        block = own.enter_context(k.nc.Block())

        @block.vector
        def _(dve):
            def program():
                if p == 0:
                    dve.memset(x.zeros[:, :], 0.0).then_inc(s.zeroed, 1)
                    dve.memset(x.here[:, :, E:E + 1], -1.0).then_inc(s.zeroed, 1)
                    dve.memset(x.scatter[:, 0, :], 0.0).then_inc(s.zeroed, 1)
                    dve.wait_ge(s.zeroed, 3)
                dve.scalar_tensor_tensor(out=here, in0=x.place[:, :, :], scalar=float(T), in1=x.chosen[:, :, :],
                                         op0=ALU.add, op1=ALU.mult).then_inc(s.hot, 1)
                dve.wait_ge(s.hot, HOT_STEPS * p + 1)
                dve.tensor_scalar(here, here, -float(T + CAP * p), None, ALU.add).then_inc(s.hot, 1)
                dve.wait_ge(s.hot, HOT_STEPS * p + 2)
                for a in range(TH):
                    w = weighted[:, :, a, :]
                    dve.tensor_tensor(w, bc(k.c("slots"), 1, E), bc(here[:, a, :], 2, CAP), ALU.is_equal).then_inc(s.hot, 1)
                    dve.wait_ge(s.hot, HOT_STEPS * p + 3 + 2 * a)
                    dve.tensor_tensor(w, w, bc(x.gate[:, a, :], 2, CAP), ALU.mult).then_inc(s.hot, 1)
            guarded(k, x, p, dve, program)

        @block.tensor
        def _(pe):
            def program():
                pe.wait_ge(s.hot, HOT_STEPS * (p + 1))
                for b in range(4):
                    for i in range(4):
                        ins = pe.transpose(k.bank(b)[0:CAP, i * P:(i + 1) * P], weighted[:, 2 * b + i // 2, i % 2, :], k.c("ident"))
                    ins.then_inc(s.scatter_turned, 1)
            guarded(k, x, p, pe, program)

        @block.scalar
        def _(act):
            def program():
                for b in range(4):
                    act.wait_ge(s.scatter_turned, 4 * p + b + 1)
                    act.copy(x.scatter[:, 2 * b + 1:2 * b + 3, :], k.bank(b)[0:CAP, :].rearrange("p (e t) -> p e t", e=2)).then_inc(s.scatter_kept, 1)
                act.wait_ge(s.scatter_kept, 4 * (p + 1))
            guarded(k, x, p, act, program)


def expert_pass(k, x, s, p):
    with ExitStack() as own:
        tile = lambda n, cols, dt: k.sb(f"expert_{n}{p}", [P, *cols], own, dt)
        w_hi, w_lo = tile("w_hi", [X_SPLIT, PIECE], F32R), tile("w_lo", [X_SPLIT, PIECE], F32R)
        tok_hi, tok_lo = tile("tok_hi", [KT, CAP], F32R), tile("tok_lo", [KT, CAP], F32R)
        hid_hi, hid_lo = tile("hid_hi", [MF, CAP], F32R), tile("hid_lo", [MF, CAP], F32R)
        hid = tile("hid", [MF * CAP], F32)
        y = flat2(k.h[:, 0:D // T, :])
        here_now, hot_now, scatter_now = tile("here_now", [TH, 1], F32), tile("hot_now", [TH, CAP], F32), tile("scatter_now", [T], F32)
        block = own.enter_context(k.nc.Block())
        x0 = E * p
        flat = lambda a: a.rearrange("p a b -> p (a b)")
        run = lambda engine, program: guarded(k, x, p, engine, program)

        @block.sync
        def _(sp):
            def program():
                if p:
                    for i in range(X_RING):
                        load_expert_half(k, sp, 0, i, HALVES * x0)
                with sp.Fori(0, E - 1) as e:
                    for i in range(X_RING, HALVES):
                        load_expert_half(k, sp, e, i, HALVES * x0)
                    for i in range(X_RING):
                        sp.wait_ge(k.lo_ready, 2 * (HALVES * (x0 + 1) + i - X_RING + 1) + PIECES * e)
                        w = expert_slot(k, i).rearrange("p (k c) -> p k c", k=2 if FFN_ORDER[i // 2][0] == "down" else 4)
                        sp.dma_start(w, expert_half(k, e + 1, i)).then_inc(k.half_filled[i], 16)
                for i in range(X_RING, HALVES):
                    load_expert_half(k, sp, E - 1, i, HALVES * x0)
            run(sp, program)

        @block.scalar
        def _(act):
            def keep_tokens(n, half):
                act.wait_ge(s.gathered, 2 * n - 1 + half)
                act.copy(flat(tok_hi[:, 4 * half:4 * half + 4, :]), k.bank(0)).then_inc(s.tokens_hi, 1)

            def keep_output(e):
                act.wait_ge(s.piece_used, X_SPLIT + PIECES * x0 + PIECES * e)
                act.wait_ge(s.out_done, FREE + (E + 1) * p + e)
                act.copy(y, k.bank(2, 2)).then_inc(s.y_kept, 1)

            def keep_hidden(n):
                act.wait_ge(s.turned, FREE + n)
                act.copy(flat(hid_hi[:, :, :]), k.bank(1)).then_inc(s.hid_hi, 1)

            def program():
                if p == 0:
                    act.sem_inc(s.gate_kept, FREE)
                for half in range(2):
                    keep_tokens((E + 1) * p + 1, half)
                with act.Fori(0, E) as e:
                    for j in range(PIECES):
                        if j == X_SPLIT:
                            keep_output(e)
                        for c in range(FC):
                            if j == last_piece("gate", c) + X_SPLIT:
                                act.wait_ge(s.piece_used, X_SPLIT + PIECES * x0 + last_piece("gate", c) + 1 + PIECES * e)
                                act.wait_ge(s.turned, FREE + FC * x0 + c + FC * e)
                                act.activation(hid[:, :], k.bank(0), ACT.Silu).then_inc(s.gate_kept, 1)
                            if c < FC - 1 and j == turn_after(c) + X_SPLIT:
                                if c == 0:
                                    act.wait_ge(s.piece_used, X_SPLIT + PIECES * x0 + PIECES * e)
                                keep_hidden(FC * x0 + c + 1 + FC * e)
                        if j == PIECES - 1:
                            keep_tokens((E + 1) * p + 2 + e, 0)
                            keep_hidden(FC * x0 + FC + FC * e)
                            keep_tokens((E + 1) * p + 2 + e, 1)
                        if j % 2 == 0:
                            act.wait_ge(k.half_filled[j // 2 % X_RING], 16 * (HALVES // X_RING * x0 + j // 2 // X_RING + 1) + 16 * (HALVES // X_RING) * e)
                        act.wait_ge(s.piece_used, PIECES * x0 + j + 1 + PIECES * e)
                        act.copy(w_hi[:, j % X_SPLIT, :], expert_slot(k, j // 2)[:, j % 2 * PIECE:(j % 2 + 1) * PIECE]).then_inc(s.hi_ready, 1)
                keep_output(E)
            run(act, program)

        @block.vector
        def _(dve):
            def rest_of_tokens(n, half):
                dve.wait_ge(s.tokens_hi, 2 * n - 1 + half)
                dve.tensor_tensor(flat(tok_lo[:, 4 * half:4 * half + 4, :]), k.bank(0), flat(tok_hi[:, 4 * half:4 * half + 4, :]).bitcast(F32),
                                  ALU.subtract).then_inc(s.tokens_ready, 1)

            def one_hot(n):
                dve.wait_ge(s.here_ready, n)
                dve.tensor_tensor(hot_now[:, :, :], bc(k.c("slots"), 1, TH), here_now[:, :, :].broadcast_to([P, TH, CAP]),
                                  ALU.is_equal).then_inc(s.hot_ready, 1)

            def rest_of_hidden(n):
                dve.wait_ge(s.hid_hi, n)
                dve.tensor_tensor(flat(hid_lo[:, :, :]), k.bank(1), flat(hid_hi[:, :, :]).bitcast(F32), ALU.subtract).then_inc(s.hid_ready, 1)

            def program():
                if p == 0:
                    dve.sem_inc(s.multiplied, FREE)
                    dve.sem_inc(s.hid_ready, FREE)
                one_hot((E + 1) * p + 1)
                for half in range(2):
                    rest_of_tokens((E + 1) * p + 1, half)
                with dve.Fori(0, E) as e:
                    for j in range(PIECES):
                        for c in range(FC):
                            if j == min(last_piece("up", c) + X_SPLIT, PIECES - 1):
                                dve.wait_ge(s.piece_used, X_SPLIT + PIECES * x0 + last_piece("up", c) + 1 + PIECES * e)
                                dve.wait_ge(s.gate_kept, FREE + FC * x0 + c + 1 + FC * e)
                                dve.tensor_tensor(hid[:, :], hid[:, :], k.bank(1), ALU.mult).then_inc(s.multiplied, 1)
                            if c < FC - 1 and j == turn_after(c) + X_SPLIT:
                                rest_of_hidden(FC * x0 + c + 1 + FC * e)
                        if j == last_piece("up", 0):
                            dve.wait_ge(s.gathered, 2 * (E + 1) * p + 2 + 2 * e)
                            one_hot((E + 1) * p + 2 + e)
                        if j == PIECES - 1:
                            rest_of_tokens((E + 1) * p + 2 + e, 0)
                            rest_of_hidden(FC * x0 + FC + FC * e)
                            rest_of_tokens((E + 1) * p + 2 + e, 1)
                        dve.wait_ge(s.hi_ready, PIECES * x0 + j + 1 + PIECES * e)
                        dve.tensor_tensor(w_lo[:, j % X_SPLIT, :], expert_slot(k, j // 2)[:, j % 2 * PIECE:(j % 2 + 1) * PIECE],
                                          w_hi[:, j % X_SPLIT, :].bitcast(F32), ALU.subtract).then_inc(k.lo_ready, 1)
                dve.wait_ge(s.out_done, FREE + (E + 1) * (p + 1))
                for i in range(2):
                    r = flat(k.res[:, 4 * i:4 * i + 4, :])
                    dve.tensor_tensor(r, r, k.bank(4 + 2 * i, 2), ALU.add).then_inc(s.added, 1)
                dve.wait_ge(s.added, 2 * (p + 1))
            run(dve, program)

        @block.gpsimd
        def _(pool):
            def program():
                pool.tensor_copy(here_now[:, :, :], x.here[:, :, 0:1]).then_inc(s.here_ready, 1)
                with pool.Fori(0, E) as e:
                    pool.wait_ge(s.hot_ready, (E + 1) * p + 1 + e)
                    pool.tensor_copy(here_now[:, :, :], x.here[:, :, bass.ds(e + 1, 1)]).then_inc(s.here_ready, 1)
                    pool.wait_ge(s.out_done, FREE + (E + 1) * p + e)
                    pool.tensor_copy(scatter_now[:, :], x.scatter[:, bass.ds(e, 1), :].rearrange("p o c -> p (o c)")).then_inc(s.scatter_ready, 1)
                pool.wait_ge(s.out_done, FREE + (E + 1) * p + E)
                pool.tensor_copy(scatter_now[:, :], x.scatter[:, E, :]).then_inc(s.scatter_ready, 1)
            run(pool, program)

        @block.tensor
        def _(pe):
            def gather(n, half):
                if half:
                    pe.wait_ge(s.tokens_ready, 2 * n - 1)
                else:
                    pe.wait_ge(s.hot_ready, n)
                for kt in range(4):
                    for a in range(TH):
                        ins = pe.matmul(k.bank(0)[:, kt * CAP:(kt + 1) * CAP], x.rows[:, a, (4 * half + kt) * P:(4 * half + kt + 1) * P],
                                        hot_now[:, a, :], start=a == 0, stop=a == 1)
                ins.then_inc(s.gathered, 1)

            def scatter(e):
                pe.wait_ge(s.y_kept, (E + 1) * p + 1 + e)
                pe.wait_ge(s.scatter_ready, (E + 1) * p + 1 + e)
                for m in range(KT):
                    ins = pe.matmul(k.bank(4 + m // 2)[:, (m % 2) * T:(m % 2 + 1) * T], y[:, m * P:(m + 1) * P], scatter_now[:, :],
                                    start=False, stop=False, skip_group_check=True)
                ins.then_inc(s.out_done, 1)

            def three(out, x_hi, x_lo, hi, lo, start, stop):
                pe.matmul(out, x_hi, hi, start=start, stop=False)
                pe.matmul(out, x_lo, hi, start=False, stop=False)
                return pe.matmul(out, x_hi, lo, start=False, stop=stop)

            def program():
                if p == 0:
                    pe.sem_inc(s.piece_used, X_SPLIT)
                    pe.sem_inc(s.turned, FREE)
                    pe.sem_inc(s.out_done, FREE)
                for b in range(4, 8):
                    pe.matmul(k.bank(b), x.zeros[:, :], k.consts[:, 0:512], start=True, stop=False, skip_group_check=True)
                for half in range(2):
                    gather((E + 1) * p + 1, half)
                with pe.Fori(0, E) as e:
                    pe.wait_ge(s.tokens_ready, 2 * (E + 1) * p + 2 + 2 * e)
                    for j in range(PIECES):
                        kind, c = FFN_ORDER[j // 4]
                        if j % 4 == 0 and kind == "down":
                            pe.wait_ge(s.hid_ready, FREE + FC * x0 + c + 1 + FC * e)
                            if c == 0:
                                pe.wait_ge(s.y_kept, (E + 1) * p + 1 + e)
                        elif j % 4 == 0 and (c or kind == "up"):
                            pe.wait_ge(s.gate_kept if kind == "gate" else s.hid_ready, FREE + FC * x0 + c + FC * e)
                        pe.wait_ge(k.lo_ready, PIECES * x0 + j + 1 + PIECES * e)
                        hi, lo = w_hi[:, j % X_SPLIT, :], w_lo[:, j % X_SPLIT, :]
                        for n in range(2):
                            cols = slice(n * CH, (n + 1) * CH)
                            if kind == "down":
                                f = j % 4
                                ins = three(k.bank(2 + n), hid_hi[:, f, :], hid_lo[:, f, :], hi[:, cols], lo[:, cols],
                                            c == 0 and f == 0, c == FC - 1 and f == MF - 1)
                            else:
                                kt = 2 * (j % 4) + n
                                ins = three(k.bank(0 if kind == "gate" else 1), tok_hi[:, kt, :], tok_lo[:, kt, :], hi[:, cols], lo[:, cols],
                                            kt == 0, kt == KT - 1)
                        ins.then_inc(s.piece_used, 1)
                        if j == last_piece("up", FC - 1):
                            pe.wait_ge(s.gate_kept, FREE + FC * (x0 + 1) + FC * e)
                            gather((E + 1) * p + 2 + e, 0)
                        for c in range(FC):
                            if j == turn_after(c):
                                pe.wait_ge(s.multiplied, FREE + FC * x0 + c + 1 + FC * e)
                                for f in range(MF):
                                    ins = pe.transpose(k.bank(1)[:, f * CAP:(f + 1) * CAP], hid[:, f * P:(f + 1) * P], k.c("ident"))
                                ins.then_inc(s.turned, 1)
                        if j == last_piece("up", FC - 1):
                            scatter(e)
                            gather((E + 1) * p + 2 + e, 1)
                scatter(E)
            run(pe, program)


def experts(k):
    with ExitStack() as own:
        k.ring_more = k.sb("ring_more", [P, X_RING - 2 * SLOTS, 2 * PIECE], own)
        k.lo_ready = k.sem("expert_lo_ready")
        k.half_filled = [k.sem(f"expert_half_filled{i}") for i in range(X_RING)]

        def first_loads(sp, start, end):
            for i in range(start, end):
                load_expert_half(k, sp, 0, i, 0)

        out_project(k, "odd_out", O_OUT, DENSE, after=lambda sp: first_loads(sp, 0, 4))
        rms_norm(k, "norm4", DENSE, after=lambda sp: first_loads(sp, 4, X_RING))
        sb = lambda n, shape, dt=F32: k.sb("expert_" + n, shape, own, dt)
        x = Names(
            rows=sb("rows", [P, TH, D]),
            chosen=sb("chosen", [P, TH, E]), gate=sb("gate", [P, TH, E]), place=sb("place", [P, TH, E]),
            here=sb("here", [P, TH, E + 1]),
            most=sb("most", [P, 1], I32), zeros=sb("zeros", [P, P]),
            scatter=sb("scatter", [CAP, E + 1, T]))
        route(k, x)
        s = Names(**{n: k.sem("expert_" + n) for n in (
            "zeroed", "hot", "here_ready", "scatter_turned", "scatter_kept", "hot_ready", "gathered", "tokens_hi", "tokens_ready", "hi_ready",
            "turned", "piece_used", "gate_kept", "multiplied", "hid_hi", "hid_ready", "y_kept", "scatter_ready", "out_done", "added")})
        for p in range(PASSES):
            expert_tables(k, x, s, p)
            expert_pass(k, x, s, p)


def emit(k):
    s = Names(**{n: k.sem("out_" + n) for n in ("gain_loaded", "turned", "squared", "root", "scaled", "stored")})
    with ExitStack() as own:
        sb = lambda n, shape: k.sb("out_" + n, shape, own)
        y, squares, gain = sb("rows", [P, TH, D]), sb("squares", [P, D]), sb("gain", [P, D])
        total, rstd = sb("total", [P, TH]), sb("rstd", [P, TH])
        block = own.enter_context(k.nc.Block())

        @block.tensor
        def _(pe):
            for a in range(TH):
                for kt in range(KT):
                    ins = pe.transpose(k.bank(2 * a + kt // 4)[:, (kt % 4) * P:(kt % 4 + 1) * P], k.res[:, kt, a * P:(a + 1) * P], k.c("ident"))
                ins.then_inc(s.turned, 1)

        @block.scalar
        def _(act):
            for a in range(TH):
                act.wait_ge(s.turned, a + 1)
                if a:
                    act.wait_ge(s.squared, a)
                act.activation(squares[:, :], k.bank(2 * a, 2), ACT.Square, accum_out=total[:, a:a + 1]).then_inc(s.squared, 1)
                act.wait_ge(s.root, 3 * a + 2)
                act.activation(rstd[:, a:a + 1], rstd[:, a:a + 1], ACT.Sqrt).then_inc(s.root, 1)

        @block.vector
        def _(dve):
            for a in range(TH):
                one = rstd[:, a:a + 1]
                dve.wait_ge(s.squared, a + 1)
                dve.tensor_scalar(one, total[:, a:a + 1], 1.0 / D, EPS, ALU.mult, ALU.add).then_inc(s.root, 1)
                dve.wait_ge(s.root, 3 * a + 1)
                dve.reciprocal(one, one).then_inc(s.root, 1)
                dve.wait_ge(s.root, 3 * a + 3)
                if a == 0:
                    dve.wait_ge(s.gain_loaded, 16)
                dve.scalar_tensor_tensor(out=y[:, a, :], in0=k.bank(2 * a, 2), scalar=one, in1=gain[:, :],
                                         op0=ALU.mult, op1=ALU.mult).then_inc(s.scaled, 1)

        @block.sync
        def _(sp):
            sp.dma_start(gain[:, :], k.g.final_norm_g.unsqueeze(0).broadcast_to([P, D])).then_inc(s.gain_loaded, 16)
            for a in range(TH):
                sp.wait_ge(s.scaled, a + 1)
                sp.dma_start(k.g.out[0, a * P:(a + 1) * P, :], y[:, a, :]).then_inc(s.stored, 16)
            sp.wait_ge(s.stored, 16 * TH)


def build(nc, g):
    with ExitStack() as ctx:
        k = Program(nc, g, ctx)
        embed(k)
        rms_norm(k, "norm1", SLOTS)
        even_mixer(k)
        out_project(k, "even_out", E_OUT, FFN + SLOTS)
        rms_norm(k, "norm2", FFN + SLOTS)
        dense_ffn(k)
        k.recycle()
        rms_norm(k, "norm3", O_IN + SLOTS)
        odd_mixer(k)
        k.recycle()
        experts(k)
        emit(k)


INPUTS = ["x", "e_w_in", "e_gla_gate_up", "e_w_out", "e_ffn_w_gate", "e_ffn_w_up", "e_ffn_w_down", "o_w_in",
          "o_rw_w_up", "o_rw_a_up", "o_rw_g_up", "o_w_out", "o_moe_router", "o_moe_w_gate", "o_moe_w_up",
          "o_moe_w_down", "final_norm_g"]


def packed_params(i):
    cols = lambda a: np.asarray(a).reshape(-1, P).T
    gate_b = np.zeros((P, 2), np.float32)
    gate_b[0:4, :] = np.asarray(i["e_ml_gate_b"]).reshape(2, 4).T
    v = {
        "norm1_e": i["e_norm1_g"], "conv_w": i["e_ml_conv_w"], "conv_b": i["e_ml_conv_b"], "ml_norm": i["e_ml_norm_g"],
        "gla_b": i["e_gla_gate_b"], "gla_norm": i["e_gla_norm_g"], "norm2_e": i["e_norm2_g"], "norm1_o": i["o_norm1_g"],
        "ret_norm": i["o_ret_norm_g"], "mu": i["o_rw_mu"], "w0": i["o_rw_w0"], "a0": i["o_rw_a0"], "k_k": i["o_rw_k_k"],
        "k_a": i["o_rw_k_a"], "r_k": i["o_rw_r_k"], "ln_g": i["o_rw_ln_g"], "ln_b": i["o_rw_ln_b"],
        "norm2_o": i["o_norm2_g"],
    }
    v["eps"], v["rw_eps"] = np.full(P, EPS, np.float32), np.full(P, RW_LN_EPS, np.float32)
    return np.concatenate([gate_b if n == "gate_b" else cols(v[n]) for n, _ in PARAM_COLS], axis=1)


def kernel(**inputs):
    import concourse.bacc as bacc
    from concourse.bass_utils import run_bass_kernel_spmd as run
    nc = bacc.Bacc("TRN2", target_bir_lowering=False, num_devices=1)
    arrays = {n: np.ascontiguousarray(inputs[n]) for n in INPUTS}
    arrays["params"] = np.ascontiguousarray(packed_params(inputs))
    arrays["consts"], arrays["ret_consts"], arrays["rw_consts"] = constants()
    sent = {f"in_{n}_dram": a for n, a in arrays.items()}
    g = Names(**{n: nc.dram_tensor(f"in_{n}_dram", a.shape, mybir.dt.from_np(a.dtype), kind="ExternalInput").ap()
                 for n, a in arrays.items()}, out=nc.dram_tensor("out_0_dram", (1, T, D), F32, kind="ExternalOutput").ap())
    build(nc, g)
    r = run(nc, [sent], core_ids=[0])
    return r.results[0]["out_0_dram"]
```
